# Optimizing a Trainium2 kernel written in Bass

```python
import math
import jax, jax.numpy as jnp
from jax import lax
import numpy as np

D_MODEL = 1024
BATCH = 1
SEQ = 256
DEPTH = 1
DEC_BATCH = 8
DEC_SEQ = 4
PAST_LEN = 2048
PAGE_SIZE = 128

H_A = 4
DK_A = 128
DV_A = 128
D_A = H_A * DK_A
DV_TOT_A = H_A * DV_A
HGRN_CHUNK = 64
H_B = 8
HD_B = 64
D_B = H_B * HD_B
LORA_W = 64
LORA_A = 64
LORA_G = 128
RW_START = 2 * D_A + 2 * DV_TOT_A
RW_COLS = 3 * D_B + LORA_W + LORA_A + LORA_G
GATE_START = RW_START + RW_COLS
D_IN = GATE_START + 2 * D_MODEL
N_EXPERTS = 32
TOP_K = 4
D_FF = 1024
SWIGLU_LIMIT = 7.0
SWIGLU_ALPHA = 1.702
MOE_BLOCK = 128
EPS = 1e-6
RWKV_GN_EPS = 64e-5

kernel_name = "hgrn2_rwkv7_gated_moe_decode_step"

def rmsnorm(x, w):
    x32 = x.astype(jnp.float32)
    y = x32 * lax.rsqrt(jnp.mean(x32 * x32, axis=-1, keepdims=True) + EPS)
    return (y * w.astype(jnp.float32)).astype(x.dtype)

def hgrn2_chunked(q, k, v, log_f, s0):
    B, T, H, K = q.shape
    V = v.shape[-1]
    C = math.gcd(T, HGRN_CHUNK)
    n = T // C

    def to_blocks(a):
        return a.reshape(B, n, C, H, a.shape[-1]).transpose(1, 0, 3, 2, 4)

    causal = jnp.tril(jnp.ones((C, C), dtype=bool))[:, :, None]

    def step(S, blk):
        qc, kc, vc, gc = blk
        b = jnp.cumsum(gc, axis=2)
        o = jnp.einsum("bhtk,bhkv->bhtv", qc * jnp.exp(b), S)
        decay = jnp.exp(jnp.where(causal, b[:, :, :, None, :] - b[:, :, None, :, :], -jnp.inf))
        scores = jnp.einsum("bhtk,bhsk,bhtsk->bhts", qc, kc, decay)
        o = o + jnp.einsum("bhts,bhsv->bhtv", scores, vc)
        b_last = b[:, :, -1]
        S = S * jnp.exp(b_last)[..., None] + jnp.einsum(
            "bhsk,bhsv->bhkv", kc * jnp.exp(b_last[:, :, None] - b), vc)
        return S, o

    S, o = lax.scan(step, s0, (to_blocks(q), to_blocks(k), to_blocks(v), to_blocks(log_f)))
    return o.transpose(1, 0, 3, 2, 4).reshape(B, T, H, V), S

def rwkv7_scan(r, w, k, v, kk, a, s0):
    def step(S, inp):
        r_t, w_t, k_t, v_t, kk_t, a_t = inp
        sa = jnp.einsum("bhvk,bhk->bhv", S, -kk_t)
        S = (S * w_t[:, :, None, :] + sa[..., None] * (kk_t * a_t)[:, :, None, :]
             + v_t[..., None] * k_t[:, :, None, :])
        return S, jnp.einsum("bhvk,bhk->bhv", S, r_t)

    xs = tuple(jnp.moveaxis(t, 1, 0) for t in (r, w, k, v, kk, a))
    S, y = lax.scan(step, s0, xs)
    return jnp.moveaxis(y, 0, 1), S

def moe(x2d, router_w, router_b, w_gu, b_gu, w_down, b_down):
    N, D = x2d.shape
    logits = x2d.astype(jnp.float32) @ router_w.astype(jnp.float32) + router_b.astype(jnp.float32)
    top_val, top_idx = lax.top_k(logits, TOP_K)
    gates = jax.nn.softmax(top_val, axis=-1).astype(x2d.dtype)
    NK = N * TOP_K
    e_flat = top_idx.reshape(-1).astype(jnp.int32)
    tok_flat = jnp.arange(NK, dtype=jnp.int32) // TOP_K
    order = jnp.argsort(e_flat * NK + jnp.arange(NK, dtype=jnp.int32))
    e_s, tok_s, g_s = e_flat[order], tok_flat[order], gates.reshape(-1)[order]
    counts = jnp.zeros((N_EXPERTS,), jnp.int32).at[e_flat].add(1)
    start = jnp.cumsum(counts) - counts
    padded = (counts + MOE_BLOCK - 1) // MOE_BLOCK * MOE_BLOCK
    pend = jnp.cumsum(padded)
    pstart = pend - padded
    dest = pstart[e_s] + (jnp.arange(NK, dtype=jnp.int32) - start[e_s])
    n_blocks = (NK + N_EXPERTS * (MOE_BLOCK - 1) + MOE_BLOCK - 1) // MOE_BLOCK
    M = n_blocks * MOE_BLOCK
    buf_tok = jnp.full((M,), N, jnp.int32).at[dest].set(tok_s)
    x_pad = jnp.concatenate([x2d, jnp.zeros((1, D), x2d.dtype)], axis=0)
    block_expert = jnp.minimum(
        jnp.searchsorted(pend, jnp.arange(n_blocks, dtype=jnp.int32) * MOE_BLOCK, side="right"),
        N_EXPERTS - 1).astype(jnp.int32)

    def expert_block(args):
        tok_b, e = args
        h = x_pad[tok_b] @ w_gu[e] + b_gu[e]
        glu = jnp.minimum(h[:, 0::2], SWIGLU_LIMIT)
        lin = jnp.clip(h[:, 1::2], -SWIGLU_LIMIT, SWIGLU_LIMIT)
        act = glu * jax.nn.sigmoid(SWIGLU_ALPHA * glu) * (lin + 1.0)
        return act @ w_down[e] + b_down[e]

    out = lax.map(expert_block, (buf_tok.reshape(n_blocks, MOE_BLOCK), block_expert)).reshape(M, D)
    return jax.ops.segment_sum(out[dest] * g_s[:, None], tok_s, num_segments=N)

def decoder_layer(x, s_hgrn, s_rwkv, shift_prev, lb, norm1_w, w_in, hgrn_gnorm_w, rwkv_mu,
                  rwkv_w0, rwkv_w2, rwkv_a0, rwkv_a2, rwkv_g2, rwkv_k_k, rwkv_k_a, rwkv_r_k,
                  rwkv_ln_w, rwkv_ln_b, w_branch_a, w_branch_b, w_out, norm2_w, router_w, router_b,
                  expert_w_gu, expert_b_gu, expert_w_down, expert_b_down):
    B, T, _ = x.shape
    f32 = jnp.float32
    xn = rmsnorm(x, norm1_w)
    proj = xn @ w_in
    hq = proj[..., :D_A].astype(f32)
    hf = proj[..., D_A:2 * D_A].astype(f32)
    hi = proj[..., 2 * D_A:2 * D_A + DV_TOT_A].astype(f32)
    hg = proj[..., 2 * D_A + DV_TOT_A:RW_START].astype(f32)
    rw = proj[..., RW_START:GATE_START].astype(f32)
    gate_a = proj[..., GATE_START:GATE_START + D_MODEL]
    gate_b = proj[..., GATE_START + D_MODEL:]

    lb = lb.astype(f32)
    f = lb + (1.0 - lb) * jax.nn.sigmoid(hf)
    o_a, s_hgrn_new = hgrn2_chunked(
        jax.nn.silu(hq).reshape(B, T, H_A, DK_A), (1.0 - f).reshape(B, T, H_A, DK_A),
        hi.reshape(B, T, H_A, DV_A), jnp.log(f).reshape(B, T, H_A, DK_A), s_hgrn.astype(f32))
    o_a = (o_a * lax.rsqrt(jnp.mean(o_a * o_a, axis=-1, keepdims=True) + EPS)
           * hgrn_gnorm_w.astype(f32) * jax.nn.silu(hg.reshape(B, T, H_A, DV_A)))
    o_a = o_a.reshape(B, T, DV_TOT_A)

    prev = (shift_prev.astype(xn.dtype) @ w_in[:, RW_START:GATE_START]).astype(f32)
    rw_prev = jnp.concatenate([prev[:, None], rw[:, :-1]], axis=1)
    rw = rw + (rw_prev - rw) * rwkv_mu.astype(f32)
    r, k, v, wlo, alo, glo = jnp.split(
        rw, [D_B, 2 * D_B, 3 * D_B, 3 * D_B + LORA_W, 3 * D_B + LORA_W + LORA_A], axis=-1)
    w_log = -jax.nn.softplus(-(rwkv_w0.astype(f32) + jnp.tanh(wlo) @ rwkv_w2.astype(f32))) - 0.5
    decay = jnp.exp(-jnp.exp(w_log))
    a = jax.nn.sigmoid(rwkv_a0.astype(f32) + alo @ rwkv_a2.astype(f32))
    g = jax.nn.sigmoid(glo) @ rwkv_g2.astype(f32)
    kk = (k * rwkv_k_k.astype(f32)).reshape(B, T, H_B, HD_B)
    kk = kk / jnp.maximum(jnp.sqrt(jnp.sum(kk * kk, axis=-1, keepdims=True)), 1e-12)
    k = k * (1.0 + (a - 1.0) * rwkv_k_a.astype(f32))
    r = r.reshape(B, T, H_B, HD_B)
    k = k.reshape(B, T, H_B, HD_B)
    v = v.reshape(B, T, H_B, HD_B)
    y, s_rwkv_new = rwkv7_scan(r, decay.reshape(B, T, H_B, HD_B), k, v, kk,
                               a.reshape(B, T, H_B, HD_B), s_rwkv.astype(f32))
    mu = jnp.mean(y, axis=-1, keepdims=True)
    var = jnp.mean(jnp.square(y - mu), axis=-1, keepdims=True)
    y = ((y - mu) * lax.rsqrt(var + RWKV_GN_EPS) * rwkv_ln_w.astype(f32).reshape(H_B, HD_B)
         + rwkv_ln_b.astype(f32).reshape(H_B, HD_B))
    y = y + jnp.sum(r * k * rwkv_r_k.astype(f32), axis=-1, keepdims=True) * v
    o_b = y.reshape(B, T, D_B) * g

    merged = (jax.nn.sigmoid(gate_a) * (o_a.astype(x.dtype) @ w_branch_a)
              + jax.nn.sigmoid(gate_b) * (o_b.astype(x.dtype) @ w_branch_b))
    x = x + merged @ w_out

    h = moe(rmsnorm(x, norm2_w).reshape(B * T, D_MODEL), router_w, router_b,
            expert_w_gu, expert_b_gu, expert_w_down, expert_b_down)
    x = x + h.reshape(B, T, D_MODEL).astype(x.dtype)
    return x, s_hgrn_new.astype(x.dtype), s_rwkv_new.astype(x.dtype), xn[:, -1]

def setup_inputs(seed: int = 0) -> dict:
    key = jax.random.key(seed)
    ks = jax.random.split(key, 32)

    def nrm(k, shape, scale):
        return jax.random.normal(k, shape, jnp.float32) * scale

    return {
        "x_prompt": nrm(ks[0], (BATCH, SEQ, D_MODEL), 1.0),
        "x_sample": nrm(ks[1], (DEC_BATCH, DEC_SEQ, D_MODEL), 1.0),
        "state_hgrn": nrm(ks[2], (DEPTH, DEC_BATCH, H_A, DK_A, DV_A), 0.5),
        "state_rwkv": nrm(ks[3], (DEPTH, DEC_BATCH, H_B, HD_B, HD_B), 0.3),
        "state_shift": nrm(ks[4], (DEPTH, DEC_BATCH, D_MODEL), 1.0),
        "norm1_w": 1.0 + nrm(ks[5], (DEPTH, D_MODEL), 0.02),
        "w_in": nrm(ks[6], (DEPTH, D_MODEL, D_IN), D_MODEL ** -0.5),
        "hgrn_lb_logits": nrm(ks[7], (DEPTH + 1, D_A), 0.5),
        "hgrn_gnorm_w": 1.0 + nrm(ks[8], (DEPTH, DV_A), 0.02),
        "rwkv_mu": jax.random.uniform(ks[9], (DEPTH, RW_COLS), jnp.float32),
        "rwkv_w0": nrm(ks[10], (DEPTH, D_B), 0.5),
        "rwkv_w2": nrm(ks[11], (DEPTH, LORA_W, D_B), 0.5 * LORA_W ** -0.5),
        "rwkv_a0": nrm(ks[12], (DEPTH, D_B), 0.1),
        "rwkv_a2": nrm(ks[13], (DEPTH, LORA_A, D_B), 0.5 * LORA_A ** -0.5),
        "rwkv_g2": nrm(ks[14], (DEPTH, LORA_G, D_B), LORA_G ** -0.5),
        "rwkv_k_k": 0.85 + nrm(ks[15], (DEPTH, D_B), 0.02),
        "rwkv_k_a": 1.0 + nrm(ks[16], (DEPTH, D_B), 0.02),
        "rwkv_r_k": nrm(ks[17], (DEPTH, H_B, HD_B), 0.1),
        "rwkv_ln_w": 1.0 + nrm(ks[18], (DEPTH, D_B), 0.02),
        "rwkv_ln_b": nrm(ks[19], (DEPTH, D_B), 0.02),
        "w_branch_a": nrm(ks[20], (DEPTH, DV_TOT_A, D_MODEL), DV_TOT_A ** -0.5),
        "w_branch_b": nrm(ks[21], (DEPTH, D_B, D_MODEL), D_B ** -0.5),
        "w_out": nrm(ks[22], (DEPTH, D_MODEL, D_MODEL), D_MODEL ** -0.5),
        "norm2_w": 1.0 + nrm(ks[23], (DEPTH, D_MODEL), 0.02),
        "router_w": nrm(ks[24], (DEPTH, D_MODEL, N_EXPERTS), D_MODEL ** -0.5),
        "router_b": nrm(ks[25], (DEPTH, N_EXPERTS), 0.01),
        "expert_w_gu": nrm(ks[26], (DEPTH, N_EXPERTS, D_MODEL, 2 * D_FF), D_MODEL ** -0.5),
        "expert_b_gu": nrm(ks[27], (DEPTH, N_EXPERTS, 2 * D_FF), 0.01),
        "expert_w_down": nrm(ks[28], (DEPTH, N_EXPERTS, D_FF, D_MODEL), D_FF ** -0.5),
        "expert_b_down": nrm(ks[29], (DEPTH, N_EXPERTS, D_MODEL), 0.01),
        "final_norm_w": 1.0 + nrm(ks[30], (D_MODEL,), 0.02),
    }

def reference(x_prompt, x_sample, state_hgrn, state_rwkv, state_shift, norm1_w, w_in, hgrn_lb_logits,
              hgrn_gnorm_w, rwkv_mu, rwkv_w0, rwkv_w2, rwkv_a0, rwkv_a2, rwkv_g2, rwkv_k_k, rwkv_k_a,
              rwkv_r_k, rwkv_ln_w, rwkv_ln_b, w_branch_a, w_branch_b, w_out, norm2_w, router_w, router_b,
              expert_w_gu, expert_b_gu, expert_w_down, expert_b_down, final_norm_w):
    lb_all = jnp.cumsum(jax.nn.softmax(hgrn_lb_logits.astype(jnp.float32), axis=0), axis=0)
    bp = x_prompt.shape[0]
    xp, xs = x_prompt, x_sample
    hgrn_p, rwkv_p, shift_p, hgrn_s, rwkv_s, shift_s = [], [], [], [], [], []
    for l in range(DEPTH):
        layer_w = (norm1_w[l], w_in[l], hgrn_gnorm_w[l], rwkv_mu[l], rwkv_w0[l], rwkv_w2[l], rwkv_a0[l],
                   rwkv_a2[l], rwkv_g2[l], rwkv_k_k[l], rwkv_k_a[l], rwkv_r_k[l], rwkv_ln_w[l], rwkv_ln_b[l],
                   w_branch_a[l], w_branch_b[l], w_out[l], norm2_w[l], router_w[l], router_b[l],
                   expert_w_gu[l], expert_b_gu[l], expert_w_down[l], expert_b_down[l])
        xp, hp, rp, sp = decoder_layer(
            xp, jnp.zeros((bp, H_A, DK_A, DV_A), jnp.float32), jnp.zeros((bp, H_B, HD_B, HD_B), jnp.float32),
            jnp.zeros((bp, D_MODEL), xp.dtype), lb_all[l], *layer_w)
        xs, hs, rs, ss = decoder_layer(xs, state_hgrn[l], state_rwkv[l], state_shift[l], lb_all[l], *layer_w)
        hgrn_p.append(hp); rwkv_p.append(rp); shift_p.append(sp)
        hgrn_s.append(hs); rwkv_s.append(rs); shift_s.append(ss)
    y_prompt = rmsnorm(xp, final_norm_w)
    y_sample = rmsnorm(xs, final_norm_w)
    return (y_prompt, y_sample, jnp.stack(hgrn_p), jnp.stack(rwkv_p), jnp.stack(shift_p),
            jnp.stack(hgrn_s), jnp.stack(rwkv_s), jnp.stack(shift_s))


_drawn_inputs = setup_inputs


def setup_inputs(seed=0):
    import zlib

    import numpy as np

    out = dict(_drawn_inputs(seed))
    spreads = {}
    factors = {'rwkv_k_k': 3.53, 'expert_b_gu': 8.0, 'expert_b_down': 8.0, 'final_norm_w': 2.764}
    for name, (base, spread) in spreads.items():
        noise = np.random.default_rng([zlib.crc32(name.encode()), seed]).standard_normal(out[name].shape)
        drawn = base * np.exp(spread * noise) if base else spread * noise
        out[name] = __import__('jax').numpy.asarray(drawn.astype(out[name].dtype))
    for name, factor in factors.items():
        out[name] = (out[name] * factor).astype(out[name].dtype)
    return out
```

```python
from contextlib import ExitStack

import concourse.bass as bass
from concourse import mybir

P = 128
F32 = mybir.dt.float32
I32 = mybir.dt.int32
BF16 = mybir.dt.bfloat16
U32 = mybir.dt.uint32
ALU = mybir.AluOpType
ACT = mybir.ActivationFunctionType
AX = mybir.AxisListType

D = 1024
KT = D // P
NP_, NS = 256, 32
NB, TS = 8, 4
NT = NP_ + NS
NX = NT + NB
TILES = [(0, 128), (128, 128), (256, 32)]
HA, DA = 4, 128
HB, DB = 8, 64
DR = HB * DB
C = 32
NC_P = NP_ // C
FM = 4 * NT
NE, TOPK = 32, 4
DFF = 1024
EPS = 1e-6
GN_EPS = 64e-5
LIMIT, ALPHA = 7.0, 1.702
W_SCALE = -0.6065306597126334

SLOTS = 64
OVER = (NT * TOPK) // (SLOTS + 1)
BLOCKS = NE + OVER
TABS = BLOCKS + 2
TW = 7
RING, CH = 12, 2048
RING_MIX = 4
CPC = 256
N_IN = 23
MIX_CHUNKS = N_IN + 4 + 4
ECH = 12


def bcast(ap, shape):
    return ap.to_broadcast(shape)


def layer_kernel(nc, x_prompt, x_sample, state_hgrn, state_rwkv, state_shift, norm1_w, w_in, hgrn_lb_logits,
                 hgrn_gnorm_w, rwkv_mu, rwkv_w0, rwkv_w2, rwkv_a0, rwkv_a2, rwkv_g2, rwkv_k_k, rwkv_k_a,
                 rwkv_r_k, rwkv_ln_w, rwkv_ln_b, w_branch_a, w_branch_b, w_out, norm2_w, router_w, router_b,
                 expert_w_gu, expert_b_gu, expert_w_down, expert_b_down, final_norm_w,
                 y_prompt, y_sample, hgrn_p, rwkv_p, shift_p, hgrn_s, rwkv_s, shift_s):
    ctx = ExitStack()
    with ctx:
        def sb(name, cols, dt=F32, rows=P):
            return ctx.enter_context(nc.sbuf_tensor(name, [rows, cols], dt))

        def sem(name):
            return ctx.enter_context(nc.semaphore(name))

        ring = sb("ring", RING * CH)
        arena = sb("arena", 28392)
        at = [0]

        def take(n):
            a = arena[:, at[0]:at[0] + n]
            at[0] += n
            return a

        ident = take(128)
        mask4 = take(512)
        lower = take(128)
        eye64 = take(64)
        ones64 = take(128)
        before = take(128)
        ones = take(128)
        head2 = take(2)
        gn_bc = take(128)
        off_lnw = at[0]
        lnw_bc = take(512)
        lnb_bc = take(512)
        rb_bc = take(32)
        off_lora = at[0]
        lora = take(512)
        g2 = take(512)
        scan_mask = take(FM)
        norm_bc = take(D)
        par = take(42)
        npar = take(42)
        smask = take(32)
        seqm = take(8)
        stat = take(64)
        gamR = take(4 * NC_P)
        gamH = take(4 * (NC_P + NB))
        wS = take(4 * NS)
        rkb = take(24)
        lb = take(4)
        omlb = take(4)
        omka = take(4)
        xnT = take(KT * NX)
        fm = [take(FM) for _ in range(12)]
        tm = take(4 * 3 * 512)
        hiT, hgT, vT, gT = (tm[:, i * 1536:(i + 1) * 1536] for i in range(4))

        scratch = ring[:, RING_MIX * CH:]
        PL, HR, ZR = scratch[:, 0:5952], scratch[:, 5952:11072], scratch[:, 11072:16384]
        xs = HR[:, 0:3 * D].rearrange("p (t d) -> p t d", t=3)
        xn = ZR[:, 0:3 * D].rearrange("p (t d) -> p t d", t=3)
        shE = [PL[:, 4096 + 297 * i:4096 + 297 * (i + 1)] for i in range(2)]
        shD = PL[:, 4690:4690 + NT]
        waT = PL[:, 4978:4978 + NT]
        glT = PL[:, 5266:5266 + NT]
        z0, z1 = ZR[:, 0:FM], ZR[:, FM:2 * FM]
        par_rows = scratch[:, 11072 + 3 * D:11072 + 3 * D + 128]
        S_s = PL[:, 0:2048]
        tmp_s = PL[:, 2048:4096]
        vec_s = PL[:, 4096:5632]
        v_s = PL[:, 5632:5760]
        sa_s = PL[:, 5760:5792]
        y_s = PL[:, 5792:5920]
        stm = HR[:, 0:3072]
        ktT, aT, sH, oH = HR[:, 0:512], HR[:, 512:1024], HR[:, 1024:3584], HR[:, 3584:5120]
        s0h, vexp = ZR[:, 0:4096], ZR[:, 4096:5120]
        yaT, wta, yO, Qm, Xm = (HR[:, 0:512], HR[:, 512:1024], HR[:, 1024:2560], HR[:, 2560:3072],
                                HR[:, 3072:3584])
        PM, PQ, phi, Rh = ZR[:, 0:2048], ZR[:, 2048:4096], ZR[:, 4096:4608], ZR[:, 4608:4864]
        bnT, knT = fm[9][:, 0:256], fm[9][:, 256:512]
        off3 = at[0] - 4 * 1536 - 12 * FM
        s_all = arena[:, off3 + 3 * FM:off3 + 3 * FM + 9 * 256]
        gate = [fm[i] for i in (0, 1, 10, 11)]

        bank = [ctx.enter_context(nc.psum_tensor(f"bank{i}", [P, 512], F32)) for i in range(8)]

        late = sb("late", 136)
        lt = [0]

        def ltake(n):
            a = late[:, lt[0]:lt[0] + n]
            lt[0] += n
            return a

        epsc = ltake(2)
        sgT = arena[:, off_lora:off_lora + 3 * 512]
        sq = arena[:, off_lora + 3 * 512:off_lora + 4 * 512]
        sq2 = fm[1][:, 0:1024]
        oaT = fm[5]
        ramp = ones64
        ramp_i = fm[11].bitcast(I32)[:, 0:2 * SLOTS]
        rw_sb = fm[9][:, 512:512 + KT * NE]
        tab = fm[11][:, 720:720 + TABS * TW]
        st2 = ltake(96)
        st3 = ltake(24)
        gselc, selc = ltake(2 * TW)[:, :], st3[:, 15:18]
        obT = fm[6]
        mT = arena[:, off3 + 7 * FM:off3 + 9 * FM]
        sqy = PM[:, 512:1024]
        btmp = PQ[:, 0:NT]
        xr = tm[:, 0:3 * D].rearrange("p (t d) -> p t d", t=3)
        x2 = tm[:, 3 * D:6 * D].rearrange("p (t d) -> p t d", t=3)
        res2 = fm[0][:, 0:D]
        x2T = xnT[:, 0:KT * NT]
        rt = [off3 + 2 * FM]

        def rtake(n):
            a = arena[:, rt[0]:rt[0] + n]
            rt[0] += n
            return a

        lg, v8, i8f, gk = rtake(96), rtake(24), rtake(24), rtake(12)
        gsum, Mk, M, Rk = rtake(6), rtake(384), rtake(96), rtake(96)
        dst_e, off_e, dest, Ck = rtake(96), rtake(NE), rtake(12), rtake(NE)
        nov, ovend, ramp64, btf = rtake(NE), rtake(NE), rtake(64), rtake(64)
        wte, pmod = rtake(96), rtake(1)
        qk, inb, sk = (rtake(3 * TABS * TOPK) for _ in range(3))
        le = qk[:, 0:(TABS - NE) * NE]
        wT = fm[1][0:NE, 0:NT]
        bt = ctx.enter_context(nc.sbuf_tensor("block_table", [1, 64], I32))
        nblk = ctx.enter_context(nc.sbuf_tensor("block_count", [1, 2], I32))
        i8 = ctx.enter_context(nc.sbuf_tensor("expert_index", [P, 24], U32))
        braw = arena[:, off_lora:off_lora + 2 * DFF]
        bdn = arena[0:NE, off_lnw:off_lnw + D]
        bgu3 = fm[6][:, 0:DFF].bitcast(BF16)
        glu, lin = fm[0][:, 0:512], fm[0][:, 512:1024]
        sig, act_s = fm[1][:, 0:512], fm[1][:, 512:1024]
        xT, actT = fm[10][:, 0:512], fm[10][:, 512:1024]
        yo, GT = fm[9][:, 0:D], fm[8][:, 0:NT]
        sel, gsel = fm[11][:, 0:3 * SLOTS], fm[11][:, 256:256 + 6 * SLOTS]
        ind = fm[11][:, 640:704].bitcast(BF16)

        smp_dram = nc.dram_tensor("smp_dram", [HB, NB, TS, 6, DB], F32, kind="Internal").ap()
        ysm_dram = nc.dram_tensor("ysm_dram", [2, HB, NB, TS, 32], F32, kind="Internal").ap()

        names = {}

        def S(name):
            if name not in names:
                names[name] = sem(name)
            return names[name]

        counts = {}

        def done(ins, name):
            ins.then_inc(S(name), 1)
            counts[name] = counts.get(name, 0) + 1
            return counts[name]

        def done_wait(eng, ins, name):
            eng.wait_ge(S(name), done(ins, name))

        ring_loaded = [sem(f"ring_loaded{i}") for i in range(RING_MIX)]
        w_loaded = [sem(f"w_loaded{c}") for c in range(KT)] + ring_loaded
        w_used = sem("w_used")

        v_in = w_in[0].rearrange("(k p) c -> p k c", p=P)
        HGRN0, RW0, GATE0 = 0, 2048, 3840
        starts = [RW0 + CPC * i for i in range(7)] + [CPC * i for i in range(8)] + [GATE0 + CPC * i for i in range(8)]
        ba, bb, wo = (w.rearrange("(k p) c -> p k c", p=P) for w in (w_branch_a[0], w_branch_b[0], w_out[0]))

        def mix_chunk(n):
            slot = ring[:, (n % RING_MIX) * CH:(n % RING_MIX + 1) * CH]
            if n < N_IN:
                return slot.rearrange("p (k c) -> p k c", k=KT), v_in[:, :, starts[n]:starts[n] + CPC]
            n -= N_IN
            src, k0 = [(ba, 0), (ba, 2), (bb, 0), (bb, 2), (wo, 0), (wo, 2), (wo, 4), (wo, 6)][n]
            return slot.rearrange("p (k c) -> p k c", k=2), src[:, k0:k0 + 2, :]

        v_gu = expert_w_gu[0].rearrange("e (k p) c -> e p k c", p=P)
        v_dn = expert_w_down[0].rearrange("e (k p) c -> e p k c", p=P)

        def w_slot(c):
            s = c + RING_MIX if c < KT else c - KT
            return ring[:, s * CH:(s + 1) * CH]

        def w_load(eng, e, c):
            if c < KT:
                eng.dma_start(w_slot(c), v_gu[bass.ds(e, 1), :, c, :].rearrange("e p c -> (e p) c")).then_inc(w_loaded[c], 16)
            else:
                k = 2 * (c - KT)
                eng.dma_start(w_slot(c).rearrange("p (k c) -> p k c", k=2),
                              v_dn[bass.ds(e, 1), :, k:k + 2, :].rearrange("e p k c -> (e p) k c")).then_inc(w_loaded[c], 16)

        def w_wait(c, i):
            mixer = 0 if c < KT else len(range(c - KT, MIX_CHUNKS, RING_MIX))
            return i * 16 + 16 * (mixer + 1)

        def acc(t, half):
            return bank[2 + 2 * t + half][:, :] if t < 2 else bank[7][NS * half:NS * half + NS, :]

        block = ctx.enter_context(nc.Block())

        def pj_after(n):
            return 2 * (n + 1) if n < 11 else 22 + 3 * (n - 10) if n < 15 else 34 + 2 * (n - 14)

        E_BLOCK = 34

        @block.sync
        def _(sp):
            for t, (o, n) in enumerate(TILES):
                src = x_prompt[0, o:o + n, :] if t < 2 else x_sample.rearrange("b t d -> (b t) d")
                sp.dma_start(xs[0:n, t, :], src).then_inc(S(f"x_loaded{t}"), 16)
            sp.dma_start(xn[NS:NS + NB, 2, :], state_shift[0]).then_inc(S("shift_loaded"), 16)
            sp.dma_start(norm_bc, norm1_w.partition_broadcast(P)).then_inc(S("norm_loaded"), 16)
            pre = MIX_CHUNKS - RING_MIX
            for n in range(MIX_CHUNKS):
                if n == pre:
                    sp.wait_ge(S("oa_done"), 3)
                    for t, (o, rows) in enumerate(TILES):
                        src = x_prompt[0, o:o + rows, :] if t < 2 else x_sample.rearrange("b t d -> (b t) d")
                        sp.dma_start(xr[0:rows, t, :], src).then_inc(S("xr_loaded"), 16)
                    sp.dma_start(norm_bc, norm2_w.partition_broadcast(P)).then_inc(S("norm_loaded"), 16)
                    sp.wait_ge(S("rws_out"), 32)
                    w_load(sp, 0, 0)
                    w_load(sp, 0, 1)
                if n >= RING_MIX:
                    m = n - RING_MIX
                    if m < N_IN:
                        sp.wait_ge(S("pj_done"), pj_after(m))
                    else:
                        sp.wait_ge(S("branch"), 8 if m < N_IN + 2 else 16)
                dst, src = mix_chunk(n)
                sp.dma_start(dst, src).then_inc(ring_loaded[n % RING_MIX], 16)
            sp.wait_ge(S("ob_var"), 3)
            for x in (0, 2, 3):
                sp.dma_start(braw[NE * x:NE * x + NE, :], expert_b_gu[0]).then_inc(S("braw_loaded"), 16)
            sp.wait_ge(S("merged"), 8)
            sp.dma_start(bdn, expert_b_down[0]).then_inc(S("bdn_loaded"), 16)
            sp.wait_ge(S("rwp_out"), 16)
            sp.wait_ge(S("ysm_st"), 32)
            for c in range(2, KT):
                w_load(sp, 0, c)
            sp.wait_ge(S("wo_done"), 3)
            for c in range(KT, ECH):
                w_load(sp, 0, c)
            sp.wait_ge(S("xn_done"), 6)
            sp.dma_start(norm_bc, final_norm_w.partition_broadcast(P)).then_inc(S("norm_loaded"), 16)
            sp.wait_ge(S("blocks"), 1)
            with sp.Fori(0, sp.value_load(nblk[0:1, 1:2], min_val=NE - 1, max_val=TABS - 2)) as i:
                e = sp.value_load(bt[0:1, bass.ds(i + 1, 1)], min_val=0, max_val=NE - 1)
                for c in range(ECH):
                    sp.wait_ge(w_used, i * ECH + (c + 1))
                    w_load(sp, e, c)
            for t, (o, rows) in enumerate(TILES):
                sp.wait_ge(S("xn_done"), 6 + t + 1)
                dst = y_prompt[0, o:o + rows, :] if t < 2 else y_sample.rearrange("b t d -> (b t) d")
                sp.dma_start(dst, xr[0:rows, t, :]).then_inc(S("y_out"), 16)
            sp.wait_ge(S("shift_out"), 32)
            sp.wait_ge(S("hgrn_out"), 32)
            sp.wait_ge(S("rws_out"), 32)
            sp.wait_ge(S("rwp_out"), 16)
            sp.wait_ge(S("y_out"), 48)

        @block.tensor
        def _(pe):
            mm = nc.tensor.matmul

            def chunk_ready(n):
                pe.wait_ge(ring_loaded[n % RING_MIX], 16 * (n // RING_MIX + 1))

            pe.wait_ge(S("masks"), 1)
            for t, (o, n) in enumerate(TILES):
                pe.wait_ge(S("xn_done"), t + 1)
                if t == 2:
                    pe.wait_ge(S("shift_loaded"), 16)
                rows = n if t < 2 else NS + NB
                for k in range(KT):
                    b = bank[2 * t + k // 4] if t < 2 else bank[4]
                    c = (k % 4) * 128 if t < 2 else k * 40
                    i = nc.tensor.transpose(b[:, c:c + rows], xn[0:rows, t, k * P:(k + 1) * P], ident[0:rows, 0:rows])
                    if k % 4 == 3 and (t < 2 or k == 7):
                        done(i, "xT_done")
            pe.wait_ge(S("par_loaded"), 16 * 9)
            done(nc.tensor.transpose(bank[5][:, 0:42], par_rows[0:42, :], ident[0:42, 0:42]), "par_T")

            xv = xnT.rearrange("p (k t) -> p k t", k=KT)

            def project(k, n, j, cols):
                slot, _ = mix_chunk(n)
                b = bank[k % 4] if k < E_BLOCK else bank[k % 2]
                for kt in range(KT):
                    i = mm(b[:, 0:cols], slot[:, kt, j * P:(j + 1) * P], xv[:, kt, 0:cols], start=(kt == 0), stop=(kt == KT - 1))
                done(i, "pj_done")

            def bank_free(k):
                if k >= E_BLOCK:
                    pe.wait_ge(S("pj_evac"), max(E_BLOCK, k - 1))
                elif k >= 4:
                    pe.wait_ge(S("pj_evac"), k - 3)

            pe.wait_ge(S("xT_evac"), 5)
            for k in range(22):
                n = k // 2
                if k % 2 == 0:
                    chunk_ready(n)
                bank_free(k)
                project(k, n, k % 2, NX if k < 14 else NT)
                if k == 17:
                    pe.wait_ge(S("lora_in"), 1)
                    for q in range(4):
                        if q >= 2:
                            pe.wait_ge(S("lora_evac"), q - 1)
                        mm(bank[4 + q % 2][:, 0:NT], lora[0:64, q * P:(q + 1) * P], waT[0:64, :], start=True, stop=True)
                        done(mm(bank[6 + q % 2][:, 0:NT], lora[64:128, q * P:(q + 1) * P], waT[64:128, :],
                                start=True, stop=True), "lora_done")
                    for q in range(4):
                        pe.wait_ge(S("ksq"), 1)
                        pe.wait_ge(S("lora_evac"), 3 + min(q, 1))
                        if q >= 2:
                            pe.wait_ge(S("kn_evac"), q - 1)
                        done(mm(bank[4 + q % 2][:, 0:NT], ones64, z1[:, q * NT:(q + 1) * NT], start=True, stop=True),
                             "kn_done")
            k = 22
            for n in range(11, 15):
                chunk_ready(n)
                slot, _ = mix_chunk(n)
                for t, (o, rows) in enumerate(TILES):
                    bank_free(k)
                    for kt in range(KT):
                        i = mm(bank[k % 4][0:rows, 0:CPC], xv[:, kt, o:o + rows], slot[:, kt, :],
                               start=(kt == 0), stop=(kt == KT - 1))
                    done(i, "pj_done")
                    k += 1
                if n == 12:
                    pe.wait_ge(S("bonus_in"), 1)
                    for t, (o, rows) in enumerate(TILES):
                        for q in range(4):
                            i = mm(bank[6][0:rows, t * 8 + 2 * q:t * 8 + 2 * q + 2], z1[:, q * NT + o:q * NT + o + rows],
                                   head2, start=True, stop=True)
                    done(i, "bonus_done")
                    pe.wait_ge(S("gl_in"), 1)
                    for t, (o, rows) in enumerate(TILES):
                        b = bank[(4, 5, 7)[t]]
                        done(mm(b[0:rows, :], glT[:, o:o + rows], g2, start=True, stop=True), "g_done")
                    pe.wait_ge(S("smp_in"), 1)
                    srcs = [fm[0], wS, fm[1], fm[9], fm[3], fm[2]]
                    for a, src in enumerate(srcs):
                        b = bank[(4, 5, 7)[a % 3]]
                        if a < 3:
                            pe.wait_ge(S("g_evac"), a + 1)
                        else:
                            pe.wait_ge(S("smp_evac"), a - 2)
                        for q in range(4):
                            v = src[:, q * NS:(q + 1) * NS] if a == 1 else src[:, q * NT + NP_:(q + 1) * NT]
                            i = nc.tensor.transpose(b[0:NS, q * P:(q + 1) * P], v, ident)
                        done(i, "smp_T")

            pe.wait_ge(S("smp_evac"), 6)
            pe.wait_ge(S("hg_in"), 1)
            qt, kt_, qh, kh = fm[10], fm[4], fm[11], fm[1]

            def f4(a, h, o, n):
                return a[:, h * NT + o:h * NT + o + n]

            pe.wait_ge(S("pj_evac"), E_BLOCK)
            def hgrn_prompt(t, i3):
                o = 128 * t
                if i3:
                    pe.wait_ge(S("hg_o_evac"), i3)
                for h in range(HA):
                    i = nc.tensor.transpose(bank[2][:, h * P:(h + 1) * P], f4(kt_, h, o, P), ident)
                done(i, "hg_kT")
                if i3:
                    pe.wait_ge(S("hg_a"), i3)
                for h in range(HA):
                    i = mm(bank[3][:, h * P:(h + 1) * P], f4(kh, h, o, P), f4(qh, h, o, P), start=True, stop=True)
                done(i, "hg_scores")
                pe.wait_ge(S("hg_kT_evac"), i3 + 1)
                if t:
                    pe.wait_ge(S("hg_upd"), 8)
                for c in range(4):
                    r = slice(C * c, C * c + C)
                    for h in range(HA):
                        i = mm(bank[4 + c][:, h * P:(h + 1) * P], ktT[r, h * P:(h + 1) * P],
                               hiT[r, t * 512 + h * P:t * 512 + (h + 1) * P], start=True, stop=True)
                    done(i, "hg_kv")
                pe.wait_ge(S("hg_a"), i3 + 1)
                for h in range(HA):
                    mm(bank[2][:, h * P:(h + 1) * P], aT[:, h * P:(h + 1) * P],
                       hiT[:, t * 512 + h * P:t * 512 + (h + 1) * P], start=(h == 0), stop=False, skip_group_check=True)
                for c in range(4):
                    g = 4 * t + c
                    if g == 0:
                        continue
                    pe.wait_ge(S("hg_state"), g)
                    for h in range(HA):
                        i = mm(bank[2][C * c:C * c + C, h * P:(h + 1) * P], f4(qt, h, o + C * c, C),
                               sH[:, (g % 5) * 512 + h * P:(g % 5) * 512 + (h + 1) * P], start=False, stop=True,
                               skip_group_check=True)
                done(i, "hg_o")

            def hgrn_sample():
                pe.wait_ge(S("hg_o_evac"), 1)
                for h in range(HA):
                    i = nc.tensor.transpose(bank[2][0:NS, h * P:(h + 1) * P], f4(kt_, h, NP_, NS), ident)
                done(i, "hg_kT")
                for h in range(HA):
                    i = mm(bank[3][0:NS, h * NS:(h + 1) * NS], f4(kh, h, NP_, NS), f4(qh, h, NP_, NS),
                           start=True, stop=True)
                done(i, "hg_scores")
                pe.wait_ge(S("hg_state"), 4)
                pe.wait_ge(S("hg_a"), 2)
                for h in range(HA):
                    mm(bank[4][:, h * NS:(h + 1) * NS], hiT[0:NS, 1024 + h * P:1024 + (h + 1) * P],
                       aT[0:NS, h * NS:(h + 1) * NS], start=(h == 0), stop=False, skip_group_check=True)
                pe.wait_ge(S("s0h_loaded"), 16)
                for h in range(HA):
                    for b in range(NB):
                        i = mm(bank[4][:, h * NS + TS * b:h * NS + TS * (b + 1)],
                               s0h[:, (b * HA + h) * P:(b * HA + h + 1) * P], f4(qt, h, NP_ + TS * b, TS),
                               start=False, stop=True, skip_group_check=True)
                done(i, "hg_oT")
                pe.wait_ge(S("hg_oT_evac"), 1)
                for h in range(HA):
                    i = nc.tensor.transpose(bank[5][0:NS, h * P:(h + 1) * P], aT[:, P + h * NS:P + (h + 1) * NS], ident)
                done(i, "hg_o")
                pe.wait_ge(S("hg_kT_evac"), 2)
                for h in range(HA):
                    pe.wait_ge(S("vexp"), h + 1)
                    for g in range(2):
                        if h:
                            pe.wait_ge(S("hg_upd"), 2 * (h - 1) + g + 1)
                        done(mm(bank[6 + g][:, :], ktT[0:NS, h * P:(h + 1) * P], vexp[0:NS, g * 512:(g + 1) * 512],
                                start=True, stop=True), "hg_skv")

            hgrn_prompt(0, 0)
            hgrn_sample()
            hgrn_prompt(1, 2)

            vR, At, Rt, Bn, Kn = fm[2], fm[5], fm[6], fm[7], fm[8]
            AR = arena[:, off3 + 5 * FM:off3 + 7 * FM].rearrange("p (a t) -> p a t", a=2)
            pe.wait_ge(S("hg_o_evac"), 3)
            pe.wait_ge(S("hg_state"), 8)
            pe.wait_ge(S("rw_in"), 1)
            gate_k = [E_BLOCK]

            def gate_tile():
                k = gate_k[0]
                if k >= E_BLOCK + 16:
                    return
                gate_k[0] += 1
                n = 15 + (k - E_BLOCK) // 2
                if k % 2 == 0:
                    chunk_ready(n)
                bank_free(k)
                project(k, n, k % 2, NT)

            for u in range(4):
                t, G = u // 2, u % 2
                o = 128 * t
                if u:
                    pe.wait_ge(S("rw_y_evac"), u)
                for q in range(2):
                    for a, src in enumerate((At, Bn, Kn, vR)):
                        i = nc.tensor.transpose(bank[2 + a // 2][:, (a % 2) * 256 + q * P:(a % 2) * 256 + (q + 1) * P],
                                                f4(src, 2 * G + q, o, P), ident)
                done(i, "rw_T")
                if u:
                    pe.wait_ge(S("rw_state"), 4 * u)
                for hh in range(4):
                    q, r = 2 * G + hh // 2, slice(64 * (hh % 2), 64 * (hh % 2) + 64)
                    c0 = q * NT + o
                    ar = AR[r, :, c0:c0 + P]
                    b = bank[4 + hh]
                    mm(b[:, 0:256], Bn[r, c0:c0 + P], ar, start=True, stop=True)
                    done(mm(b[:, 256:512], Kn[r, c0:c0 + P], ar, start=True, stop=True), "rw_scores")
                pe.wait_ge(S("rw_T_evac"), u + 1)
                for hh in range(4):
                    q, r = 2 * G + hh // 2, slice(64 * (hh % 2), 64 * (hh % 2) + 64)
                    c0 = q * NT + o
                    i = mm(bank[2 + hh % 2][:, (hh // 2) * P:(hh // 2 + 1) * P], At[r, c0:c0 + P], Bn[r, c0:c0 + P],
                           start=True, stop=True)
                done(i, "rw_L")
                gate_tile()
                for lev in range(4):
                    if lev == 0:
                        pe.wait_ge(S("rw_masked"), 6 * (u + 1))
                    else:
                        pe.wait_ge(S("rw_sq_evac"), 4 * u + lev)
                    src, dst = (PQ[:, 0:1024], PQ[:, 1024:2048])[::1 if lev % 2 else -1]
                    for hh in range(4):
                        if lev == 0:
                            Pm, Q = PM[:, hh * 512:hh * 512 + P], Qm[:, hh * P:(hh + 1) * P]
                        else:
                            Pm, Q = src[:, hh * 256:hh * 256 + P], src[:, hh * 256 + P:(hh + 1) * 256]
                        b, c0 = bank[4 + hh // 2], (hh % 2) * 256
                        if lev < 3:
                            mm(b[:, c0:c0 + P], Q, Pm, start=True, stop=True)
                        i = mm(b[:, c0 + P:c0 + 256], Pm, Q, start=True, stop=True)
                    done(i, "rw_sq")
                    if lev < 3:
                        gate_tile()
                    pe.wait_ge(S("rw_sq_evac"), 4 * u + lev + 1)
                    pe.wait_ge(S("rw_X"), 5 * u + lev + 1)
                    for hh in range(4):
                        i = mm(bank[6][:, hh * P:(hh + 1) * P], dst[:, hh * 256 + P:(hh + 1) * 256],
                               Xm[:, hh * P:(hh + 1) * P], start=True, stop=True)
                    done(i, "rw_XQ")
                for hh in range(4):
                    i = mm(bank[7][:, hh * 64:(hh + 1) * 64], PM[:, hh * 512 + 256:hh * 512 + 384],
                           vT[:, t * 512 + (4 * G + hh) * 64:t * 512 + (4 * G + hh + 1) * 64], start=True, stop=True)
                done(i, "rw_Y1")
                pe.wait_ge(S("rw_X"), 5 * u + 5)
                pe.wait_ge(S("rw_Y1_evac"), u + 1)
                for hh in range(4):
                    i = mm(bank[6][:, hh * P:(hh + 1) * P], Xm[:, hh * P:(hh + 1) * P], yaT[:, hh * P:(hh + 1) * P],
                           start=True, stop=True)
                done(i, "rw_WT")
                pe.wait_ge(S("rw_WT_evac"), u + 1)
                for hh in range(4):
                    i = mm(bank[7][64 * (hh % 2):64 * (hh % 2) + 64, (hh // 2) * P:(hh // 2 + 1) * P],
                           wta[:, hh * P + 64:(hh + 1) * P], PM[:, hh * 512 + P:hh * 512 + 256], start=True, stop=True)
                done(i, "rw_R")
                for hh in range(4):
                    out = bank[2 + hh % 2][:, (hh // 2) * 64:(hh // 2 + 1) * 64]
                    h = 4 * G + hh
                    mm(out, PM[:, hh * 512 + P:hh * 512 + 256], wta[:, hh * P:hh * P + 64], start=(hh < 2), stop=False,
                       skip_group_check=True)
                    mm(out, PM[:, hh * 512 + 384:hh * 512 + 512], vT[:, t * 512 + h * 64:t * 512 + (h + 1) * 64],
                       start=False, stop=False, skip_group_check=True)
                pe.wait_ge(S("rw_R_evac"), u + 1)
                for c in range(4):
                    r = slice(C * c, C * c + C)
                    for hh in range(4):
                        h, s, hp = 4 * G + hh, 64 * (hh % 2), hh // 2
                        W, TA = wta[r, hh * P:hh * P + 64], wta[r, hh * P + 64:(hh + 1) * P]
                        mm(bank[4 + c][s:s + 64, hp * 64:(hp + 1) * 64], TA, bnT[r, hh * 64:(hh + 1) * 64],
                           start=(hh < 2), stop=True, skip_group_check=True)
                        out = bank[4 + c][s:s + 64, P + hp * 64:P + (hp + 1) * 64]
                        mm(out, knT[r, hh * 64:(hh + 1) * 64], vT[r, t * 512 + h * 64:t * 512 + (h + 1) * 64],
                           start=False, stop=False, skip_group_check=True)
                        i = mm(out, bnT[r, hh * 64:(hh + 1) * 64], W, start=False, stop=False, skip_group_check=True)
                    done(i, "rw_chunk")
                for c in range(4):
                    g = 4 * t + c
                    pe.wait_ge(S("rw_phi"), 4 * u + c + 1)
                    if c:
                        pe.wait_ge(S("rw_state"), 4 * u + c)
                    for hh in range(4):
                        s, hp = 64 * (hh % 2), hh // 2
                        q = 2 * G + hp
                        i = mm(bank[4 + c][s:s + 64, P + hp * 64:P + (hp + 1) * 64],
                               phi[s:s + 64, c * P + hp * 64:c * P + (hp + 1) * 64],
                               s_all[s:s + 64, g * 256 + q * 64:g * 256 + (q + 1) * 64], start=False, stop=True,
                               skip_group_check=True)
                    done(i, "rw_chain")
                for c in range(4):
                    g = 4 * t + c
                    for hh in range(4):
                        s, hp = 64 * (hh % 2), hh // 2
                        q = 2 * G + hp
                        i = mm(bank[2 + hh % 2][C * c:C * c + C, hp * 64:(hp + 1) * 64],
                               Rh[s:s + 64, hp * P + C * c:hp * P + C * c + C],
                               s_all[s:s + 64, g * 256 + q * 64:g * 256 + (q + 1) * 64], start=False, stop=True,
                               skip_group_check=True)
                done(i, "rw_y")
            while gate_k[0] < E_BLOCK + 16:
                gate_tile()
            pe.wait_ge(S("rw_state"), 16)
            pe.wait_ge(S("rw_y_evac"), 4)
            for q in range(4):
                i = nc.tensor.transpose(bank[4][0:64, q * P:(q + 1) * P], s_all[:, 8 * 256 + q * 64:8 * 256 + (q + 1) * 64], ident)
            done(i, "rw_end")

            def gated_T(t, src, b):
                rows = TILES[t][1]
                for q in range(4):
                    i = nc.tensor.transpose(b[:, q * P:q * P + rows], src[0:rows, t * 512 + q * P:t * 512 + (q + 1) * P],
                                            ident[0:rows, 0:rows])
                done(i, "gated_T")

            pe.wait_ge(S("oa_done"), 3)
            for t in range(3):
                gated_T(t, oH, bank[5 + t])
            pe.wait_ge(S("pj_evac"), E_BLOCK + 16)
            for br in range(2):
                chunk_ready(N_IN + 2 * br)
                chunk_ready(N_IN + 2 * br + 1)
                if br:
                    for t in range(3):
                        pe.wait_ge(S("ob_done"), t + 1)
                        gated_T(t, yO, bank[5 + t])
                pe.wait_ge(S("gated_T_evac"), 3 * (br + 1))
                for j in range(KT):
                    n = 8 * br + j
                    if n >= 2:
                        pe.wait_ge(S("br_evac"), n - 1)
                    for kt in range(4):
                        slot, _ = mix_chunk(N_IN + 2 * br + kt // 2)
                        i = mm(bank[n % 2][:, 0:NT], slot[:, kt % 2, j * P:(j + 1) * P],
                               (obT if br else oaT)[:, kt * NT:(kt + 1) * NT], start=(kt == 0), stop=(kt == 3))
                    done(i, "branch")
            pe.wait_ge(S("xr_loaded"), 48)
            pe.wait_ge(S("rwp_end"), 1)
            for t, (o, rows) in enumerate(TILES):
                for h in range(2):
                    mm(acc(t, h), ident[0:rows, 0:rows], xr[0:rows, t, h * 512:(h + 1) * 512], start=True, stop=False,
                       skip_group_check=True)
            for kt in range(KT):
                if kt % 2 == 0:
                    chunk_ready(N_IN + 4 + kt // 2)
                slot, _ = mix_chunk(N_IN + 4 + kt // 2)
                pe.wait_ge(S("merged"), kt + 1)
                for t, (o, rows) in enumerate(TILES):
                    for h in range(2):
                        i = mm(acc(t, h), mT[:, kt * NT + o:kt * NT + o + rows], slot[:, kt % 2, h * 512:(h + 1) * 512],
                               start=False, stop=True, skip_group_check=True)
                    if kt == KT - 1:
                        done(i, "wo_done")
            for t, (o, rows) in enumerate(TILES):
                pe.wait_ge(S("xn_done"), 3 + t + 1)
                if t == 1:
                    pe.wait_ge(S("x2T_evac"), 2)
                for k in range(KT):
                    b, c = (bank[k // 4], (k % 4) * P) if t < 2 else (bank[6], k * NS)
                    i = nc.tensor.transpose(b[:, c:c + rows], x2[0:rows, t, k * P:(k + 1) * P], ident[0:rows, 0:rows])
                    if k % 4 == 3 and (t < 2 or k == 7):
                        done(i, "x2T")
            pe.wait_ge(S("x2T_evac"), 5)
            pe.wait_ge(S("router_loaded"), 16)
            for t, (o, rows) in enumerate(TILES):
                for kt in range(KT):
                    i = mm(bank[1][0:rows, t * NE:(t + 1) * NE], x2T[:, kt * NT + o:kt * NT + o + rows],
                           rw_sb[:, kt * NE:(kt + 1) * NE], start=(kt == 0), stop=(kt == KT - 1))
            done(i, "logits")
            pe.wait_ge(S("chosen"), 1)
            for t, (o, rows) in enumerate(TILES):
                for s in range(t + 1):
                    n = TILES[s][1]
                    i = mm(bank[6][0:rows, t * NE:(t + 1) * NE], (before if s == t else ones)[0:n, 0:rows],
                           M[0:n, s * NE:(s + 1) * NE], start=(s == 0), stop=(s == t))
            for s, (o, n) in enumerate(TILES):
                i = mm(bank[6][:, 3 * NE:4 * NE], ones[0:n, :], M[0:n, s * NE:(s + 1) * NE], start=(s == 0), stop=(s == 2))
            done(i, "ranks")

            def pick():
                for kt in range(KT):
                    for t, (o, rows) in enumerate(TILES):
                        i = mm(bank[6][:, kt * SLOTS:(kt + 1) * SLOTS], x2[0:rows, t, kt * P:(kt + 1) * P],
                               sel[0:rows, t * SLOTS:(t + 1) * SLOTS], start=(t == 0), stop=(t == 2))
                i.then_inc(S("picked"), 1)

            pe.wait_ge(S("weights_ready"), 1)
            for t, (o, rows) in enumerate(TILES):
                i = nc.tensor.transpose(bank[0][0:NE, o:o + rows], wte[0:rows, t * NE:(t + 1) * NE], ident[0:rows, 0:rows])
            done(i, "wT")
            pe.wait_ge(S("bdn_loaded"), 16)
            pe.wait_ge(S("wT_evac"), 1)
            for t, (o, rows) in enumerate(TILES):
                for h in range(2):
                    mm(acc(t, h), wT[:, o:o + rows], bdn[:, h * 512:(h + 1) * 512], start=False, stop=True, skip_group_check=True)

            def add():
                for t, (o, rows) in enumerate(TILES):
                    for h in range(2):
                        ins = mm(acc(t, h), GT[:, o:o + rows], yo[:, h * 512:(h + 1) * 512], start=False, stop=True,
                                 skip_group_check=True)
                ins.then_inc(S("added"), 1)

            pe.wait_ge(S("sel_ready"), 1)
            pick()
            pe.wait_ge(S("bgu3"), 1)
            pairs = pe.value_load(nblk[0:1, 0:1], min_val=NE // 2, max_val=TABS // 2)
            with pe.Fori(0, pairs) as i:
                for x in range(2):
                    pe.wait_ge(S("rows_evac"), i * 2 + x + 1)
                    if x == 1:
                        for t, (o, rows) in enumerate(TILES):
                            ins = nc.tensor.transpose(bank[6][:, o:o + rows], gsel[0:rows, t * P:(t + 1) * P], ident[0:rows, 0:rows])
                        ins.then_inc(S("gt_T"), 1)
                    for c in range(KT):
                        pe.wait_ge(w_loaded[c], i * 32 + (w_wait(c, 0) + 16 * x))
                        if c == 3:
                            if x == 0:
                                pe.wait_ge(S("gsel_ready"), i + 1)
                            for q in (0, 2, 1, 3):
                                mm(bank[q % 2][64 * (q // 2):64 * (q // 2) + 64, :], ind[:, x * SLOTS:(x + 1) * SLOTS],
                                   bgu3[:, q * 512:(q + 1) * 512], start=False, stop=False, skip_group_check=True)
                        for q in (0, 2, 1, 3):
                            if c == 0 and q == 1:
                                pe.wait_ge(S("y_evac"), i * 4 + 2 * x + 2)
                            ins = mm(bank[q % 2][64 * (q // 2):64 * (q // 2) + 64, :], xT[:, c * SLOTS:(c + 1) * SLOTS],
                                     w_slot(c)[:, q * 512:(q + 1) * 512], start=(c == 0), stop=(c == KT - 1), skip_group_check=True)
                        ins.then_inc(w_used, 1)
                    pe.wait_ge(S("sel_ready"), i * 2 + x + 2)
                    pe.wait_ge(S("gt_evac"), i + 1 + x)
                    pick()
                    if x == 0:
                        add()
                    pe.wait_ge(S("act_ready"), i * 2 + x + 1)
                    for q in range(4):
                        ins = nc.tensor.transpose(bank[0][:, q * P:(q + 1) * P], act_s[:, q * P:(q + 1) * P], ident)
                    ins.then_inc(S("actT"), 1)
                    pe.wait_ge(S("actT_evac"), i * 2 + x + 1)
                    for c in range(KT, ECH):
                        pe.wait_ge(w_loaded[c], i * 32 + (w_wait(c, 0) + 16 * x))
                        for kk in range(2):
                            kt = 2 * (c - KT) + kk
                            lhs = actT[:, (kt % 4) * P + SLOTS * (kt // 4):(kt % 4) * P + SLOTS * (kt // 4) + SLOTS]
                            for h in range(2):
                                ins = mm(bank[1][64 * h:64 * h + 64, :], lhs, w_slot(c)[:, kk * D + h * 512:kk * D + (h + 1) * 512],
                                         start=(kt == 0), stop=(kt == KT - 1), skip_group_check=True)
                        ins.then_inc(w_used, 1)
            pe.wait_ge(S("y_evac"), pairs * 4 + 2)
            add()

        @block.scalar
        def _(act):
            def fn(out, in_, f, **kw):
                return nc.scalar.activation(out, in_, f, **kw)

            xv = xnT.rearrange("p (k t) -> p k t", k=KT)
            for t, (o, n) in enumerate(TILES):
                act.wait_ge(S(f"x_loaded{t}"), 16)
                done_wait(act, fn(xn[0:n, t, :], xs[0:n, t, :], ACT.Square, accum_out=stat[0:n, t:t + 1]), "act_step")
                act.wait_ge(S("eps"), 1)
                done_wait(act, fn(stat[0:n, 4 + t:5 + t], stat[0:n, t:t + 1], ACT.Ln, scale=1.0 / D, bias=epsc[0:n, 0:1]), "act_step")
                done(fn(stat[0:n, 8 + t:9 + t], stat[0:n, 4 + t:5 + t], ACT.Exp, scale=-0.5), "rstd")
            act.wait_ge(S("xn_done"), 3)
            act.dma_start(shift_p[0], xn[127:128, 1, :]).then_inc(S("shift_out"), 16)
            act.dma_start(shift_s[0], xn[3:NS:4, 2, :]).then_inc(S("shift_out"), 16)
            for e in range(5):
                act.wait_ge(S("xT_done"), e + 1)
                t, k0 = e // 2, 4 * (e % 2)
                if e < 4:
                    i = fn(xv[:, k0:k0 + 4, 128 * t:128 * t + 128], bank[e].rearrange("p (k t) -> p k t", k=4), ACT.Copy)
                else:
                    i = fn(xv[:, :, NP_:NX], bank[4][:, 0:8 * 40].rearrange("p (k t) -> p k t", k=KT), ACT.Copy)
                done(i, "xT_evac")
            act.wait_ge(S("par_T"), 1)
            fn(npar, bank[5][:, 0:42], ACT.Copy, scale=-1.0)
            done(fn(par, bank[5][:, 0:42], ACT.Copy), "par")
            act.wait_ge(S("lb_in"), 1)
            done(fn(stat[:, 16:24], stat[:, 16:24], ACT.Exp), "lb_exp")
            act.wait_ge(S("shift_zero"), 2)
            for k in range(14):
                act.wait_ge(S("pj_done"), k + 1)
                if k >= 2:
                    act.wait_ge(S("shift_done"), k - 1)
                e, b = shE[k % 2], bank[k % 4]
                es = e[:, 257:297].rearrange("p (b j) -> p b j", j=5)
                fn(e[:, 1:257], b[:, 0:NP_], ACT.Copy)
                fn(es[:, :, 1:5], b[:, NP_:NT].rearrange("p (b j) -> p b j", j=TS), ACT.Copy)
                done(fn(es[:, :, 0:1], b[:, NT:NX].rearrange("p (b j) -> p b j", j=1), ACT.Copy), "pj_evac")
            act.wait_ge(S("shift_done"), 13)
            done(fn(waT[0:64, :], waT[0:64, :], ACT.Exp, scale=2.0), "th_exp")
            act.wait_ge(S("shift_done"), 14)
            done(fn(glT, glT, ACT.Exp, scale=-1.0), "gl_exp")

            def evac_qf(k):
                act.wait_ge(S("pj_done"), k + 1)
                b, q = bank[k % 4][:, 0:NT], (k - 14) % 4
                cols = slice(q * NT, (q + 1) * NT)
                if k < 18:
                    fn(fm[10][:, cols], b, ACT.Copy)
                    i = fn(fm[11][:, cols], b, ACT.Exp, scale=-1.0)
                else:
                    i = fn(z0[:, cols], b, ACT.Exp, scale=-1.0)
                done(i, "pj_evac")

            def evac_ig(k):
                act.wait_ge(S("pj_done"), k + 1)
                n, t = 11 + (k - 22) // 3, (k - 22) % 3
                rows, dst = TILES[t][1], (hiT if n < 13 else hgT)
                c = t * 512 + CPC * ((n - 11) % 2)
                done(fn(dst[0:rows, c:c + CPC], bank[k % 4][0:rows, 0:CPC], ACT.Copy), "pj_evac")

            for k in range(14, 18):
                evac_qf(k)
            for q in range(4):
                act.wait_ge(S("lora_done"), q + 1)
                cols = slice(q * NT, (q + 1) * NT)
                fn(fm[3][:, cols], bank[4 + q % 2][:, 0:NT], ACT.Exp, scale=-1.0, bias=npar[:, 14 + q:15 + q])
                done(fn(fm[4][:, cols], bank[6 + q % 2][:, 0:NT], ACT.Exp, scale=-1.0, bias=npar[:, 18 + q:19 + q]), "lora_evac")
            for q in range(4):
                act.wait_ge(S("kn_done"), q + 1)
                done(fn(fm[5][:, q * NT:(q + 1) * NT], bank[4 + q % 2][:, 0:NT], ACT.Sqrt), "kn_evac")
            for k in range(18, 22):
                evac_qf(k)
            for k in range(22, 24):
                evac_ig(k)
            act.wait_ge(S("rw_logw"), 1)
            done(fn(wS.rearrange("p (q t) -> p q t", q=4), fm[3].rearrange("p (q t) -> p q t", q=4)[:, :, NP_:NT], ACT.Exp), "wS_done")
            evac_ig(24)
            act.wait_ge(S("rw_cex"), 1)
            done(fn(fm[3], fm[3], ACT.Exp), "rw_exp")
            done(fn(fm[8], fm[7], ACT.Exp), "rw_exp")
            done(fn(fm[7], fm[7], ACT.Exp, scale=-1.0), "rw_exp")
            for k in range(25, 28):
                evac_ig(k)
            act.wait_ge(S("bonus_done"), 1)
            fn(rkb[:, 0:16], bank[6][:, 0:16], ACT.Copy)
            done(fn(rkb[0:NS, 16:24], bank[6][0:NS, 16:24], ACT.Copy), "bonus_evac")
            for t, (o, rows) in enumerate(TILES):
                act.wait_ge(S("g_done"), t + 1)
                done(fn(gT[0:rows, t * 512:(t + 1) * 512], bank[(4, 5, 7)[t]][0:rows, :], ACT.Copy), "g_evac")
            for a in range(6):
                act.wait_ge(S("smp_T"), a + 1)
                b = bank[(4, 5, 7)[a % 3]]
                if a == 5:
                    fn(vT[0:NS, 1024:1536], b[0:NS, :], ACT.Copy)
                done(fn(stm[0:NS, a * 512:(a + 1) * 512], b[0:NS, :], ACT.Copy), "smp_evac")
            for k in range(28, 34):
                evac_ig(k)
            act.wait_ge(S("hg_f"), 1)
            done(fn(fm[3], z0, ACT.Ln), "hg_log")
            act.wait_ge(S("hg_b"), 1)
            done(fn(fm[11], fm[3], ACT.Exp), "hg_exp")
            done(fn(fm[1], fm[3], ACT.Exp, scale=-1.0), "hg_exp")
            done(fn(fm[0], fm[9], ACT.Exp), "hg_exp")
            act.wait_ge(S("hg_rev"), 1)
            done(fn(fm[9], fm[9], ACT.Exp), "hg_exp")
            for n3, t in enumerate((0, 2, 1)):
                act.wait_ge(S("hg_kT"), n3 + 1)
                rows = TILES[t][1]
                done(fn(ktT[0:rows, :], bank[2][0:rows, :], ACT.Copy), "hg_kT_evac")
                if t == 2:
                    act.wait_ge(S("hg_oT"), 1)
                    done(fn(aT[:, P:2 * P], bank[4][:, 0:P], ACT.Copy), "hg_oT_evac")
                act.wait_ge(S("hg_o"), n3 + 1)
                src = bank[5] if t == 2 else bank[2]
                if n3:
                    act.wait_ge(S("hg_o_evac"), n3)
                for h in range(HA):
                    fn(sq[0:rows, h * P:(h + 1) * P], src[0:rows, h * P:(h + 1) * P], ACT.Square, accum_out=stat[0:rows, 4 * t + h:4 * t + h + 1])
                done(fn(oH[0:rows, t * 512:(t + 1) * 512], src[0:rows, :], ACT.Copy), "hg_o_evac")
                if t == 2:
                    act.wait_ge(S("hg_upd"), 8)
                    act.dma_start(hgrn_s[0].rearrange("b h k v -> k (b h) v"), s0h.rearrange("p (b h v) -> p (b h) v", b=NB, h=HA))\
                       .then_inc(S("hgrn_out"), 16)
            act.wait_ge(S("hg_state"), 8)
            act.dma_start(hgrn_p[0, 0].rearrange("h k v -> k h v"), sH[:, 3 * 512:4 * 512].rearrange("p (h v) -> p h v", h=HA))\
               .then_inc(S("hgrn_out"), 16)
            gate_k = [E_BLOCK]

            def gate_evac():
                k = gate_k[0]
                gate_k[0] += 1
                g = k - E_BLOCK
                act.wait_ge(S("pj_done"), k + 1)
                done(fn(gate[g // 4][:, (g % 4) * NT:(g % 4 + 1) * NT], bank[k % 2][:, 0:NT], ACT.Exp, scale=-1.0), "pj_evac")

            both = [(slice(0, P), 0, 2), (slice(0, NS), 2, 3)]

            def oa_factors():
                act.wait_ge(S("pj_evac"), E_BLOCK)
                for r, t0, t1 in both:
                    i = fn(sgT[r, t0 * 512:t1 * 512], hgT[r, t0 * 512:t1 * 512], ACT.Exp, scale=-1.0)
                    i = fn(stat[r, 12 + 4 * t0:12 + 4 * t1], stat[r, 4 * t0:4 * t1], ACT.Ln, scale=1.0 / DA, bias=epsc[r, 0:1])
                done_wait(act, i, "act_step")
                for r, t0, t1 in both:
                    i = fn(sgT[r, t0 * 512:t1 * 512], sgT[r, t0 * 512:t1 * 512], ACT.Ln, bias=ones[r, 0:1])
                done_wait(act, i, "act_step")
                for r, t0, t1 in both:
                    fn(sgT[r, t0 * 512:t1 * 512], sgT[r, t0 * 512:t1 * 512], ACT.Exp, scale=-1.0)
                    i = fn(stat[r, 24 + 4 * t0:24 + 4 * t1], stat[r, 12 + 4 * t0:12 + 4 * t1], ACT.Exp, scale=-0.5)
                done(i, "oa_in")

            def ob_rstd(n3, t):
                r = slice(0, TILES[t][1])
                act.wait_ge(S("ob_var"), n3 + 1)
                done_wait(act, fn(st2[r, 72 + 8 * t:80 + 8 * t], st2[r, 48 + 8 * t:56 + 8 * t], ACT.Ln, scale=1.0 / DB,
                                  bias=epsc[r, 1:2]), "act_step")
                done(fn(st2[r, 72 + 8 * t:80 + 8 * t], st2[r, 72 + 8 * t:80 + 8 * t], ACT.Exp, scale=-0.5), "ob_rstd")

            ya = yaT.rearrange("p (h c) -> p h c", h=4)
            for u in range(4):
                t, G = u // 2, u % 2
                act.wait_ge(S("rw_T"), u + 1)
                fn(ya[:, :, 64:128], bank[2][:, 0:256].rearrange("p (h c) -> p h c", h=4), ACT.Copy)
                fn(bnT, bank[2][:, 256:512], ACT.Copy)
                fn(knT, bank[3][:, 0:256], ACT.Copy)
                c = t * 512 + 256 * G
                done(fn(vT[:, c:c + 256], bank[3][:, 256:512], ACT.Copy), "rw_T_evac")
                gate_evac()
                for lev in range(4):
                    act.wait_ge(S("rw_sq"), 4 * u + lev + 1)
                    d0 = 1024 * ((lev + 1) % 2 == 0)
                    for x in range(2):
                        src, dst = bank[4 + x][:, :], PQ[:, d0 + 512 * x:d0 + 512 * (x + 1)]
                        if lev == 3:
                            src, dst = (v.rearrange("p (h c) -> p h c", h=2)[:, :, P:2 * P] for v in (src, dst))
                        i = fn(dst, src, ACT.Copy)
                    done(i, "rw_sq_evac")
                    if lev < 3:
                        gate_evac()
                act.wait_ge(S("rw_WT"), u + 1)
                done(fn(wta, bank[6][:, :], ACT.Copy), "rw_WT_evac")
                act.wait_ge(S("pj_evac"), E_BLOCK + 4 * (u + 1))
                done_wait(act, fn(gate[u], gate[u], ACT.Ln, bias=ones[:, 0:1]), "act_step")
                done(fn(gate[u], gate[u], ACT.Exp, scale=-1.0), "sgate")
                if u == 0:
                    oa_factors()
            act.wait_ge(S("rw_end"), 1)
            done_wait(act, fn(PM[0:64, 0:512], bank[4][0:64, :], ACT.Copy), "rwp_end")
            act.dma_start(rwkv_p[0, 0].rearrange("h v k -> v h k"), PM[0:64, 0:512].rearrange("p (h k) -> p h k", h=HB))\
               .then_inc(S("rwp_out"), 16)
            for n3, t in enumerate((0, 2, 1)):
                ob_rstd(n3, t)
            def evac_T(br, dst):
                for t, (o, rows) in enumerate(TILES):
                    act.wait_ge(S("gated_T"), 3 * br + t + 1)
                    done(fn(dst.rearrange("p (q t) -> p q t", q=4)[:, :, o:o + rows],
                            bank[5 + t].rearrange("p (q t) -> p q t", q=4)[:, :, 0:rows], ACT.Copy), "gated_T_evac")

            evac_T(0, oaT)
            evac_T(1, obT)

            def residual_norm(ready):
                for t, (o, rows) in enumerate(TILES):
                    ready(t)
                    r = slice(0, rows)
                    if t < 2:
                        for h in range(2):
                            i = fn(sq2[r, h * 512:(h + 1) * 512], acc(t, h), ACT.Square, accum_out=st3[r, 2 * t + h:2 * t + h + 1])
                    else:
                        for h in range(2):
                            i = fn(res2[r, h * 512:(h + 1) * 512], acc(t, h), ACT.Copy)
                        done_wait(act, i, "act_step")
                        for h in range(2):
                            i = fn(sq2[r, h * 512:(h + 1) * 512], res2[r, h * 512:(h + 1) * 512], ACT.Square, accum_out=st3[r, 4 + h:5 + h])
                    done_wait(act, i, "act_step")
                    done_wait(act, fn(st3[r, 6 + t:7 + t], st3[r, 2 * t:2 * t + 1], ACT.Identity, bias=st3[r, 2 * t + 1:2 * t + 2]), "act_step")
                    done_wait(act, fn(st3[r, 9 + t:10 + t], st3[r, 6 + t:7 + t], ACT.Ln, scale=1.0 / D, bias=epsc[r, 0:1]), "act_step")
                    done(fn(st3[r, 12 + t:13 + t], st3[r, 9 + t:10 + t], ACT.Exp, scale=-0.5), "rstd")

            residual_norm(lambda t: act.wait_ge(S("wo_done"), t + 1))
            x2v = x2T.rearrange("p (k t) -> p k t", k=KT)
            for e in range(5):
                act.wait_ge(S("x2T"), e + 1)
                t, k0 = e // 2, 4 * (e % 2)
                if e < 4:
                    i = fn(x2v[:, k0:k0 + 4, 128 * t:128 * t + 128], bank[e % 2].rearrange("p (k t) -> p k t", k=4), ACT.Copy)
                else:
                    i = fn(x2v[:, :, NP_:NT], bank[6][:, 0:KT * NS].rearrange("p (k t) -> p k t", k=KT), ACT.Copy)
                done(i, "x2T_evac")
            act.wait_ge(S("gk_in"), 1)
            done(fn(gk, gk, ACT.Exp), "gk_exp")
            act.wait_ge(S("wT"), 1)
            fn(wT, bank[0][0:NE, 0:NT], ACT.Copy).then_inc(S("wT_evac"), 1)
            act.wait_ge(S("picked"), 1)
            fn(xT, bank[6][:, :], ACT.Copy).then_inc(S("rows_evac"), 1)
            act.wait_ge(S("blocks"), 1)
            pairs = act.value_load(nblk[0:1, 0:1], min_val=NE // 2, max_val=TABS // 2)
            nc.scalar.preload_act_table_set("sigmoid_and_others")
            with act.Fori(0, pairs) as i:
                for x in range(2):
                    if x == 1:
                        act.wait_ge(S("gt_T"), i + 1)
                        act.wait_ge(S("added"), i + 1)
                        fn(GT, bank[6][:, 0:NT], ACT.Copy).then_inc(S("gt_evac"), 1)
                    act.wait_ge(S("glu_ready"), i * 2 + x + 1)
                    fn(sig, glu, ACT.Sigmoid, scale=ALPHA).then_inc(S("sig_ready"), 1)
                    act.wait_ge(S("picked"), i * 2 + x + 2)
                    fn(xT, bank[6][:, :], ACT.Copy).then_inc(S("rows_evac"), 1)
                    act.wait_ge(S("actT"), i * 2 + x + 1)
                    fn(actT, bank[0][:, :], ACT.Copy).then_inc(S("actT_evac"), 1)
                    act.wait_ge(w_used, i * (2 * ECH) + ECH * (x + 1))
                    fn(yo[64 * x:64 * x + 64, 0:512], bank[1][0:64, :], ACT.Copy).then_inc(S("y_evac"), 1)
            nc.scalar.preload_act_table_set("natural_log_exp_and_others")
            act.wait_ge(S("added"), pairs + 1)
            residual_norm(lambda t: None)

        @block.vector
        def _(dve):
            v = nc.vector

            def step(ins, name="dve_step"):
                done_wait(dve, ins, name)

            def pc(a, c):
                return a[:, c:c + 1]

            def quarter(a, q):
                return a[:, q * NT:(q + 1) * NT]

            dve.wait_ge(S("norm_loaded"), 16)
            for t, (o, n) in enumerate(TILES):
                dve.wait_ge(S("rstd"), t + 1)
                step(v.scalar_tensor_tensor(out=xn[0:n, t, :], in0=xs[0:n, t, :], scalar=stat[0:n, 8 + t:9 + t],
                                            in1=norm_bc[0:n, :], op0=ALU.mult, op1=ALU.mult), "xn_done")
            dve.wait_ge(S("par"), 1)
            step(v.tensor_tensor(stat[:, 24:28], par[:, 34:38], par[:, 38:42], ALU.max))
            step(v.tensor_tensor(stat[:, 16:20], par[:, 34:38], stat[:, 24:28], ALU.subtract))
            step(v.tensor_tensor(stat[:, 20:24], par[:, 38:42], stat[:, 24:28], ALU.subtract), "lb_in")
            step(v.tensor_scalar(omka, par[:, 26:30], -1.0, 1.0, ALU.mult, ALU.add))
            dve.wait_ge(S("lb_exp"), 1)
            step(v.tensor_tensor(stat[:, 24:28], stat[:, 16:20], stat[:, 20:24], ALU.add))
            step(v.reciprocal(stat[:, 28:32], stat[:, 24:28]))
            step(v.tensor_tensor(lb, stat[:, 16:20], stat[:, 28:32], ALU.mult))
            step(v.tensor_tensor(omlb, stat[:, 20:24], stat[:, 28:32], ALU.mult))
            for k in range(14):
                dve.wait_ge(S("pj_evac"), k + 1)
                e = shE[k % 2]
                es = e[:, 257:297].rearrange("p (b j) -> p b j", j=5)
                ds_ = shD[:, NP_:NT].rearrange("p (b j) -> p b j", j=TS)
                dst = quarter(fm[k // 4], k % 4) if k < 12 else (waT, glT)[k - 12]
                v.tensor_tensor(ds_, es[:, :, 0:4], es[:, :, 1:5], ALU.subtract).then_inc(S("shift_d"), 1)
                v.tensor_tensor(shD[:, 0:NP_], e[:, 0:256], e[:, 1:257], ALU.subtract).then_inc(S("shift_d"), 1)
                dve.wait_ge(S("shift_d"), 2 * k + 2)
                v.scalar_tensor_tensor(out=dst[:, NP_:NT].rearrange("p (b j) -> p b j", j=TS), in0=ds_, scalar=pc(par, k),
                                       in1=es[:, :, 1:5], op0=ALU.mult, op1=ALU.add)
                step(v.scalar_tensor_tensor(out=dst[:, 0:NP_], in0=shD[:, 0:NP_], scalar=pc(par, k), in1=e[:, 1:257],
                                            op0=ALU.mult, op1=ALU.add), "shift_done")
            dve.wait_ge(S("th_exp"), 1)
            step(v.tensor_scalar(waT[0:64, :], waT[0:64, :], 1.0, None, ALU.add))
            step(v.reciprocal(waT[0:64, :], waT[0:64, :]))
            step(v.tensor_scalar(waT[0:64, :], waT[0:64, :], -2.0, 1.0, ALU.mult, ALU.add), "lora_in")
            for q in range(4):
                i = v.tensor_scalar(quarter(fm[9], q), quarter(fm[1], q), pc(par, 22 + q), None, ALU.mult)
            step(i)
            dve.wait_ge(S("xT_done"), 5)
            dve.wait_ge(S("shift_out"), 32)
            step(v.tensor_tensor(z1, fm[9], fm[9], ALU.mult), "ksq")
            dve.wait_ge(S("gl_exp"), 1)
            step(v.tensor_scalar(glT, glT, 1.0, None, ALU.add))
            step(v.reciprocal(glT, glT), "gl_in")
            dve.wait_ge(S("lora_evac"), 4)
            dve.wait_ge(S("masks"), 1)
            step(v.tensor_scalar(fm[3], fm[3], 1.0, None, ALU.add))
            step(v.reciprocal(fm[3], fm[3]))
            step(v.tensor_scalar(fm[3], fm[3], W_SCALE, None, ALU.mult), "rw_logw")
            step(v.tensor_tensor_scan(fm[7], scan_mask, fm[3], 0.0, ALU.mult, ALU.add))
            dve.wait_ge(S("wS_done"), 1)
            step(v.tensor_tensor(fm[3], fm[7], fm[3], ALU.subtract), "rw_cex")
            step(v.tensor_scalar(fm[4], fm[4], 1.0, None, ALU.add))
            step(v.reciprocal(fm[4], fm[4]))
            dve.wait_ge(S("kn_evac"), 4)
            step(v.tensor_scalar(fm[5], fm[5], 1e-12, None, ALU.max))
            step(v.reciprocal(fm[5], fm[5]))
            step(v.tensor_tensor(fm[9], fm[9], fm[5], ALU.mult))
            for q in range(4):
                i = v.tensor_scalar(quarter(fm[5], q), quarter(fm[4], q), pc(par, 26 + q), pc(omka, q), ALU.mult, ALU.add)
            step(i)
            step(v.tensor_tensor(fm[1], fm[1], fm[5], ALU.mult))
            dve.wait_ge(S("kn_done"), 4)
            for q in range(4):
                i = v.scalar_tensor_tensor(out=quarter(z1, q), in0=quarter(fm[0], q), scalar=pc(par, 30 + q),
                                           in1=quarter(fm[1], q), op0=ALU.mult, op1=ALU.mult)
            step(i, "bonus_in")
            dve.wait_ge(S("rw_exp"), 3)
            step(v.scalar_tensor_tensor(out=fm[5], in0=fm[9], scalar=-1.0, in1=fm[3], op0=ALU.mult, op1=ALU.mult))
            step(v.tensor_tensor(fm[3], fm[9], fm[4], ALU.mult), "smp_in")
            step(v.tensor_tensor(fm[6], fm[0], fm[8], ALU.mult))

            def chunk_last(a):
                a4 = a.rearrange("p (q t) -> p q t", q=4)
                return (a4[:, :, 0:NP_].rearrange("p q (c j) -> p q c j", j=C)[:, :, :, C - 1],
                        a4[:, :, NP_:NT].rearrange("p q (c j) -> p q c j", j=TS)[:, :, :, TS - 1])

            step(v.tensor_copy(gamR.rearrange("p (q c) -> p q c", q=4), chunk_last(fm[8])[0]))
            step(v.tensor_tensor(fm[8], fm[1], fm[7], ALU.mult))
            step(v.tensor_tensor(fm[7], fm[3], fm[7], ALU.mult))
            dve.wait_ge(S("pj_evac"), 22)
            step(v.tensor_scalar(z0, z0, 1.0, None, ALU.add))
            step(v.reciprocal(z0, z0))
            for q in range(4):
                i = v.tensor_scalar(quarter(z0, q), quarter(z0, q), pc(omlb, q), pc(lb, q), ALU.mult, ALU.add)
            step(i)
            dve.wait_ge(S("smp_T"), 6)
            step(v.tensor_scalar(fm[4], z0, -1.0, 1.0, ALU.mult, ALU.add), "hg_f")
            step(v.tensor_scalar(fm[11], fm[11], 1.0, None, ALU.add))
            step(v.reciprocal(fm[11], fm[11]))
            step(v.tensor_tensor(fm[10], fm[10], fm[11], ALU.mult))
            dve.wait_ge(S("hg_log"), 1)
            step(v.tensor_tensor_scan(fm[9], scan_mask, fm[3], 0.0, ALU.mult, ALU.add))

            def chunks(a):
                a4 = a.rearrange("p (q t) -> p q t", q=4)
                return (a4[:, :, 0:NP_].rearrange("p q (c j) -> p q c j", j=C),
                        a4[:, :, NP_:NT].rearrange("p q (c j) -> p q c j", j=TS))

            for s, (n, mid) in enumerate(((C, C // 2 - 1), (TS, TS // 2 - 1))):
                src, dst = chunks(fm[9])[s], chunks(fm[3])[s]
                i = v.tensor_tensor(dst, src, bcast(src[:, :, :, mid:mid + 1], [P, 4, NB, n]), ALU.subtract)
            step(i, "hg_b")
            last = stat[:, 0:64].rearrange("p (q c) -> p q c", q=4)
            gam = gamH.rearrange("p (q c) -> p q c", q=4)
            for s in range(2):
                i = v.tensor_copy(last[:, :, 8 * s:8 * s + 8], chunk_last(fm[9])[s])
            step(i)
            dve.wait_ge(S("hg_exp"), 3)
            for s, n in enumerate((C, TS)):
                a = chunks(fm[9])[s]
                i = v.tensor_tensor(a, bcast(last[:, :, 8 * s:8 * s + 8].unsqueeze(3), [P, 4, NB, n]), a, ALU.subtract)
            step(i, "hg_rev")
            for s in range(2):
                v.tensor_copy(gam[:, :, 8 * s:8 * s + 8], chunk_last(fm[0])[s])
            step(v.tensor_tensor(fm[11], fm[10], fm[11], ALU.mult))
            step(v.tensor_tensor(fm[1], fm[4], fm[1], ALU.mult))
            step(v.tensor_tensor(fm[10], fm[10], fm[0], ALU.mult))
            dve.wait_ge(S("smp_st"), 96)
            v.memset(sH[:, 0:512], 0.0)
            dve.wait_ge(S("hg_exp"), 4)
            step(v.tensor_tensor(fm[4], fm[4], fm[9], ALU.mult), "hg_in")

            incl = mask4[:, P:2 * P]

            def hg_mask(n3, t):
                dve.wait_ge(S("hg_scores"), n3 + 1)
                if t < 2:
                    i = v.tensor_tensor(aT.rearrange("p (h t) -> p h t", h=4), bank[3].rearrange("p (h t) -> p h t", h=4),
                                        bcast(incl.unsqueeze(1), [P, 4, P]), ALU.mult)
                else:
                    i = v.tensor_tensor(aT[0:NS, 0:P].rearrange("p (h t) -> p h t", h=4),
                                        bank[3][0:NS, 0:P].rearrange("p (h t) -> p h t", h=4),
                                        bcast(smask[0:NS, :].unsqueeze(1), [NS, 4, NS]), ALU.mult)
                step(i, "hg_a")

            def hg_states(t):
                if t:
                    dve.wait_ge(S("hg_o"), 1)
                for c in range(4):
                    g = 4 * t + c
                    dve.wait_ge(S("hg_kv"), g + 1)
                    for h in range(HA):
                        a, b = (g % 5) * 512 + h * P, ((g + 1) % 5) * 512 + h * P
                        i = v.scalar_tensor_tensor(out=sH[:, b:b + P], in0=sH[:, a:a + P], scalar=pc(gamH, h * 16 + g),
                                                   in1=bank[4 + c][:, h * P:(h + 1) * P], op0=ALU.mult, op1=ALU.add)
                    step(i, "hg_state")

            hg_mask(0, 0)
            hg_states(0)
            hg_mask(1, 2)
            s0v = s0h.rearrange("p (b h v) -> p b h v", b=NB, h=HA)
            for h in range(HA):
                if h:
                    dve.wait_ge(S("hg_skv"), 2 * h)
                hv = hiT[0:NS, 1024 + h * P:1024 + (h + 1) * P]
                step(v.tensor_tensor(vexp[0:NS, :].rearrange("p (b v) -> p b v", b=NB), bcast(hv.unsqueeze(1), [NS, NB, P]),
                                     bcast(seqm[0:NS, :].unsqueeze(2), [NS, NB, P]), ALU.mult), "vexp")
                dve.wait_ge(S("hg_oT"), 1)
                for g in range(2):
                    a = s0v[:, 4 * g:4 * g + 4, h, :]
                    i = v.tensor_tensor(a, a, bcast(gam[:, h, 8 + 4 * g:12 + 4 * g].unsqueeze(2), [P, 4, P]), ALU.mult)
                step(i)
                for g in range(2):
                    dve.wait_ge(S("hg_skv"), 2 * h + g + 1)
                    a = s0v[:, 4 * g:4 * g + 4, h, :]
                    step(v.tensor_tensor(a, a, bank[6 + g].rearrange("p (b v) -> p b v", b=4), ALU.add), "hg_upd")
            hg_mask(2, 1)
            hg_states(1)
            dve.wait_ge(S("hg_o_evac"), 3)
            dve.wait_ge(S("hgrn_out"), 32)
            step(v.memset(s_all[:, 0:256], 0.0), "rw_in")
            def heads(a, t, n, h=HB):
                return a[0:n, t * 512:(t + 1) * 512].rearrange("p (h c) -> p h c", h=h)

            def gate_a(t):
                n = TILES[t][1]
                c = slice(t * 512, (t + 1) * 512)
                dve.wait_ge(S("oa_in"), 1)
                step(v.tensor_tensor(hgT[0:n, c], hgT[0:n, c], sgT[0:n, c], ALU.mult))
                step(v.tensor_tensor(heads(hgT, t, n, HA), heads(hgT, t, n, HA), bcast(gn_bc[0:n, :].unsqueeze(1), [n, HA, DA]), ALU.mult))
                for h in range(HA):
                    a = slice(t * 512 + h * DA, t * 512 + (h + 1) * DA)
                    i = v.scalar_tensor_tensor(out=oH[0:n, a], in0=oH[0:n, a], scalar=stat[0:n, 24 + 4 * t + h:25 + 4 * t + h],
                                               in1=hgT[0:n, a], op0=ALU.mult, op1=ALU.mult)
                step(i, "oa_done")

            def center_b(t):
                n = TILES[t][1]
                if t == 2:
                    dve.wait_ge(S("ysm_ld"), 32)
                y = heads(yO, t, n)
                sums, means = st2[0:n, 8 * t:8 * t + 8], st2[0:n, 24 + 8 * t:32 + 8 * t]
                step(v.tensor_reduce(sums, y, AX.X, ALU.add))
                step(v.tensor_scalar(means, sums, 1.0 / DB, None, ALU.mult))
                step(v.tensor_tensor(y, y, bcast(means.unsqueeze(2), [n, HB, DB]), ALU.subtract))
                step(v.tensor_tensor(sqy[0:n, :], yO[0:n, t * 512:(t + 1) * 512], yO[0:n, t * 512:(t + 1) * 512], ALU.mult))
                step(v.tensor_reduce(st2[0:n, 48 + 8 * t:56 + 8 * t], sqy[0:n, :].rearrange("p (h c) -> p h c", h=HB), AX.X, ALU.add),
                     "ob_var")

            def gate_b(n3, t):
                n = TILES[t][1]
                c = slice(t * 512, (t + 1) * 512)
                y, b = heads(yO, t, n), [n, HB, DB]
                vv = heads(vT, t, n)
                dve.wait_ge(S("bonus_evac"), 1)
                step(v.tensor_tensor(vv, vv, bcast(rkb[0:n, 8 * t:8 * t + 8].unsqueeze(2), b), ALU.mult))
                step(v.tensor_tensor(vT[0:n, c], vT[0:n, c], lnb_bc[0:n, :], ALU.add))
                dve.wait_ge(S("ob_rstd"), n3 + 1)
                step(v.tensor_tensor(y, y, bcast(st2[0:n, 72 + 8 * t:80 + 8 * t].unsqueeze(2), b), ALU.mult))
                step(v.tensor_tensor(yO[0:n, c], yO[0:n, c], lnw_bc[0:n, :], ALU.mult))
                step(v.tensor_tensor(yO[0:n, c], yO[0:n, c], vT[0:n, c], ALU.add))
                dve.wait_ge(S("g_evac"), 3)
                step(v.tensor_tensor(yO[0:n, c], yO[0:n, c], gT[0:n, c], ALU.mult), "ob_done")

            Q4 = Qm.rearrange("p (a b c) -> p a b c", a=2, b=2)
            PM4 = PM.rearrange("p (h c) -> p h c", h=4)
            X4 = Xm.rearrange("p (h c) -> p h c", h=4)
            for u in range(4):
                t, G = u // 2, u % 2
                for hh in range(4):
                    dve.wait_ge(S("rw_scores"), 4 * u + hh + 1)
                    step(v.tensor_tensor(PM4[:, hh, :], bank[4 + hh][:, :], mask4, ALU.mult), "rw_masked")
                dve.wait_ge(S("rw_L"), u + 1)
                for x in range(2):
                    step(v.tensor_tensor(Q4[:, :, x, :], bank[2 + x][:, 0:256].rearrange("p (a c) -> p a c", a=2),
                                         bcast(lower.unsqueeze(1), [P, 2, P]), ALU.mult), "rw_masked")
                step(v.tensor_tensor(X4, PM4[:, :, 0:P], bcast(ident.unsqueeze(1), [P, 4, P]), ALU.add), "rw_X")
                for lev in range(4):
                    dve.wait_ge(S("rw_XQ"), 4 * u + lev + 1)
                    step(v.tensor_tensor(Xm, Xm, bank[6][:, :], ALU.add), "rw_X")
                dve.wait_ge(S("rw_Y1"), u + 1)
                step(v.tensor_copy(yaT.rearrange("p (h c) -> p h c", h=4)[:, :, 0:64],
                                   bank[7][:, 0:256].rearrange("p (h c) -> p h c", h=4)), "rw_Y1_evac")
                dve.wait_ge(S("rw_R"), u + 1)
                rt = fm[6].rearrange("p (q t) -> p q t", q=4)[:, 2 * G:2 * G + 2, 128 * t:128 * t + 128]
                step(v.tensor_tensor(Rh.rearrange("p (q t) -> p q t", q=2), bank[7][:, 0:256].rearrange("p (q t) -> p q t", q=2),
                                     rt, ALU.add), "rw_R_evac")
                for c in range(4):
                    dve.wait_ge(S("rw_chunk"), 4 * u + c + 1)
                    step(v.tensor_tensor(phi[:, c * P:(c + 1) * P].rearrange("p (q c) -> p q c", q=2),
                                         bank[4 + c][:, 0:P].rearrange("p (q c) -> p q c", q=2),
                                         bcast(eye64.unsqueeze(1), [P, 2, 64]), ALU.add), "rw_phi")
                gr = gamR.rearrange("p (q c) -> p q c", q=4)
                for c in range(4):
                    g = 4 * t + c
                    dve.wait_ge(S("rw_chain"), 4 * u + c + 1)
                    a = (g + 1) * 256 + 2 * G * 64
                    step(v.tensor_tensor(s_all[:, a:a + P].rearrange("p (q v) -> p q v", q=2),
                                         bank[4 + c][:, P:2 * P].rearrange("p (q v) -> p q v", q=2),
                                         bcast(gr[:, 2 * G:2 * G + 2, g:g + 1], [P, 2, 64]), ALU.mult), "rw_state")
                dve.wait_ge(S("rw_y"), u + 1)
                y4 = yO[:, t * 512 + 256 * G:t * 512 + 256 * (G + 1)].rearrange("p (a b c) -> p a b c", a=2, b=2)
                v.tensor_copy(y4[:, :, 0, :], bank[2][:, 0:P].rearrange("p (a c) -> p a c", a=2))
                step(v.tensor_copy(y4[:, :, 1, :], bank[3][:, 0:P].rearrange("p (a c) -> p a c", a=2)), "rw_y_evac")
                if u == 1:
                    gate_a(0)
                if u == 2:
                    gate_a(1)
                    gate_a(2)
            for n3, t in enumerate((0, 2, 1)):
                center_b(t)
            for n3, t in enumerate((0, 2, 1)):
                gate_b(n3, t)
            for n in range(16):
                dve.wait_ge(S("branch"), n + 1)
                dve.wait_ge(S("sgate"), n // 4 + 1)
                dst, sg = mT[:, (n % 8) * NT:(n % 8 + 1) * NT], quarter(gate[n // 4], n % 4)
                if n < 8:
                    step(v.tensor_tensor(dst, bank[n % 2][:, 0:NT], sg, ALU.mult), "br_evac")
                else:
                    step(v.tensor_tensor(btmp, bank[n % 2][:, 0:NT], sg, ALU.mult), "br_evac")
                    step(v.tensor_tensor(dst, dst, btmp, ALU.add), "merged")
            dve.wait_ge(S("norm_loaded"), 32)

            def norm_rows(n, dst):
                for t, (o, rows) in enumerate(TILES):
                    dve.wait_ge(S("rstd"), 3 * n + t + 1)
                    for h in range(2):
                        src = acc(t, h) if t < 2 else res2[0:rows, h * 512:(h + 1) * 512]
                        i = v.scalar_tensor_tensor(out=dst[0:rows, t, h * 512:(h + 1) * 512], in0=src, scalar=st3[0:rows, 12 + t:13 + t],
                                                   in1=norm_bc[0:rows, h * 512:(h + 1) * 512], op0=ALU.mult, op1=ALU.mult)
                    step(i, "xn_done")

            norm_rows(1, x2)
            dve.wait_ge(S("ramp"), 1)
            dve.wait_ge(S("logits"), 1)
            v.tensor_tensor(lg[0:NS, 64:96], bank[1][0:NS, 64:96], rb_bc[0:NS, :], ALU.add)
            step(v.tensor_tensor(lg[:, 0:64].rearrange("p (t e) -> p t e", t=2), bank[1][:, 0:64].rearrange("p (t e) -> p t e", t=2),
                                 bcast(rb_bc.unsqueeze(1), [P, 2, NE]), ALU.add))
            for t in range(3):
                i = v.max(v8[:, 8 * t:8 * t + 8], lg[:, NE * t:NE * (t + 1)])
            step(i)
            for t in range(3):
                i = v.max_index(i8[:, 8 * t:8 * t + 8], v8[:, 8 * t:8 * t + 8], lg[:, NE * t:NE * (t + 1)])
            step(i)
            step(v.tensor_copy(i8f, i8[:, :]))
            top = i8f.rearrange("p (t j) -> p t j", t=3)[:, :, 0:TOPK]
            vals = v8.rearrange("p (t j) -> p t j", t=3)
            M4 = Mk.rearrange("p (t k e) -> p t k e", t=3, k=TOPK)
            k4 = [P, 3, TOPK, NE]
            step(v.tensor_tensor(M4, bcast(top.unsqueeze(3), k4), bcast(ramp[:, 0:NE].unsqueeze(1).unsqueeze(1), k4), ALU.is_equal))
            step(v.tensor_reduce(M.rearrange("p (t e) -> p t e", t=3), Mk.rearrange("p (t k e) -> p t e k", t=3, k=TOPK), AX.X, ALU.add),
                 "chosen")
            gk3 = gk.rearrange("p (t k) -> p t k", t=3)
            step(v.tensor_tensor(gk3, vals[:, :, 0:TOPK], bcast(vals[:, :, 0:1], [P, 3, TOPK]), ALU.subtract), "gk_in")
            dve.wait_ge(S("gk_exp"), 1)
            step(v.tensor_reduce(gsum[:, 0:3], gk3, AX.X, ALU.add))
            step(v.reciprocal(gsum[:, 3:6], gsum[:, 0:3]))
            step(v.tensor_tensor(gk3, gk3, bcast(gsum[:, 3:6].unsqueeze(2), [P, 3, TOPK]), ALU.mult))
            W4 = sk[:, 0:3 * TOPK * NE].rearrange("p (t k e) -> p t k e", t=3, k=TOPK)
            step(v.tensor_tensor(W4, M4, bcast(gk3.unsqueeze(3), k4), ALU.mult))
            step(v.tensor_reduce(wte.rearrange("p (t e) -> p t e", t=3), W4.rearrange("p t k e -> p t e k"), AX.X, ALU.add), "weights_ready")
            dve.wait_ge(S("ranks"), 1)
            v.tensor_copy(Rk[:, 0:64], bank[6][:, 0:64])
            v.tensor_copy(Rk[0:NS, 64:96], bank[6][0:NS, 64:96])
            step(v.tensor_copy(Ck, bank[6][:, 96:128]))
            step(v.tensor_scalar(nov, Ck, float(SLOTS), None, ALU.is_gt))
            for j in range(2, (NT - 1) // SLOTS + 1):
                step(v.scalar_tensor_tensor(out=nov, in0=Ck, scalar=float(SLOTS * j), in1=nov, op0=ALU.is_gt, op1=ALU.add))
            step(v.tensor_tensor_scan(ovend, ones[:, 0:NE], nov, 0.0, ALU.mult, ALU.add))
            le3, j3 = le.rearrange("p (j e) -> p j e", e=NE), [P, TABS - NE, NE]
            v.tensor_copy(btf[:, 0:NE], ramp[:, 0:NE])
            v.tensor_scalar(Ck[0:1, 0:OVER], ramp[0:1, 0:OVER], 2.0, ovend[0:1, NE - 1:NE], ALU.mult, ALU.is_lt)
            step(v.tensor_tensor(le3, bcast(ovend.unsqueeze(1), j3), bcast(ramp[:, 0:TABS - NE].unsqueeze(2), j3), ALU.is_le))
            step(v.tensor_reduce(btf[:, NE:TABS], le3, AX.X, ALU.add))
            v.tensor_reduce(gsum[0:1, 1:2], Ck[0:1, 0:OVER], AX.X, ALU.add)
            step(v.tensor_scalar(btf[:, 0:TABS], btf[:, 0:TABS], float(NE - 1), None, ALU.min))
            v.tensor_copy(bt[0:1, 0:TABS], btf[0:1, 0:TABS])
            v.tensor_scalar(nblk[0:1, 0:1], gsum[0:1, 1:2], float(NE // 2), None, ALU.add)
            step(v.tensor_scalar(nblk[0:1, 1:2], gsum[0:1, 1:2], 2.0, float(NE - 1), ALU.mult, ALU.add), "blocks")
            step(v.tensor_tensor(off_e, ovend, nov, ALU.subtract))
            step(v.scalar_tensor_tensor(out=off_e, in0=off_e, scalar=float(SLOTS), in1=ramp64[:, 0:NE], op0=ALU.mult, op1=ALU.subtract))
            step(v.tensor_scalar(off_e, off_e, float(SLOTS * (NE - 1)), None, ALU.add))
            d3, r3 = (a.rearrange("p (t e) -> p t e", t=3) for a in (dst_e, Rk))
            e3 = [P, 3, NE]
            step(v.scalar_tensor_tensor(out=d3, in0=r3, scalar=float(SLOTS), in1=bcast(off_e.unsqueeze(1), e3),
                                        op0=ALU.is_ge, op1=ALU.mult))
            step(v.tensor_tensor(d3, d3, r3, ALU.add))
            step(v.tensor_tensor(d3, d3, bcast(ramp64[:, 0:NE].unsqueeze(1), e3), ALU.add))
            step(v.tensor_tensor(M4, M4, bcast(d3.unsqueeze(2), k4), ALU.mult))
            step(v.tensor_reduce(dest.rearrange("p (t k) -> p t k", t=3), M4, AX.X, ALU.add))
            b4 = [P, 3, TABS, TOPK]
            q4, in4, s4 = (a.rearrange("p (t b k) -> p t b k", t=3, b=TABS) for a in (qk, inb, sk))
            tab3 = tab.rearrange("p (b s) -> p s b", s=TW)
            step(v.tensor_tensor(q4, bcast(dest.rearrange("p (t k) -> p t k", t=3).unsqueeze(2), b4),
                                 bcast(ramp64[:, 0:TABS].unsqueeze(1).unsqueeze(3), b4), ALU.subtract))
            step(v.tensor_scalar(inb, qk, 0.0, None, ALU.is_ge))
            step(v.scalar_tensor_tensor(out=inb, in0=qk, scalar=float(SLOTS), in1=inb, op0=ALU.is_lt, op1=ALU.mult))
            step(v.scalar_tensor_tensor(out=sk, in0=qk, scalar=1.0, in1=inb, op0=ALU.add, op1=ALU.mult))
            step(v.tensor_reduce(tab3[:, 0:3, :], s4, AX.X, ALU.add))
            step(v.tensor_scalar(tab3[:, 0:3, :], tab3[:, 0:3, :], -1.0, None, ALU.add))
            step(v.tensor_tensor(s4, in4, bcast(gk3.unsqueeze(2), b4), ALU.mult))
            step(v.tensor_reduce(tab3[:, 3:6, :], s4, AX.X, ALU.add))
            step(v.tensor_scalar(tab3[:, 6, :], btf[:, 0:TABS], pmod, None, ALU.is_equal))

            def onehot(out, c0, w, slots, weights=None):
                for t, (o, rows) in enumerate(TILES):
                    dst, src, s1 = out[0:rows, t * w + c0:t * w + c0 + SLOTS], ramp[0:rows, 0:SLOTS], slots[0:rows, t:t + 1]
                    if weights is None:
                        i = v.tensor_scalar(dst, src, s1, None, ALU.is_equal)
                    else:
                        i = v.tensor_scalar(dst, src, s1, weights[0:rows, t:t + 1], ALU.is_equal, ALU.mult)
                return i

            step(onehot(sel, 0, SLOTS, tab[:, 0:3]), "sel_ready")
            LOOP_STEPS = 7
            with dve.Fori(0, dve.value_load(nblk[0:1, 0:1], min_val=NE // 2, max_val=TABS // 2)) as i:
                v.tensor_copy(gselc, tab[:, bass.ds(i * (2 * TW), 2 * TW)]).then_inc(S("loop_step"), 1)
                dve.wait_ge(S("loop_step"), i * LOOP_STEPS + 1)
                for x in range(2):
                    v.tensor_scalar(ind[:, x * SLOTS:(x + 1) * SLOTS], ones[:, 0:SLOTS],
                                    gselc[:, x * TW + 6:x * TW + 7], None, ALU.mult)
                    ins = onehot(gsel, x * SLOTS, P, gselc[:, x * TW:x * TW + 3], gselc[:, x * TW + 3:x * TW + 6])
                ins.then_inc(S("gsel_ready"), 1)
                dve.wait_ge(S("gsel_ready"), i + 1)
                for x in range(2):
                    dve.wait_ge(S("picked"), i * 2 + x + 1)
                    v.tensor_copy(selc, tab[:, bass.ds(i * (2 * TW) + TW * (x + 1), 3)]).then_inc(S("loop_step"), 1)
                    dve.wait_ge(S("loop_step"), i * LOOP_STEPS + 3 * x + 2)
                    onehot(sel, 0, SLOTS, selc).then_inc(S("sel_ready"), 1)
                    dve.wait_ge(S("sel_ready"), i * 2 + x + 2)
                    dve.wait_ge(w_used, i * (2 * ECH) + (ECH * x + KT))
                    for b in range(2):
                        ins = v.tensor_scalar(glu[:, b * 256:(b + 1) * 256], bank[b][:, 0:512:2], LIMIT, None, ALU.min)
                    ins.then_inc(S("glu_ready"), 1)
                    for b in range(2):
                        ins = v.tensor_scalar(lin[:, b * 256:(b + 1) * 256], bank[b][:, 1:512:2], LIMIT, -LIMIT, ALU.min, ALU.max)
                    ins.then_inc(S("loop_step"), 1)
                    dve.wait_ge(S("loop_step"), i * LOOP_STEPS + 3 * x + 3)
                    v.scalar_tensor_tensor(out=lin, in0=lin, scalar=1.0, in1=glu, op0=ALU.add, op1=ALU.mult).then_inc(S("loop_step"), 1)
                    dve.wait_ge(S("loop_step"), i * LOOP_STEPS + 3 * x + 4)
                    dve.wait_ge(S("sig_ready"), i * 2 + x + 1)
                    v.tensor_tensor(act_s, lin, sig, ALU.mult).then_inc(S("act_ready"), 1)
                    dve.wait_ge(w_used, i * (2 * ECH) + ECH * (x + 1))
                    v.tensor_copy(yo[64 * x:64 * x + 64, 512:1024], bank[1][64:128, :]).then_inc(S("y_evac"), 1)
                    dve.wait_ge(S("act_ready"), i * 2 + x + 1)
            dve.wait_ge(S("norm_loaded"), 48)
            norm_rows(2, xr)

        @block.gpsimd
        def _(pool):
            g = nc.gpsimd

            def step(ins, name="pool_step"):
                done_wait(pool, ins, name)

            r = 0
            for a in (rwkv_mu[0], rwkv_w0[0], rwkv_a0[0], rwkv_k_k[0], rwkv_k_a[0], None, hgrn_lb_logits[0], hgrn_lb_logits[1]):
                src = rwkv_r_k[0].rearrange("(q h) n -> q (h n)", q=4) if a is None else a.rearrange("(r p) -> r p", p=P)
                n = src.shape[0]
                pool.dma_start(par_rows[r:r + n, :], src).then_inc(S("par_loaded"), 16)
                r += n
            pool.dma_start(gn_bc, hgrn_gnorm_w.partition_broadcast(P)).then_inc(S("par_loaded"), 16)
            pool.dma_start(lora[0:64, :], rwkv_w2[0]).then_inc(S("const_loaded"), 16)
            pool.dma_start(lora[64:128, :], rwkv_a2[0]).then_inc(S("const_loaded"), 16)
            pool.dma_start(g2, rwkv_g2[0]).then_inc(S("const_loaded"), 16)
            pool.dma_start(lnw_bc, rwkv_ln_w.partition_broadcast(P)).then_inc(S("const_loaded"), 16)
            pool.dma_start(lnb_bc, rwkv_ln_b.partition_broadcast(P)).then_inc(S("const_loaded"), 16)
            pool.dma_start(rb_bc, router_b.partition_broadcast(P)).then_inc(S("const_loaded"), 16)
            step(g.memset(epsc[:, 0:1], EPS), "eps")
            step(g.memset(ident, 0.0))
            step(g.memset(ones, 1.0))
            step(g.memset(mask4, 0.0))
            step(g.memset(lower, 0.0))
            step(g.memset(before, 1.0))
            step(g.memset(eye64, 0.0))
            step(g.memset(ones64, 0.0))
            step(g.memset(head2, 0.0))
            step(g.memset(smask[0:NS, :], 1.0))
            step(g.memset(seqm[0:NS, :], 1.0))
            step(g.memset(scan_mask, 1.0))

            def sel(out, op, base, pattern, mult, fill):
                return g.affine_select(out=out, in_=out, compare_op=op, fill=fill, base=base, pattern=pattern,
                                       channel_multiplier=mult)

            step(sel(ident, ALU.not_equal, 0, [[-1, P]], 1, 1.0))
            step(sel(before, ALU.is_gt, 0, [[1, P]], -1, 0.0))
            for x in range(2):
                step(sel(eye64[64 * x:64 * x + 64, :], ALU.not_equal, 0, [[-1, 64]], 1, 1.0))
                step(g.memset(ones64[64 * x:64 * x + 64, 64 * x:64 * x + 64], 1.0))
                step(g.memset(head2[64 * x:64 * x + 64, x:x + 1], 1.0))
            for c in range(4):
                rr = slice(C * c, C * c + C)
                for m in range(4):
                    step(g.memset(mask4[rr, m * P + C * c:m * P + C * c + C], 1.0))
                step(g.memset(lower[rr, C * c:C * c + C], 1.0))
            a4 = scan_mask.rearrange("p (q t) -> p q t", q=4)
            step(g.memset(a4[:, :, 0:NP_].rearrange("p q (c j) -> p q c j", j=C)[:, :, :, 0:1], 0.0))
            step(g.memset(a4[:, :, NP_:NT].rearrange("p q (c j) -> p q c j", j=TS)[:, :, :, 0:1], 0.0))
            for c in range(4):
                rr = slice(C * c, C * c + C)
                for m in range(4):
                    step(sel(mask4[rr, m * P + C * c:m * P + C * c + C], ALU.is_gt if m % 2 == 0 else ALU.is_ge, 0, [[1, C]], -1, 0.0))
                step(sel(lower[rr, C * c:C * c + C], ALU.is_gt, 0, [[-1, C]], 1, 0.0))
            sm = smask[0:NS, :].rearrange("p (b j) -> p b j", j=TS)
            step(sel(smask[0:NS, :], ALU.is_ge, 0, [[1, NS]], -1, 0.0))
            step(sel(sm, ALU.is_ge, 0, [[-TS, NB], [0, TS]], 1, 0.0))
            step(sel(seqm[0:NS, :], ALU.is_ge, 0, [[-TS, NB]], 1, 0.0))
            step(sel(seqm[0:NS, :], ALU.is_ge, TS - 1, [[TS, NB]], -1, 0.0))
            pool.wait_ge(S("const_loaded"), 16 * 6)
            step(g.memset(epsc[:, 1:2], GN_EPS), "masks")
            for x in range(2):
                step(g.memset(shE[x][:, 0:1], 0.0), "shift_zero")
            for x in range(2):
                pool.dma_start(S_s[64 * x:64 * x + 64, :],
                               state_rwkv[0][:, :, 32 * x:32 * x + 32, :].rearrange("b h v k -> h b (v k)"))\
                    .then_inc(S("smp_ld"), 16)
            pool.wait_ge(S("hg_log"), 1)
            pool.wait_ge(S("bonus_done"), 1)
            pool.dma_start(s0h.rearrange("p (b h v) -> p (b h) v", b=NB, h=HA), state_hgrn[0].rearrange("b h k v -> k (b h) v"))\
                .then_inc(S("s0h_loaded"), 16)
            pool.wait_ge(S("smp_evac"), 6)
            for a in range(6):
                pool.dma_start(smp_dram[:, :, :, a, :].rearrange("h b t c -> (b t) h c"),
                               stm[0:NS, a * 512:(a + 1) * 512].rearrange("p (h c) -> p h c", h=HB)).then_inc(S("smp_st"), 16)
            pool.wait_ge(S("smp_st"), 96)
            for x in range(2):
                pool.dma_start(vec_s[64 * x:64 * x + 64, :], smp_dram.rearrange("h b t a c -> (h b) (t a c)")).then_inc(S("smp_ld"), 16)
                pool.dma_start(v_s[64 * x:64 * x + 64, :].rearrange("p (t v) -> p t v", t=TS),
                               smp_dram[:, :, :, 5, 32 * x:32 * x + 32].rearrange("h b t v -> (h b) t v")).then_inc(S("smp_ld"), 16)
            pool.wait_ge(S("smp_ld"), 96)
            S3, T3 = (a.rearrange("p (v k) -> p v k", k=DB) for a in (S_s, tmp_s))

            def row_sums(out):
                w = DB // 2
                while w >= 1:
                    o = T3[:, :, 0:w] if w > 1 else out.unsqueeze(2)
                    step(g.tensor_tensor(o, T3[:, :, 0:w], T3[:, :, w:2 * w], ALU.add))
                    w //= 2

            def k_row(t, a):
                c = (t * 6 + a) * DB
                return bcast(vec_s[:, c:c + DB].unsqueeze(1), [P, 32, DB])

            def v_col(a):
                return bcast(a.unsqueeze(2), [P, 32, DB])

            for t in range(TS):
                step(g.tensor_tensor(T3, S3, k_row(t, 3), ALU.mult))
                row_sums(sa_s)
                step(g.tensor_tensor(S3, S3, k_row(t, 1), ALU.mult))
                step(g.tensor_tensor(T3, v_col(sa_s), k_row(t, 4), ALU.mult))
                step(g.tensor_tensor(S3, S3, T3, ALU.subtract))
                step(g.tensor_tensor(T3, v_col(v_s[:, t * 32:(t + 1) * 32]), k_row(t, 2), ALU.mult))
                step(g.tensor_tensor(S3, S3, T3, ALU.add))
                step(g.tensor_tensor(T3, S3, k_row(t, 0), ALU.mult))
                row_sums(y_s[:, t * 32:(t + 1) * 32])
            for x in range(2):
                pool.dma_start(rwkv_s[0][:, :, 32 * x:32 * x + 32, :].rearrange("b h v k -> h b (v k)"),
                               S_s[64 * x:64 * x + 64, :]).then_inc(S("rws_out"), 16)
                pool.dma_start(ysm_dram[x].rearrange("h b t v -> (h b) (t v)"), y_s[64 * x:64 * x + 64, :]).then_inc(S("ysm_st"), 16)
            pool.wait_ge(S("ysm_st"), 32)
            pool.wait_ge(S("rw_in"), 1)
            for x in range(2):
                pool.dma_start(yO[0:NS, 1024:1536].rearrange("p (h x v) -> p h x v", h=HB, x=2)[:, :, x, :],
                               ysm_dram[x].rearrange("h b t v -> (b t) h v")).then_inc(S("ysm_ld"), 16)
            pool.dma_start(rw_sb.rearrange("p (k e) -> p k e", k=KT), router_w[0].rearrange("(k p) e -> p k e", p=P))\
                .then_inc(S("router_loaded"), 16)
            pool.wait_ge(S("kn_done"), 4)
            pool.wait_ge(S("merged"), 8)
            step(g.iota(ramp_i.rearrange("p (a b) -> p a b", a=2), pattern=[[0, 2], [1, SLOTS]], base=0, channel_multiplier=0))
            step(g.tensor_copy(ramp, ramp_i))
            pool.wait_ge(S("rw_end"), 1)
            step(g.memset(lg, 0.0))
            step(g.memset(Rk, 0.0))
            for x in range(4):
                step(g.iota(ramp_i[NE * x:NE * x + NE, 0:1], pattern=[[0, 1]], base=0, channel_multiplier=1))
            step(g.tensor_copy(pmod, ramp_i[:, 0:1]))
            step(g.tensor_scalar(ramp64, ramp[:, 0:64], float(SLOTS), None, ALU.mult), "ramp")
            pool.wait_ge(S("braw_loaded"), 48)
            step(g.memset(bgu3[32:64, :], 0.0))
            step(g.tensor_copy(bgu3[0:32, :], braw[0:32, :]))
            step(g.tensor_copy(bgu3[64:128, :], braw[64:128, :]))
            for r in (slice(64, 128), slice(96, 128)):
                step(g.tensor_tensor(braw[r, :], braw[r, :], bgu3[r, :], ALU.subtract))
                i = g.tensor_copy(bgu3[r, :], braw[r, :])
                step(i, "bgu3" if r.start == 96 else "pool_step")
            pool.wait_ge(S("logits"), 1)
            g.memset(GT, 0.0).then_inc(S("gt_evac"), 1)
            for x in range(2):
                g.memset(yo[:, x * 512:(x + 1) * 512], 0.0).then_inc(S("y_evac"), 1)


_INS = ("x_prompt", "x_sample", "state_hgrn", "state_rwkv", "state_shift", "norm1_w", "w_in", "hgrn_lb_logits", "hgrn_gnorm_w",
        "rwkv_mu", "rwkv_w0", "rwkv_w2", "rwkv_a0", "rwkv_a2", "rwkv_g2", "rwkv_k_k", "rwkv_k_a", "rwkv_r_k", "rwkv_ln_w",
        "rwkv_ln_b", "w_branch_a", "w_branch_b", "w_out", "norm2_w", "router_w", "router_b", "expert_w_gu", "expert_b_gu",
        "expert_w_down", "expert_b_down", "final_norm_w")
_OUTS = ((1, NP_, D), (NB, TS, D), (1, 1, HA, DA, DA), (1, 1, HB, DB, DB), (1, 1, D), (1, NB, HA, DA, DA), (1, NB, HB, DB, DB),
         (1, NB, D))


def kernel(**inputs):
    import numpy as _np
    import concourse.bacc as _bacc
    from concourse import mybir as _mybir
    from concourse.bass_utils import run_bass_kernel_spmd as _run

    nc = _bacc.Bacc("TRN2", target_bir_lowering=False, num_devices=1)
    arrays, args = {}, []
    for name in _INS:
        a = _np.ascontiguousarray(inputs[name])
        arrays[f"in_{name}_dram"] = a
        args.append(nc.dram_tensor(f"in_{name}_dram", a.shape, _mybir.dt.from_np(a.dtype), kind="ExternalInput").ap())
    for i, shape in enumerate(_OUTS):
        args.append(nc.dram_tensor(f"out_{i}_dram", shape, _mybir.dt.float32, kind="ExternalOutput").ap())
    layer_kernel(nc, *args)
    r = _run(nc, [arrays], core_ids=[0])
    return tuple(r.results[0][f"out_{i}_dram"] for i in range(len(_OUTS)))
```

```python
from contextlib import ExitStack

import concourse.bass as bass
from concourse import mybir

P = 128
F32 = mybir.dt.float32
I32 = mybir.dt.int32
BF16 = mybir.dt.bfloat16
U32 = mybir.dt.uint32
ALU = mybir.AluOpType
ACT = mybir.ActivationFunctionType
AX = mybir.AxisListType

D = 1024
KT = D // P
NP_, NS = 256, 32
NB, TS = 8, 4
NT = NP_ + NS
NX = NT + NB
TILES = [(0, 128), (128, 128), (256, 32)]
HA, DA = 4, 128
HB, DB = 8, 64
DR = HB * DB
C = 32
NC_P = NP_ // C
FM = 4 * NT
NE, TOPK = 32, 4
DFF = 1024
EPS = 1e-6
GN_EPS = 64e-5
LIMIT, ALPHA = 7.0, 1.702
W_SCALE = -0.6065306597126334

SLOTS = 64
OVER = (NT * TOPK) // (SLOTS + 1)
BLOCKS = NE + OVER
TABS = BLOCKS + 2
TW = 7
RING, CH = 12, 2048
RING_MIX = 4
CPC = 256
N_IN = 23
MIX_CHUNKS = N_IN + 4 + 4
ECH = 12


def bcast(ap, shape):
    return ap.to_broadcast(shape)


def layer_kernel(nc, x_prompt, x_sample, state_hgrn, state_rwkv, state_shift, norm1_w, w_in, hgrn_lb_logits,
                 hgrn_gnorm_w, rwkv_mu, rwkv_w0, rwkv_w2, rwkv_a0, rwkv_a2, rwkv_g2, rwkv_k_k, rwkv_k_a,
                 rwkv_r_k, rwkv_ln_w, rwkv_ln_b, w_branch_a, w_branch_b, w_out, norm2_w, router_w, router_b,
                 expert_w_gu, expert_b_gu, expert_w_down, expert_b_down, final_norm_w,
                 y_prompt, y_sample, hgrn_p, rwkv_p, shift_p, hgrn_s, rwkv_s, shift_s):
    ctx = ExitStack()
    with ctx:
        def sb(name, cols, dt=F32, rows=P):
            return ctx.enter_context(nc.sbuf_tensor(name, [rows, cols], dt))

        def sem(name):
            return ctx.enter_context(nc.semaphore(name))

        ring = sb("ring", RING * CH)
        arena = sb("arena", 28392)
        at = [0]

        def take(n):
            a = arena[:, at[0]:at[0] + n]
            at[0] += n
            return a

        ident = take(128)
        mask4 = take(512)
        lower = take(128)
        eye64 = take(64)
        ones64 = take(128)
        before = take(128)
        ones = take(128)
        head2 = take(2)
        gn_bc = take(128)
        off_lnw = at[0]
        lnw_bc = take(512)
        lnb_bc = take(512)
        rb_bc = take(32)
        off_lora = at[0]
        lora = take(512)
        g2 = take(512)
        scan_mask = take(FM)
        norm_bc = take(D)
        par = take(42)
        npar = take(42)
        smask = take(32)
        seqm = take(8)
        stat = take(64)
        gamR = take(4 * NC_P)
        gamH = take(4 * (NC_P + NB))
        wS = take(4 * NS)
        rkb = take(24)
        lb = take(4)
        omlb = take(4)
        omka = take(4)
        xnT = take(KT * NX)
        fm = [take(FM) for _ in range(12)]
        tm = take(4 * 3 * 512)
        hiT, hgT, vT, gT = (tm[:, i * 1536:(i + 1) * 1536] for i in range(4))

        scratch = ring[:, RING_MIX * CH:]
        PL, HR, ZR = scratch[:, 0:5952], scratch[:, 5952:11072], scratch[:, 11072:16384]
        xs = HR[:, 0:3 * D].rearrange("p (t d) -> p t d", t=3)
        xn = ZR[:, 0:3 * D].rearrange("p (t d) -> p t d", t=3)
        shE = [PL[:, 4096 + 297 * i:4096 + 297 * (i + 1)] for i in range(2)]
        shD = PL[:, 4690:4690 + NT]
        waT = PL[:, 4978:4978 + NT]
        glT = PL[:, 5266:5266 + NT]
        z0, z1 = ZR[:, 0:FM], ZR[:, FM:2 * FM]
        par_rows = scratch[:, 11072 + 3 * D:11072 + 3 * D + 128]
        S_s = PL[:, 0:2048]
        tmp_s = PL[:, 2048:4096]
        vec_s = PL[:, 4096:5632]
        v_s = PL[:, 5632:5760]
        sa_s = PL[:, 5760:5792]
        y_s = PL[:, 5792:5920]
        stm = HR[:, 0:3072]
        ktT, aT, sH, oH = HR[:, 0:512], HR[:, 512:1024], HR[:, 1024:3584], HR[:, 3584:5120]
        s0h, vexp = ZR[:, 0:4096], ZR[:, 4096:5120]
        yaT, wta, yO, Qm, Xm = (HR[:, 0:512], HR[:, 512:1024], HR[:, 1024:2560], HR[:, 2560:3072],
                                HR[:, 3072:3584])
        PM, PQ, phi, Rh = ZR[:, 0:2048], ZR[:, 2048:4096], ZR[:, 4096:4608], ZR[:, 4608:4864]
        bnT, knT = fm[9][:, 0:256], fm[9][:, 256:512]
        off3 = at[0] - 4 * 1536 - 12 * FM
        s_all = arena[:, off3 + 3 * FM:off3 + 3 * FM + 9 * 256]
        gate = [fm[i] for i in (0, 1, 10, 11)]
        qm = fm[3]

        bank = [ctx.enter_context(nc.psum_tensor(f"bank{i}", [P, 512], F32)) for i in range(8)]

        late = sb("late", 136)
        lt = [0]

        def ltake(n):
            a = late[:, lt[0]:lt[0] + n]
            lt[0] += n
            return a

        epsc = ltake(2)
        sgT = arena[:, off_lora:off_lora + 3 * 512]
        sq = arena[:, off_lora + 3 * 512:off_lora + 4 * 512]
        sq2 = fm[1][:, 0:1024]
        oaT = fm[5]
        ramp = ones64
        ramp_i = fm[11].bitcast(I32)[:, 0:2 * SLOTS]
        rw_sb = fm[9][:, 512:512 + KT * NE]
        tab = fm[11][:, 720:720 + TABS * TW]
        st2 = ltake(96)
        st3 = ltake(24)
        gselc, selc = ltake(2 * TW), st3[:, 15:18]
        obT = fm[6]
        mT = arena[:, off3 + 7 * FM:off3 + 9 * FM]
        sqy = arena[:, off_lora + 3 * 512:off_lora + 4 * 512]
        btmp = PQ[:, 0:NT]
        xr = tm[:, 0:3 * D].rearrange("p (t d) -> p t d", t=3)
        x2 = tm[:, 3 * D:6 * D].rearrange("p (t d) -> p t d", t=3)
        res2 = fm[0][:, 0:D]
        x2T = xnT[:, 0:KT * NT]
        rt = [off3 + 2 * FM]

        def rtake(n):
            a = arena[:, rt[0]:rt[0] + n]
            rt[0] += n
            return a

        lg, v8, i8f, gk = rtake(96), rtake(24), rtake(24), rtake(12)
        gsum, Mk, M, Rk = rtake(6), rtake(384), rtake(96), rtake(96)
        dst_e, off_e, dest, Ck = rtake(96), rtake(NE), rtake(12), rtake(NE)
        nov, ovend, ramp64, btf = rtake(NE), rtake(NE), rtake(64), rtake(64)
        wte, pmod = rtake(96), rtake(1)
        qk, inb, sk = (rtake(3 * TABS * TOPK) for _ in range(3))
        le = qk[:, 0:(TABS - NE) * NE]
        wT = fm[1][0:NE, 0:NT]
        bt = ctx.enter_context(nc.sbuf_tensor("block_table", [1, 64], I32))
        nblk = ctx.enter_context(nc.sbuf_tensor("block_count", [1, 2], I32))
        i8 = ctx.enter_context(nc.sbuf_tensor("expert_index", [P, 24], U32))
        braw = arena[:, off_lora:off_lora + 2 * DFF]
        bdn = arena[0:NE, off_lnw:off_lnw + D]
        bgu3 = fm[6][:, 0:DFF].bitcast(BF16)
        glu, lin = fm[0][:, 0:512], fm[0][:, 512:1024]
        sig, act_s = fm[1][:, 0:512], fm[1][:, 512:1024]
        xg = fm[7][:, 0:512]
        xT, actT = fm[10][:, 0:512], fm[10][:, 512:1024]
        yo, GT = fm[9][:, 0:D], fm[8][:, 0:NT]
        sel, gsel = fm[11][:, 0:3 * SLOTS], fm[11][:, 256:256 + 6 * SLOTS]
        ind = fm[11][:, 640:704].bitcast(BF16)

        smp_dram = nc.dram_tensor("smp_dram", [HB, NB, TS, 6, DB], F32, kind="Internal").ap()
        ysm_dram = nc.dram_tensor("ysm_dram", [2, HB, NB, TS, 32], F32, kind="Internal").ap()

        names = {}

        def S(name):
            if name not in names:
                names[name] = sem(name)
            return names[name]

        counts = {}

        def done(ins, name):
            ins.then_inc(S(name), 1)
            counts[name] = counts.get(name, 0) + 1
            return counts[name]

        def done_wait(eng, ins, name):
            eng.wait_ge(S(name), done(ins, name))

        ring_loaded = [sem(f"ring_loaded{i}") for i in range(RING_MIX)]
        w_loaded = [sem(f"w_loaded{c}") for c in range(KT)] + ring_loaded
        w_used = sem("w_used")

        v_in = w_in[0].rearrange("(k p) c -> p k c", p=P)
        HGRN0, RW0, GATE0 = 0, 2048, 3840
        starts = [RW0 + CPC * i for i in range(7)] + [CPC * i for i in range(8)] + [GATE0 + CPC * i for i in range(8)]
        ba, bb, wo = (w.rearrange("(k p) c -> p k c", p=P) for w in (w_branch_a[0], w_branch_b[0], w_out[0]))

        def mix_chunk(n):
            s = n % RING_MIX if n < N_IN + 6 else n - (N_IN + 6) + RING_MIX
            slot = ring[:, s * CH:(s + 1) * CH]
            if n < N_IN:
                return slot.rearrange("p (k c) -> p k c", k=KT), v_in[:, :, starts[n]:starts[n] + CPC]
            n -= N_IN
            src, k0 = [(ba, 0), (ba, 2), (bb, 0), (bb, 2), (wo, 0), (wo, 2), (wo, 4), (wo, 6)][n]
            return slot.rearrange("p (k c) -> p k c", k=2), src[:, k0:k0 + 2, :]

        v_gu = expert_w_gu[0].rearrange("e (k p) c -> e p k c", p=P)
        v_dn = expert_w_down[0].rearrange("e (k p) c -> e p k c", p=P)

        def w_slot(c):
            s = c + RING_MIX if c < KT else c - KT
            return ring[:, s * CH:(s + 1) * CH]

        def w_at(c, second):
            return extra[c][0] if second and c < len(extra) else w_slot(c)

        def w_load(eng, e, c, second=False):
            loaded = S(extra[c][1]) if second and c < len(extra) else w_loaded[c]
            if c < KT:
                eng.dma_start(w_at(c, second), v_gu[bass.ds(e, 1), :, c, :].rearrange("e p c -> (e p) c")).then_inc(loaded, 16)
            else:
                k = 2 * (c - KT)
                eng.dma_start(w_slot(c).rearrange("p (k c) -> p k c", k=2),
                              v_dn[bass.ds(e, 1), :, k:k + 2, :].rearrange("e p k c -> (e p) k c")).then_inc(loaded, 16)

        extra = [(tm[:, 0:CH], "xr_loaded", 64), (braw, "braw_loaded", 64), (xnT[:, 0:CH], "shift_loaded", 32)]

        def pe_w_wait(c, i, x, first):
            if first and x == 1 and c < len(extra):
                nc.tensor.wait_ge(S(extra[c][1]), extra[c][2])
                return
            earlier = int(c < 2) if c < KT else len(range(c - KT, MIX_CHUNKS - 2, RING_MIX))
            if not first and c < len(extra):
                earlier -= 1
            nc.tensor.wait_ge(w_loaded[c], i * 32 + 16 * (earlier + 1 + x))

        def acc(t, half):
            return bank[2 + 2 * t + half][:, :] if t < 2 else bank[7][NS * half:NS * half + NS, :]

        block = ctx.enter_context(nc.Block())

        def pj_after(n):
            return 2 * (n + 1) if n < 11 else 27 if n < 13 else 32 if n < 15 else 32 + 2 * (n - 14)

        E_BLOCK = 32

        @block.sync
        def _(sp):
            for t, (o, n) in enumerate(TILES):
                src = x_prompt[0, o:o + n, :] if t < 2 else x_sample.rearrange("b t d -> (b t) d")
                sp.dma_start(xs[0:n, t, :], src).then_inc(S(f"x_loaded{t}"), 16)
            sp.dma_start(xn[NS:NS + NB, 2, :], state_shift[0]).then_inc(S("shift_loaded"), 16)
            sp.dma_start(norm_bc, norm1_w.partition_broadcast(P)).then_inc(S("norm_loaded"), 16)
            for n in list(range(N_IN + 4)) + [N_IN + 6, N_IN + 7, N_IN + 4, N_IN + 5]:
                if n == N_IN + 6:
                    sp.wait_ge(S("oa_done"), 3)
                    for t, (o, rows) in enumerate(TILES):
                        src = x_prompt[0, o:o + rows, :] if t < 2 else x_sample.rearrange("b t d -> (b t) d")
                        sp.dma_start(xr[0:rows, t, :], src).then_inc(S("xr_loaded"), 16)
                    sp.dma_start(norm_bc, norm2_w.partition_broadcast(P)).then_inc(S("norm_loaded"), 16)
                    sp.wait_ge(S("rws_out"), 32)
                if n >= RING_MIX and n < N_IN + 6:
                    m = n - RING_MIX
                    if m < N_IN:
                        sp.wait_ge(S("pj_done"), pj_after(m))
                    else:
                        sp.wait_ge(S("branch"), 8)
                if n == 1:
                    sp.wait_ge(S("par_loaded"), 16 * 9)
                dst, src = mix_chunk(n)
                sp.dma_start(dst, src).then_inc(ring_loaded[n % RING_MIX] if n < N_IN + 6 else w_loaded[n - N_IN - 6], 16)
            sp.wait_ge(S("ob_var"), 3)
            for x in (0, 2, 3):
                sp.dma_start(braw[NE * x:NE * x + NE, :], expert_b_gu[0]).then_inc(S("braw_loaded"), 16)
            sp.wait_ge(S("merged"), 8)
            sp.dma_start(bdn, expert_b_down[0]).then_inc(S("bdn_loaded"), 16)
            sp.wait_ge(S("rwp_out"), 16)
            sp.wait_ge(S("ysm_st"), 32)
            for c in range(2, KT):
                w_load(sp, 0, c)
            sp.wait_ge(S("wo_done"), 3)
            for c in [0, 1] + list(range(KT, ECH)):
                w_load(sp, 0, c)
            w_load(sp, 1, 0, True)
            sp.wait_ge(S("xn_done"), 6)
            sp.dma_start(norm_bc, final_norm_w.partition_broadcast(P)).then_inc(S("norm_loaded"), 16)
            sp.wait_ge(S("bgu3"), 1)
            w_load(sp, 1, 1, True)
            sp.wait_ge(S("logits"), 1)
            w_load(sp, 1, 2, True)
            for c in range(len(extra), ECH):
                sp.wait_ge(w_used, c + 1)
                w_load(sp, 1, c)
            sp.wait_ge(S("blocks"), 1)
            with sp.Fori(1, sp.value_load(nblk[0:1, 1:2], min_val=NE - 1, max_val=TABS - 2)) as i:
                e = sp.value_load(bt[0:1, bass.ds(i + 1, 1)], min_val=0, max_val=NE - 1)
                for c in range(ECH):
                    sp.wait_ge(w_used, i * ECH + (c + 1))
                    w_load(sp, e, c)
            for t, (o, rows) in enumerate(TILES):
                sp.wait_ge(S("xn_done"), 6 + t + 1)
                dst = y_prompt[0, o:o + rows, :] if t < 2 else y_sample.rearrange("b t d -> (b t) d")
                sp.dma_start(dst, xr[0:rows, t, :]).then_inc(S("y_out"), 16)
            sp.wait_ge(S("shift_out"), 32)
            sp.wait_ge(S("hgrn_out"), 32)
            sp.wait_ge(S("rws_out"), 32)
            sp.wait_ge(S("rwp_out"), 16)
            sp.wait_ge(S("y_out"), 48)

        @block.tensor
        def _(pe):
            mm = nc.tensor.matmul

            def chunk_ready(n):
                if n < N_IN + 6:
                    pe.wait_ge(ring_loaded[n % RING_MIX], 16 * (n // RING_MIX + 1))
                else:
                    pe.wait_ge(w_loaded[n - N_IN - 6], 16)

            pe.wait_ge(S("ident"), 1)
            for t, (o, n) in enumerate(TILES):
                pe.wait_ge(S("xn_done"), t + 1)
                if t == 2:
                    pe.wait_ge(S("shift_loaded"), 16)
                rows = n if t < 2 else NS + NB
                for k in range(KT):
                    b = bank[2 * t + k // 4] if t < 2 else bank[4]
                    c = (k % 4) * 128 if t < 2 else k * 40
                    i = nc.tensor.transpose(b[:, c:c + rows], xn[0:rows, t, k * P:(k + 1) * P], ident[0:rows, 0:rows])
                    if k % 4 == 3 and (t < 2 or k == 7):
                        done(i, "xT_done")
            xv = xnT.rearrange("p (k t) -> p k t", k=KT)

            def project(k, n, j, cols):
                slot, _ = mix_chunk(n)
                b = bank[k % 4] if k < E_BLOCK else bank[k % 2]
                for kt in range(KT):
                    i = mm(b[:, 0:cols], slot[:, kt, j * P:(j + 1) * P], xv[:, kt, 0:cols], start=(kt == 0), stop=(kt == KT - 1))
                done(i, "pj_done")

            def bank_free(k):
                if k >= E_BLOCK:
                    pe.wait_ge(S("pj_evac"), max(E_BLOCK, k - 1))
                elif k >= 4:
                    pe.wait_ge(S("pj_evac"), k - 3)

            pe.wait_ge(S("xT_evac"), 5)
            for k in range(22):
                n = k // 2
                if k % 2 == 0:
                    chunk_ready(n)
                bank_free(k)
                project(k, n, k % 2, NX if k < 14 else NT)
                if k == 0:
                    pe.wait_ge(S("par_loaded"), 16 * 9)
                    done(nc.tensor.transpose(bank[5][:, 0:42], par_rows[0:42, :], ident[0:42, 0:42]), "par_T")
                if k == 17:
                    pe.wait_ge(S("masks"), 1)
                    pe.wait_ge(S("lora_in"), 1)
                    for q in range(4):
                        if q >= 2:
                            pe.wait_ge(S("lora_evac"), q - 1)
                        mm(bank[4 + q % 2][:, 0:NT], lora[0:64, q * P:(q + 1) * P], waT[0:64, :], start=True, stop=True)
                        done(mm(bank[6 + q % 2][:, 0:NT], lora[64:128, q * P:(q + 1) * P], waT[64:128, :],
                                start=True, stop=True), "lora_done")
                    for q in range(4):
                        pe.wait_ge(S("ksq"), 1)
                        pe.wait_ge(S("lora_evac"), 3 + min(q, 1))
                        if q >= 2:
                            pe.wait_ge(S("kn_evac"), q - 1)
                        done(mm(bank[4 + q % 2][:, 0:NT], ones64, z1[:, q * NT:(q + 1) * NT], start=True, stop=True),
                             "kn_done")
            k = 22
            for n in range(11, 15):
                chunk_ready(n)
                slot, _ = mix_chunk(n)
                for t in range(2):
                    bank_free(k)
                    for kt in range(KT):
                        i = mm(bank[k % 4][:, 0:CPC], xv[:, kt, P * t:P * (t + 1)], slot[:, kt, :],
                               start=(kt == 0), stop=(kt == KT - 1))
                    done(i, "pj_done")
                    k += 1
                if n % 2 == 0:
                    before_slot, _ = mix_chunk(n - 1)
                    bank_free(k)
                    for kt in range(KT):
                        for x, w in enumerate((before_slot, slot)):
                            i = mm(bank[k % 4][NS * x:NS * x + NS, 0:CPC], xv[:, kt, NP_:NT], w[:, kt, :],
                                   start=(kt == 0), stop=(kt == KT - 1), skip_group_check=True)
                    done(i, "pj_done")
                    k += 1
                if n == 12:
                    pe.wait_ge(S("bonus_in"), 1)
                    for t, (o, rows) in enumerate(TILES):
                        for q in range(4):
                            i = mm(bank[6][0:rows, t * 8 + 2 * q:t * 8 + 2 * q + 2], z1[:, q * NT + o:q * NT + o + rows],
                                   head2, start=True, stop=True)
                    done(i, "bonus_done")
                    pe.wait_ge(S("recip"), 2)
                    for t, (o, rows) in enumerate(TILES):
                        b = bank[(4, 5, 7)[t]]
                        done(mm(b[0:rows, :], glT[:, o:o + rows], g2, start=True, stop=True), "g_done")
                    pe.wait_ge(S("smp_in"), 1)
                    srcs = [fm[0], wS, fm[1], fm[9], fm[3], fm[2]]
                    for a, src in enumerate(srcs):
                        b = bank[(4, 5, 7)[a % 3]]
                        if a < 3:
                            pe.wait_ge(S("g_evac"), a + 1)
                        else:
                            pe.wait_ge(S("smp_evac"), a - 2)
                        for q in range(4):
                            v = src[:, q * NS:(q + 1) * NS] if a == 1 else src[:, q * NT + NP_:(q + 1) * NT]
                            i = nc.tensor.transpose(b[0:NS, q * P:(q + 1) * P], v, ident)
                        done(i, "smp_T")

            pe.wait_ge(S("smp_evac"), 6)
            pe.wait_ge(S("hg_in"), 1)
            qt, kt_, qh, kh = fm[10], fm[4], fm[11], fm[1]

            def f4(a, h, o, n):
                return a[:, h * NT + o:h * NT + o + n]

            pe.wait_ge(S("pj_evac"), E_BLOCK)
            gate_k = [E_BLOCK]

            def gate_tile():
                k = gate_k[0]
                if k >= E_BLOCK + 16:
                    return
                gate_k[0] += 1
                n = 15 + (k - E_BLOCK) // 2
                if k % 2 == 0:
                    chunk_ready(n)
                bank_free(k)
                project(k, n, k % 2, NT)

            def hgrn_prompt(t, i3):
                o = 128 * t
                if i3:
                    pe.wait_ge(S("hg_o_evac"), i3)
                for h in range(HA):
                    i = nc.tensor.transpose(bank[2][:, h * P:(h + 1) * P], f4(kt_, h, o, P), ident)
                done(i, "hg_kT")
                if i3:
                    pe.wait_ge(S("hg_a"), i3)
                for h in range(HA):
                    i = mm(bank[3][:, h * P:(h + 1) * P], f4(kh, h, o, P), f4(qh, h, o, P), start=True, stop=True)
                done(i, "hg_scores")
                pe.wait_ge(S("hg_kT_evac"), i3 + 1)
                if t:
                    pe.wait_ge(S("hg_upd"), 8)
                for c in range(4):
                    r = slice(C * c, C * c + C)
                    for h in range(HA):
                        i = mm(bank[4 + c][:, h * P:(h + 1) * P], ktT[r, h * P:(h + 1) * P],
                               hiT[r, t * 512 + h * P:t * 512 + (h + 1) * P], start=True, stop=True)
                    done(i, "hg_kv")
                pe.wait_ge(S("hg_a"), i3 + 1)
                for h in range(HA):
                    mm(bank[2][:, h * P:(h + 1) * P], aT[:, h * P:(h + 1) * P],
                       hiT[:, t * 512 + h * P:t * 512 + (h + 1) * P], start=(h == 0), stop=False, skip_group_check=True)
                if t:
                    gate_tile()
                for c in range(4):
                    g = 4 * t + c
                    if g == 0:
                        continue
                    pe.wait_ge(S("hg_state"), g)
                    for h in range(HA):
                        i = mm(bank[2][C * c:C * c + C, h * P:(h + 1) * P], f4(qt, h, o + C * c, C),
                               sH[:, (g % 5) * 512 + h * P:(g % 5) * 512 + (h + 1) * P], start=False, stop=True,
                               skip_group_check=True)
                done(i, "hg_o")

            def hgrn_sample():
                pe.wait_ge(S("hg_o_evac"), 1)
                for h in range(HA):
                    i = nc.tensor.transpose(bank[2][0:NS, h * P:(h + 1) * P], f4(kt_, h, NP_, NS), ident)
                done(i, "hg_kT")
                for h in range(HA):
                    i = mm(bank[3][0:NS, h * NS:(h + 1) * NS], f4(kh, h, NP_, NS), f4(qh, h, NP_, NS),
                           start=True, stop=True)
                done(i, "hg_scores")
                pe.wait_ge(S("hg_state"), 4)
                pe.wait_ge(S("hg_a"), 2)
                for h in range(HA):
                    mm(bank[4][NS * h:NS * h + NS, 0:P], aT[0:NS, h * NS:(h + 1) * NS],
                       hiT[0:NS, 1024 + h * P:1024 + (h + 1) * P], start=True, stop=False, skip_group_check=True)
                pe.wait_ge(S("s0h_loaded"), 16)
                for b in range(NB):
                    for h in range(HA):
                        i = mm(bank[4][NS * h:NS * h + NS, 0:P], qm[:, h * NT + NS * b:h * NT + NS * b + NS],
                               s0h[:, (b * HA + h) * P:(b * HA + h + 1) * P], start=False, stop=(b == NB - 1),
                               skip_group_check=True)
                done(i, "hg_o")
                pe.wait_ge(S("hg_kT_evac"), 2)
                for h in range(HA):
                    if h:
                        gate_tile()
                    pe.wait_ge(S("vexp"), h + 1)
                    for g in range(2):
                        if h:
                            pe.wait_ge(S("hg_upd"), 2 * (h - 1) + g + 1)
                        done(mm(bank[6 + g][:, :], ktT[0:NS, h * P:(h + 1) * P], vexp[0:NS, g * 512:(g + 1) * 512],
                                start=True, stop=True), "hg_skv")

            hgrn_prompt(0, 0)
            hgrn_sample()
            hgrn_prompt(1, 2)

            vR, At, Rt, Bn, Kn = fm[2], fm[5], fm[6], fm[7], fm[8]
            AR = arena[:, off3 + 5 * FM:off3 + 7 * FM].rearrange("p (a t) -> p a t", a=2)
            pe.wait_ge(S("hg_o_evac"), 3)
            pe.wait_ge(S("hg_state"), 8)
            pe.wait_ge(S("rw_in"), 1)
            for u in range(4):
                t, G = u // 2, u % 2
                o = 128 * t
                if u:
                    pe.wait_ge(S("rw_y_evac"), u)
                for q in range(2):
                    for a, src in enumerate((At, Bn, Kn, vR)):
                        i = nc.tensor.transpose(bank[2 + a // 2][:, (a % 2) * 256 + q * P:(a % 2) * 256 + (q + 1) * P],
                                                f4(src, 2 * G + q, o, P), ident)
                done(i, "rw_T")
                if u:
                    pe.wait_ge(S("rw_state"), 4 * u)
                for hh in range(4):
                    q, r = 2 * G + hh // 2, slice(64 * (hh % 2), 64 * (hh % 2) + 64)
                    c0 = q * NT + o
                    ar = AR[r, :, c0:c0 + P]
                    b = bank[4 + hh]
                    mm(b[:, 0:256], Bn[r, c0:c0 + P], ar, start=True, stop=True)
                    done(mm(b[:, 256:512], Kn[r, c0:c0 + P], ar, start=True, stop=True), "rw_scores")
                pe.wait_ge(S("rw_T_evac"), u + 1)
                for hh in range(4):
                    q, r = 2 * G + hh // 2, slice(64 * (hh % 2), 64 * (hh % 2) + 64)
                    c0 = q * NT + o
                    i = mm(bank[2 + hh % 2][:, (hh // 2) * P:(hh // 2 + 1) * P], At[r, c0:c0 + P], Bn[r, c0:c0 + P],
                           start=True, stop=True)
                done(i, "rw_L")
                gate_tile()
                for lev in range(4):
                    if lev == 0:
                        pe.wait_ge(S("rw_masked"), 6 * (u + 1))
                    else:
                        pe.wait_ge(S("rw_sq_evac"), 4 * u + lev)
                    src, dst = (PQ[:, 0:1024], PQ[:, 1024:2048])[::1 if lev % 2 else -1]
                    for hh in range(4):
                        if lev == 0:
                            Pm, Q = PM[:, hh * 512:hh * 512 + P], Qm[:, hh * P:(hh + 1) * P]
                        else:
                            Pm, Q = src[:, hh * 256:hh * 256 + P], src[:, hh * 256 + P:(hh + 1) * 256]
                        b, c0 = bank[4 + hh // 2], (hh % 2) * 256
                        if lev < 3:
                            mm(b[:, c0:c0 + P], Q, Pm, start=True, stop=True)
                        i = mm(b[:, c0 + P:c0 + 256], Pm, Q, start=True, stop=True)
                    done(i, "rw_sq")
                    if lev < 2:
                        gate_tile()
                    pe.wait_ge(S("rw_sq_evac"), 4 * u + lev + 1)
                    pe.wait_ge(S("rw_X"), 5 * u + lev + 1)
                    for hh in range(4):
                        i = mm(bank[6][:, hh * P:(hh + 1) * P], dst[:, hh * 256 + P:(hh + 1) * 256],
                               Xm[:, hh * P:(hh + 1) * P], start=True, stop=True)
                    done(i, "rw_XQ")
                for hh in range(4):
                    i = mm(bank[7][:, hh * 64:(hh + 1) * 64], PM[:, hh * 512 + 256:hh * 512 + 384],
                           vT[:, t * 512 + (4 * G + hh) * 64:t * 512 + (4 * G + hh + 1) * 64], start=True, stop=True)
                done(i, "rw_Y1")
                pe.wait_ge(S("rw_X"), 5 * u + 5)
                pe.wait_ge(S("rw_Y1_evac"), u + 1)
                for hh in range(4):
                    i = mm(bank[6][:, hh * P:(hh + 1) * P], Xm[:, hh * P:(hh + 1) * P], yaT[:, hh * P:(hh + 1) * P],
                           start=True, stop=True)
                done(i, "rw_WT")
                pe.wait_ge(S("rw_WT_evac"), u + 1)
                for hh in range(4):
                    i = mm(bank[7][64 * (hh % 2):64 * (hh % 2) + 64, (hh // 2) * P:(hh // 2 + 1) * P],
                           wta[:, hh * P + 64:(hh + 1) * P], PM[:, hh * 512 + P:hh * 512 + 256], start=True, stop=True)
                done(i, "rw_R")
                for hh in range(4):
                    out = bank[2 + hh % 2][:, (hh // 2) * 64:(hh // 2 + 1) * 64]
                    h = 4 * G + hh
                    mm(out, PM[:, hh * 512 + P:hh * 512 + 256], wta[:, hh * P:hh * P + 64], start=(hh < 2), stop=False,
                       skip_group_check=True)
                    mm(out, PM[:, hh * 512 + 384:hh * 512 + 512], vT[:, t * 512 + h * 64:t * 512 + (h + 1) * 64],
                       start=False, stop=False, skip_group_check=True)
                pe.wait_ge(S("rw_R_evac"), u + 1)
                for c in range(4):
                    r = slice(C * c, C * c + C)
                    for hh in range(4):
                        h, s, hp = 4 * G + hh, 64 * (hh % 2), hh // 2
                        W, TA = wta[r, hh * P:hh * P + 64], wta[r, hh * P + 64:(hh + 1) * P]
                        mm(bank[4 + c][s:s + 64, hp * 64:(hp + 1) * 64], TA, bnT[r, hh * 64:(hh + 1) * 64],
                           start=(hh < 2), stop=True, skip_group_check=True)
                        out = bank[4 + c][s:s + 64, P + hp * 64:P + (hp + 1) * 64]
                        mm(out, knT[r, hh * 64:(hh + 1) * 64], vT[r, t * 512 + h * 64:t * 512 + (h + 1) * 64],
                           start=False, stop=False, skip_group_check=True)
                        i = mm(out, bnT[r, hh * 64:(hh + 1) * 64], W, start=False, stop=False, skip_group_check=True)
                    done(i, "rw_chunk")
                for c in range(4):
                    g = 4 * t + c
                    pe.wait_ge(S("rw_phi"), 4 * u + c + 1)
                    if c:
                        pe.wait_ge(S("rw_state"), 4 * u + c)
                    for hh in range(4):
                        s, hp = 64 * (hh % 2), hh // 2
                        q = 2 * G + hp
                        i = mm(bank[4 + c][s:s + 64, P + hp * 64:P + (hp + 1) * 64],
                               phi[s:s + 64, c * P + hp * 64:c * P + (hp + 1) * 64],
                               s_all[s:s + 64, g * 256 + q * 64:g * 256 + (q + 1) * 64], start=False, stop=True,
                               skip_group_check=True)
                    done(i, "rw_chain")
                    for hh in range(4):
                        s, hp = 64 * (hh % 2), hh // 2
                        q = 2 * G + hp
                        i = mm(bank[2 + hh % 2][C * c:C * c + C, hp * 64:(hp + 1) * 64],
                               Rh[s:s + 64, hp * P + C * c:hp * P + C * c + C],
                               s_all[s:s + 64, g * 256 + q * 64:g * 256 + (q + 1) * 64], start=False, stop=True,
                               skip_group_check=True)
                done(i, "rw_y")
            while gate_k[0] < E_BLOCK + 16:
                gate_tile()
            pe.wait_ge(S("rw_state"), 16)
            pe.wait_ge(S("rw_y_evac"), 4)
            for q in range(4):
                i = nc.tensor.transpose(bank[4][0:64, q * P:(q + 1) * P], s_all[:, 8 * 256 + q * 64:8 * 256 + (q + 1) * 64], ident)
            done(i, "rw_end")

            def gated_T(t, src, b):
                rows = TILES[t][1]
                for q in range(4):
                    i = nc.tensor.transpose(b[:, q * P:q * P + rows], src[0:rows, t * 512 + q * P:t * 512 + (q + 1) * P],
                                            ident[0:rows, 0:rows])
                done(i, "gated_T")

            pe.wait_ge(S("oa_done"), 3)
            for t in range(3):
                gated_T(t, oH, bank[5 + t])
            pe.wait_ge(S("pj_evac"), E_BLOCK + 16)
            for br in range(2):
                chunk_ready(N_IN + 2 * br)
                chunk_ready(N_IN + 2 * br + 1)
                if br:
                    for t in range(3):
                        pe.wait_ge(S("ob_done"), t + 1)
                        gated_T(t, yO, bank[5 + t])
                pe.wait_ge(S("gated_T_evac"), 3 * (br + 1))
                for j in range(KT):
                    n = 8 * br + j
                    if n >= 2:
                        pe.wait_ge(S("br_evac"), n - 1)
                    for kt in range(4):
                        slot, _ = mix_chunk(N_IN + 2 * br + kt // 2)
                        i = mm(bank[n % 2][:, 0:NT], slot[:, kt % 2, j * P:(j + 1) * P],
                               (obT if br else oaT)[:, kt * NT:(kt + 1) * NT], start=(kt == 0), stop=(kt == 3))
                    done(i, "branch")
            pe.wait_ge(S("xr_loaded"), 48)
            pe.wait_ge(S("rwp_end"), 1)
            for t, (o, rows) in enumerate(TILES):
                for h in range(2):
                    mm(acc(t, h), ident[0:rows, 0:rows], xr[0:rows, t, h * 512:(h + 1) * 512], start=True, stop=False,
                       skip_group_check=True)
            def w_out_tile(t, k0, k1):
                o, rows = TILES[t]
                for kt in range(k0, k1):
                    if t == 0 and kt % 2 == 0:
                        chunk_ready(N_IN + 4 + kt // 2)
                    slot, _ = mix_chunk(N_IN + 4 + kt // 2)
                    if t == 0:
                        pe.wait_ge(S("merged"), kt + 1)
                    for h in range(2):
                        i = mm(acc(t, h), mT[:, kt * NT + o:kt * NT + o + rows], slot[:, kt % 2, h * 512:(h + 1) * 512],
                               start=False, stop=True, skip_group_check=True)
                if k1 == KT:
                    done(i, "wo_done")

            def x2_T(t):
                rows = TILES[t][1]
                pe.wait_ge(S("xn_done"), 3 + t + 1)
                if t == 1:
                    pe.wait_ge(S("x2T_evac"), 2)
                for k in range(KT):
                    b, c = (bank[k // 4], (k % 4) * P) if t < 2 else (bank[6], k * NS)
                    i = nc.tensor.transpose(b[:, c:c + rows], x2[0:rows, t, k * P:(k + 1) * P], ident[0:rows, 0:rows])
                    if k % 4 == 3 and (t < 2 or k == 7):
                        done(i, "x2T")

            def logits(t):
                o, rows = TILES[t]
                for kt in range(KT):
                    i = mm(bank[0][0:rows, t * NE:(t + 1) * NE], x2T[:, kt * NT + o:kt * NT + o + rows],
                           rw_sb[:, kt * NE:(kt + 1) * NE], start=(kt == 0), stop=(kt == KT - 1))
                return i

            def keep_busy(n):
                for _ in range(n):
                    mm(bank[1][:, 0:P], ident, ones, start=True, stop=True)

            w_out_tile(0, 0, KT)
            w_out_tile(1, 0, KT)
            x2_T(0)
            w_out_tile(2, 0, 6)
            x2_T(1)
            w_out_tile(2, 6, KT)
            pe.wait_ge(S("router_loaded"), 16)
            pe.wait_ge(S("x2T_evac"), 4)
            logits(0)
            logits(1)
            keep_busy(8)
            x2_T(2)
            keep_busy(4)
            pe.wait_ge(S("x2T_evac"), 5)
            done(logits(2), "logits")
            keep_busy(14)
            pe.wait_ge(S("chosen"), 1)
            for t, (o, rows) in enumerate(TILES):
                for s in range(t + 1):
                    n = TILES[s][1]
                    i = mm(bank[6][0:rows, t * NE:(t + 1) * NE], (before if s == t else ones)[0:n, 0:rows],
                           M[0:n, s * NE:(s + 1) * NE], start=(s == 0), stop=(s == t))
            for s, (o, n) in enumerate(TILES):
                i = mm(bank[6][:, 3 * NE:4 * NE], ones[0:n, :], M[0:n, s * NE:(s + 1) * NE], start=(s == 0), stop=(s == 2))
            done(i, "ranks")
            keep_busy(6)

            def pick():
                for t, (o, rows) in enumerate(TILES):
                    for h in range(2):
                        i = mm(bank[6][64 * h:64 * h + 64, :], sel[0:rows, t * SLOTS:(t + 1) * SLOTS],
                               x2[0:rows, t, h * 512:(h + 1) * 512], start=(t == 0), stop=(t == 2), skip_group_check=True)
                i.then_inc(S("picked"), 1)

            def pick_T():
                for q in range(4):
                    i = nc.tensor.transpose(bank[6][:, q * P:(q + 1) * P], xg[:, q * P:(q + 1) * P], ident)
                i.then_inc(S("picked_T"), 1)

            def lhs_cols(a, kt):
                c = (kt % 4) * P + SLOTS * (kt // 4)
                return a[:, c:c + SLOTS]

            def b_down(t):
                o, rows = TILES[t]
                for h in range(2):
                    mm(acc(t, h), wT[:, o:o + rows], bdn[:, h * 512:(h + 1) * 512], start=False, stop=True, skip_group_check=True)

            def add(t):
                o, rows = TILES[t]
                for h in range(2):
                    i = mm(acc(t, h), GT[:, o:o + rows], yo[:, h * 512:(h + 1) * 512], start=False, stop=True,
                           skip_group_check=True)
                return i

            pe.wait_ge(S("weights_ready"), 1)
            for t, (o, rows) in enumerate(TILES):
                i = nc.tensor.transpose(bank[0][0:NE, o:o + rows], wte[0:rows, t * NE:(t + 1) * NE], ident[0:rows, 0:rows])
            done(i, "wT")
            pe.wait_ge(S("sel_ready"), 1)
            pick()
            pe.wait_ge(S("bdn_loaded"), 16)
            pe.wait_ge(S("wT_evac"), 1)
            b_down(0)
            pe.wait_ge(S("xg_evac"), 1)
            pick_T()
            b_down(1)
            b_down(2)
            pe.wait_ge(S("bgu3"), 1)
            def pe_pair(i, first=False):
                for x in range(2):
                    pe.wait_ge(S("rows_evac"), i * 2 + x + 1)
                    if x == 1:
                        for t, (o, rows) in enumerate(TILES):
                            ins = nc.tensor.transpose(bank[6][:, o:o + rows], gsel[0:rows, t * P:(t + 1) * P], ident[0:rows, 0:rows])
                        ins.then_inc(S("gt_T"), 1)
                    for c in range(KT):
                        pe_w_wait(c, i, x, first)
                        if c == 6:
                            if x == 0:
                                pe.wait_ge(S("gsel_ready"), i + 1)
                            for q in (0, 2, 1, 3):
                                mm(bank[q % 2][64 * (q // 2):64 * (q // 2) + 64, :], ind[:, x * SLOTS:(x + 1) * SLOTS],
                                   bgu3[:, q * 512:(q + 1) * 512], start=False, stop=False, skip_group_check=True)
                        for q in (0, 2, 1, 3):
                            if c == 0 and q == 1:
                                pe.wait_ge(S("y_evac"), i * 4 + 2 * x + 2)
                            ins = mm(bank[q % 2][64 * (q // 2):64 * (q // 2) + 64, :], lhs_cols(xT, c),
                                     w_at(c, first and x == 1)[:, q * 512:(q + 1) * 512], start=(c == 0), stop=(c == KT - 1), skip_group_check=True)
                        ins.then_inc(w_used, 1)
                    pe.wait_ge(S("sel_ready"), i * 2 + x + 2)
                    pe.wait_ge(S("gt_evac"), i + 1 + x)
                    pick()
                    if x == 0:
                        for t in range(3):
                            ins = add(t)
                        ins.then_inc(S("added"), 1)
                        pe.wait_ge(S("xg_evac"), i * 2 + 2)
                        pick_T()
                    pe.wait_ge(S("act_ready"), i * 2 + x + 1)
                    for q in range(4):
                        ins = nc.tensor.transpose(bank[0][:, q * P:(q + 1) * P], act_s[:, q * P:(q + 1) * P], ident)
                    ins.then_inc(S("actT"), 1)
                    if x == 1:
                        pe.wait_ge(S("xg_evac"), i * 2 + 3)
                        pick_T()
                    pe.wait_ge(S("actT_evac"), i * 2 + x + 1)
                    for c in range(KT, ECH):
                        pe_w_wait(c, i, x, first)
                        for kk in range(2):
                            kt = 2 * (c - KT) + kk
                            for h in range(2):
                                ins = mm(bank[1][64 * h:64 * h + 64, :], lhs_cols(actT, kt), w_slot(c)[:, kk * D + h * 512:kk * D + (h + 1) * 512],
                                         start=(kt == 0), stop=(kt == KT - 1), skip_group_check=True)
                        ins.then_inc(w_used, 1)

            pe_pair(0, True)
            pe.wait_ge(S("blocks"), 1)
            pairs = pe.value_load(nblk[0:1, 0:1], min_val=NE // 2, max_val=TABS // 2)
            with pe.Fori(1, pairs) as i:
                pe_pair(i)
            pe.wait_ge(S("y_evac"), pairs * 4 + 2)
            for t in range(3):
                done(add(t), "wo_done")

        @block.scalar
        def _(act):
            def fn(out, in_, f, **kw):
                return nc.scalar.activation(out, in_, f, **kw)

            nc.scalar.preload_act_table_set("natural_log_exp_and_others")
            r = 0
            for a in (rwkv_mu[0], rwkv_w0[0], rwkv_a0[0], rwkv_k_k[0], rwkv_k_a[0], None, hgrn_lb_logits[0], hgrn_lb_logits[1]):
                src = rwkv_r_k[0].rearrange("(q h) n -> q (h n)", q=4) if a is None else a.rearrange("(r p) -> r p", p=P)
                n = src.shape[0]
                act.dma_start(par_rows[r:r + n, :], src).then_inc(S("par_loaded"), 16)
                r += n
            act.dma_start(gn_bc, hgrn_gnorm_w.partition_broadcast(P)).then_inc(S("par_loaded"), 16)
            xv = xnT.rearrange("p (k t) -> p k t", k=KT)
            for t, (o, n) in enumerate(TILES):
                act.wait_ge(S(f"x_loaded{t}"), 16)
                done_wait(act, fn(xn[0:n, t, :], xs[0:n, t, :], ACT.Square, accum_out=stat[0:n, t:t + 1]), "act_step")
                act.wait_ge(S("eps"), 1)
                done_wait(act, fn(stat[0:n, 4 + t:5 + t], stat[0:n, t:t + 1], ACT.Ln, scale=1.0 / D, bias=epsc[0:n, 0:1]), "act_step")
                done(fn(stat[0:n, 8 + t:9 + t], stat[0:n, 4 + t:5 + t], ACT.Exp, scale=-0.5), "rstd")
            act.wait_ge(S("xn_done"), 3)
            act.dma_start(shift_p[0], xn[127:128, 1, :]).then_inc(S("shift_out"), 16)
            act.dma_start(shift_s[0], xn[3:NS:4, 2, :]).then_inc(S("shift_out"), 16)
            for e in range(5):
                act.wait_ge(S("xT_done"), e + 1)
                t, k0 = e // 2, 4 * (e % 2)
                if e < 4:
                    i = fn(xv[:, k0:k0 + 4, 128 * t:128 * t + 128], bank[e].rearrange("p (k t) -> p k t", k=4), ACT.Copy)
                else:
                    i = fn(xv[:, :, NP_:NX], bank[4][:, 0:8 * 40].rearrange("p (k t) -> p k t", k=KT), ACT.Copy)
                done(i, "xT_evac")
            act.wait_ge(S("par_T"), 1)
            fn(npar, bank[5][:, 0:42], ACT.Copy, scale=-1.0)
            done(fn(par, bank[5][:, 0:42], ACT.Copy), "par")
            act.wait_ge(S("lb_in"), 1)
            done(fn(stat[:, 16:24], stat[:, 16:24], ACT.Exp), "par")
            act.wait_ge(S("shift_zero"), 2)
            for k in range(14):
                act.wait_ge(S("pj_done"), k + 1)
                if k >= 2:
                    act.wait_ge(S("shift_done"), k - 1)
                e, b = shE[k % 2], bank[k % 4]
                es = e[:, 257:297].rearrange("p (b j) -> p b j", j=5)
                fn(e[:, 1:257], b[:, 0:NP_], ACT.Copy)
                fn(es[:, :, 1:5], b[:, NP_:NT].rearrange("p (b j) -> p b j", j=TS), ACT.Copy)
                done(fn(es[:, :, 0:1], b[:, NT:NX].rearrange("p (b j) -> p b j", j=1), ACT.Copy), "pj_evac")
            act.wait_ge(S("shift_done"), 13)
            act.wait_ge(S("masks"), 1)

            def recip(a):
                done_wait(act, fn(a, a, ACT.Ln, bias=ones[0:a.shape[0], 0:1]), "act_step")
                done(fn(a, a, ACT.Exp, scale=-1.0), "recip")

            done_wait(act, fn(waT[0:64, :], waT[0:64, :], ACT.Exp, scale=2.0), "act_step")
            recip(waT[0:64, :])
            act.wait_ge(S("shift_done"), 14)
            done_wait(act, fn(glT, glT, ACT.Exp, scale=-1.0), "act_step")
            recip(glT)

            def evac_qf(k):
                act.wait_ge(S("pj_done"), k + 1)
                b, q = bank[k % 4][:, 0:NT], (k - 14) % 4
                cols = slice(q * NT, (q + 1) * NT)
                if k < 18:
                    fn(fm[10][:, cols], b, ACT.Copy)
                    i = fn(fm[11][:, cols], b, ACT.Exp, scale=-1.0)
                else:
                    i = fn(z0[:, cols], b, ACT.Exp, scale=-1.0)
                done(i, "pj_evac")

            def evac_ig(k):
                act.wait_ge(S("pj_done"), k + 1)
                dst, m = (hiT, hgT)[(k - 22) // 5], (k - 22) % 5
                if m < 4:
                    c = (m % 2) * 512 + CPC * (m // 2)
                    i = fn(dst[:, c:c + CPC], bank[k % 4][:, 0:CPC], ACT.Copy)
                else:
                    for x in range(2):
                        c = 1024 + CPC * x
                        i = fn(dst[0:NS, c:c + CPC], bank[k % 4][NS * x:NS * x + NS, 0:CPC], ACT.Copy)
                done(i, "pj_evac")

            for k in range(14, 18):
                evac_qf(k)
            for q in range(4):
                act.wait_ge(S("lora_done"), q + 1)
                cols = slice(q * NT, (q + 1) * NT)
                fn(fm[3][:, cols], bank[4 + q % 2][:, 0:NT], ACT.Exp, scale=-1.0, bias=npar[:, 14 + q:15 + q])
                done(fn(fm[4][:, cols], bank[6 + q % 2][:, 0:NT], ACT.Exp, scale=-1.0, bias=npar[:, 18 + q:19 + q]), "lora_evac")
            act.wait_ge(S("lora_evac"), 4)
            recip(fm[3])
            act.wait_ge(S("kn_evac"), 4)
            done_wait(act, fn(fm[5], fm[5], ACT.Ln), "act_step")
            done(fn(fm[5], fm[5], ACT.Exp, scale=-0.5), "kn_rs")
            for k in range(18, 20):
                evac_qf(k)
            recip(fm[4])
            act.wait_ge(S("pj_evac"), 18)
            recip(fm[11])
            for k in range(20, 22):
                evac_qf(k)
            act.wait_ge(S("pj_evac"), 22)
            recip(z0)
            for k in range(22, 24):
                evac_ig(k)
            act.wait_ge(S("rw_logw"), 1)
            done(fn(wS.rearrange("p (q t) -> p q t", q=4), fm[3].rearrange("p (q t) -> p q t", q=4)[:, :, NP_:NT], ACT.Exp), "rw_exp")
            evac_ig(24)
            act.wait_ge(S("rw_cex"), 1)
            done(fn(fm[3], fm[3], ACT.Exp), "rw_exp")
            done(fn(fm[8], fm[7], ACT.Exp), "rw_exp")
            done(fn(fm[7], fm[7], ACT.Exp, scale=-1.0), "rw_exp")
            for k in range(25, 27):
                evac_ig(k)
            act.wait_ge(S("bonus_done"), 1)
            fn(rkb[:, 0:16], bank[6][:, 0:16], ACT.Copy)
            done(fn(rkb[0:NS, 16:24], bank[6][0:NS, 16:24], ACT.Copy), "bonus_evac")
            for t, (o, rows) in enumerate(TILES):
                act.wait_ge(S("g_done"), t + 1)
                done(fn(gT[0:rows, t * 512:(t + 1) * 512], bank[(4, 5, 7)[t]][0:rows, :], ACT.Copy), "g_evac")
            for a in range(6):
                act.wait_ge(S("smp_T"), a + 1)
                b = bank[(4, 5, 7)[a % 3]]
                if a == 5:
                    fn(vT[0:NS, 1024:1536], b[0:NS, :], ACT.Copy)
                done(fn(stm[0:NS, a * 512:(a + 1) * 512], b[0:NS, :], ACT.Copy), "smp_evac")
            act.wait_ge(S("hg_f"), 1)
            done(fn(fm[3], z0, ACT.Ln), "hg_log")
            for k in range(27, 29):
                evac_ig(k)
            act.wait_ge(S("hg_b"), 1)
            done(fn(fm[11], fm[3], ACT.Exp), "hg_exp")
            done(fn(fm[1], fm[3], ACT.Exp, scale=-1.0), "hg_exp")
            done(fn(fm[0], fm[9], ACT.Exp), "hg_exp")
            evac_ig(29)
            act.wait_ge(S("hg_rev"), 1)
            done(fn(fm[9], fm[9], ACT.Exp), "hg_exp")
            for k in range(30, 32):
                evac_ig(k)
            gate_k = [E_BLOCK]

            def gate_evac():
                k = gate_k[0]
                gate_k[0] += 1
                g = k - E_BLOCK
                act.wait_ge(S("pj_done"), k + 1)
                done(fn(gate[g // 4][:, (g % 4) * NT:(g % 4 + 1) * NT], bank[k % 2][:, 0:NT], ACT.Exp, scale=-1.0), "pj_evac")

            for n3, t in enumerate((0, 2, 1)):
                act.wait_ge(S("hg_kT"), n3 + 1)
                rows = TILES[t][1]
                done(fn(ktT[0:rows, :], bank[2][0:rows, :], ACT.Copy), "hg_kT_evac")
                if t == 1:
                    gate_evac()
                act.wait_ge(S("hg_o"), n3 + 1)
                if t < 2:
                    i = fn(oH[:, t * 512:(t + 1) * 512], bank[2][:, :], ACT.Copy)
                else:
                    for h in range(HA):
                        i = fn(oH[0:NS, 1024 + h * P:1024 + (h + 1) * P], bank[4][NS * h:NS * h + NS, 0:P], ACT.Copy)
                done(i, "hg_o_evac")
                if t == 2:
                    act.wait_ge(S("hg_in"), 1)
                    for h in range(3):
                        gate_evac()
                    act.wait_ge(S("hg_upd"), 8)
                    act.dma_start(hgrn_s[0].rearrange("b h k v -> k (b h) v"), s0h.rearrange("p (b h v) -> p (b h) v", b=NB, h=HA))\
                       .then_inc(S("hgrn_out"), 16)
            act.wait_ge(S("hg_state"), 8)
            act.dma_start(hgrn_p[0, 0].rearrange("h k v -> k h v"), sH[:, 3 * 512:4 * 512].rearrange("p (h v) -> p h v", h=HA))\
               .then_inc(S("hgrn_out"), 16)
            both = [(slice(0, P), 0, 2), (slice(0, NS), 2, 3)]

            def oa_factors():
                act.wait_ge(S("pj_evac"), E_BLOCK)
                for t, (o, rows) in enumerate(TILES):
                    for h in range(HA):
                        c = t * 512 + h * P
                        i = fn(sq[0:rows, h * P:(h + 1) * P], oH[0:rows, c:c + P], ACT.Square, accum_out=stat[0:rows, 4 * t + h:4 * t + h + 1])
                    done_wait(act, i, "act_step")
                for r, t0, t1 in both:
                    i = fn(sgT[r, t0 * 512:t1 * 512], hgT[r, t0 * 512:t1 * 512], ACT.Exp, scale=-1.0)
                    i = fn(stat[r, 12 + 4 * t0:12 + 4 * t1], stat[r, 4 * t0:4 * t1], ACT.Ln, scale=1.0 / DA, bias=epsc[r, 0:1])
                done_wait(act, i, "act_step")
                for r, t0, t1 in both:
                    i = fn(sgT[r, t0 * 512:t1 * 512], sgT[r, t0 * 512:t1 * 512], ACT.Ln, bias=ones[r, 0:1])
                done_wait(act, i, "act_step")
                for r, t0, t1 in both:
                    fn(sgT[r, t0 * 512:t1 * 512], sgT[r, t0 * 512:t1 * 512], ACT.Exp, scale=-1.0)
                    i = fn(stat[r, 24 + 4 * t0:24 + 4 * t1], stat[r, 12 + 4 * t0:12 + 4 * t1], ACT.Exp, scale=-0.5)
                done(i, "oa_in")

            def ob_rstd(n3, t):
                r = slice(0, TILES[t][1])
                act.wait_ge(S("ob_var"), n3 + 1)
                done_wait(act, fn(st2[r, 72 + 8 * t:80 + 8 * t], st2[r, 48 + 8 * t:56 + 8 * t], ACT.Ln, scale=1.0 / DB,
                                  bias=epsc[r, 1:2]), "act_step")
                done(fn(st2[r, 72 + 8 * t:80 + 8 * t], st2[r, 72 + 8 * t:80 + 8 * t], ACT.Exp, scale=-0.5), "ob_rstd")

            ya = yaT.rearrange("p (h c) -> p h c", h=4)
            for u in range(4):
                t, G = u // 2, u % 2
                act.wait_ge(S("rw_T"), u + 1)
                fn(ya[:, :, 64:128], bank[2][:, 0:256].rearrange("p (h c) -> p h c", h=4), ACT.Copy)
                fn(bnT, bank[2][:, 256:512], ACT.Copy)
                fn(knT, bank[3][:, 0:256], ACT.Copy)
                c = t * 512 + 256 * G
                done(fn(vT[:, c:c + 256], bank[3][:, 256:512], ACT.Copy), "rw_T_evac")
                gate_evac()
                for lev in range(4):
                    act.wait_ge(S("rw_sq"), 4 * u + lev + 1)
                    d0 = 1024 * ((lev + 1) % 2 == 0)
                    for x in range(2):
                        src, dst = bank[4 + x][:, :], PQ[:, d0 + 512 * x:d0 + 512 * (x + 1)]
                        if lev == 3:
                            src, dst = (v.rearrange("p (h c) -> p h c", h=2)[:, :, P:2 * P] for v in (src, dst))
                        i = fn(dst, src, ACT.Copy)
                    done(i, "rw_sq_evac")
                    if lev < 2:
                        gate_evac()
                    if u >= 2 and lev == 1:
                        ob_rstd(u - 2, (0, 2)[u - 2])
                act.wait_ge(S("rw_WT"), u + 1)
                done(fn(wta, bank[6][:, :], ACT.Copy), "rw_WT_evac")
                act.wait_ge(S("pj_evac"), E_BLOCK + 4 * (u + 1))
                done_wait(act, fn(gate[u], gate[u], ACT.Ln, bias=ones[:, 0:1]), "act_step")
                done(fn(gate[u], gate[u], ACT.Exp, scale=-1.0), "sgate")
                if u == 0:
                    oa_factors()
            act.wait_ge(S("rw_end"), 1)
            done_wait(act, fn(PM[0:64, 0:512], bank[4][0:64, :], ACT.Copy), "rwp_end")
            act.dma_start(rwkv_p[0, 0].rearrange("h v k -> v h k"), PM[0:64, 0:512].rearrange("p (h k) -> p h k", h=HB))\
               .then_inc(S("rwp_out"), 16)
            def evac_T(br, dst):
                for t, (o, rows) in enumerate(TILES):
                    act.wait_ge(S("gated_T"), 3 * br + t + 1)
                    done(fn(dst.rearrange("p (q t) -> p q t", q=4)[:, :, o:o + rows],
                            bank[5 + t].rearrange("p (q t) -> p q t", q=4)[:, :, 0:rows], ACT.Copy), "gated_T_evac")

            evac_T(0, oaT)
            ob_rstd(2, 1)
            evac_T(1, obT)

            def residual_norm(t):
                r = slice(0, TILES[t][1])
                if t < 2:
                    for h in range(2):
                        i = fn(sq2[r, h * 512:(h + 1) * 512], acc(t, h), ACT.Square, accum_out=st3[r, 2 * t + h:2 * t + h + 1])
                else:
                    for h in range(2):
                        i = fn(res2[r, h * 512:(h + 1) * 512], acc(t, h), ACT.Copy)
                    done_wait(act, i, "act_step")
                    for h in range(2):
                        i = fn(sq2[r, h * 512:(h + 1) * 512], res2[r, h * 512:(h + 1) * 512], ACT.Square, accum_out=st3[r, 4 + h:5 + h])
                done_wait(act, i, "act_step")
                done_wait(act, fn(st3[r, 6 + t:7 + t], st3[r, 2 * t:2 * t + 1], ACT.Identity, bias=st3[r, 2 * t + 1:2 * t + 2]), "act_step")
                done_wait(act, fn(st3[r, 9 + t:10 + t], st3[r, 6 + t:7 + t], ACT.Ln, scale=1.0 / D, bias=epsc[r, 0:1]), "act_step")
                done(fn(st3[r, 12 + t:13 + t], st3[r, 9 + t:10 + t], ACT.Exp, scale=-0.5), "rstd")

            x2v = x2T.rearrange("p (k t) -> p k t", k=KT)

            def x2_evac(t):
                for k0 in (0, 4) if t < 2 else (0,):
                    act.wait_ge(S("x2T"), 2 * t + k0 // 4 + 1)
                    if t < 2:
                        i = fn(x2v[:, k0:k0 + 4, 128 * t:128 * t + 128], bank[k0 // 4].rearrange("p (k t) -> p k t", k=4), ACT.Copy)
                    else:
                        i = fn(x2v[:, :, NP_:NT], bank[6][:, 0:KT * NS].rearrange("p (k t) -> p k t", k=KT), ACT.Copy)
                    done(i, "x2T_evac")

            for t in range(3):
                if t == 2:
                    x2_evac(1)
                act.wait_ge(S("wo_done"), t + 1)
                residual_norm(t)
                if t == 1:
                    x2_evac(0)
            x2_evac(2)
            act.wait_ge(S("gk_in"), 1)
            done(fn(gk, gk, ACT.Exp), "gk_exp")
            act.wait_ge(S("wT"), 1)
            fn(wT, bank[0][0:NE, 0:NT], ACT.Copy).then_inc(S("wT_evac"), 1)
            act.wait_ge(S("picked"), 1)
            fn(xg, bank[6][:, :], ACT.Copy).then_inc(S("xg_evac"), 1)
            act.wait_ge(S("picked_T"), 1)
            fn(xT, bank[6][:, :], ACT.Copy).then_inc(S("rows_evac"), 1)
            act.wait_ge(S("blocks"), 1)
            nc.scalar.preload_act_table_set("sigmoid_and_others")
            def act_pair(i):
                for x in range(2):
                    if x == 1:
                        act.wait_ge(S("gt_T"), i + 1)
                        act.wait_ge(S("added"), i + 1)
                        fn(GT, bank[6][:, 0:NT], ACT.Copy).then_inc(S("gt_evac"), 1)
                    act.wait_ge(S("glu_ready"), i * 2 + x + 1)
                    fn(sig, glu, ACT.Sigmoid, scale=ALPHA).then_inc(S("sig_ready"), 1)
                    act.wait_ge(S("picked"), i * 2 + x + 2)
                    fn(xg, bank[6][:, :], ACT.Copy).then_inc(S("xg_evac"), 1)

                    def rows_T():
                        act.wait_ge(S("picked_T"), i * 2 + x + 2)
                        fn(xT, bank[6][:, :], ACT.Copy).then_inc(S("rows_evac"), 1)

                    if x == 0:
                        rows_T()
                    act.wait_ge(S("actT"), i * 2 + x + 1)
                    fn(actT, bank[0][:, :], ACT.Copy).then_inc(S("actT_evac"), 1)
                    if x == 1:
                        rows_T()
                    act.wait_ge(w_used, i * (2 * ECH) + ECH * (x + 1))
                    fn(yo[64 * x:64 * x + 64, 0:512], bank[1][0:64, :], ACT.Copy).then_inc(S("y_evac"), 1)

            act_pair(0)
            with act.Fori(1, act.value_load(nblk[0:1, 0:1], min_val=NE // 2, max_val=TABS // 2)) as i:
                act_pair(i)
            nc.scalar.preload_act_table_set("natural_log_exp_and_others")
            for t in range(3):
                act.wait_ge(S("wo_done"), 3 + t + 1)
                residual_norm(t)

        @block.vector
        def _(dve):
            v = nc.vector

            def step(ins, name="dve_step"):
                done_wait(dve, ins, name)

            def pc(a, c):
                return a[:, c:c + 1]

            def quarter(a, q):
                return a[:, q * NT:(q + 1) * NT]

            dve.wait_ge(S("norm_loaded"), 16)
            for t, (o, n) in enumerate(TILES):
                dve.wait_ge(S("rstd"), t + 1)
                step(v.scalar_tensor_tensor(out=xn[0:n, t, :], in0=xs[0:n, t, :], scalar=stat[0:n, 8 + t:9 + t],
                                            in1=norm_bc[0:n, :], op0=ALU.mult, op1=ALU.mult), "xn_done")
            dve.wait_ge(S("par"), 1)
            step(v.tensor_tensor(stat[:, 24:28], par[:, 34:38], par[:, 38:42], ALU.max))
            step(v.tensor_tensor(stat[:, 16:20], par[:, 34:38], stat[:, 24:28], ALU.subtract))
            step(v.tensor_tensor(stat[:, 20:24], par[:, 38:42], stat[:, 24:28], ALU.subtract), "lb_in")
            step(v.tensor_scalar(omka, par[:, 26:30], -1.0, 1.0, ALU.mult, ALU.add))
            dve.wait_ge(S("par"), 2)
            step(v.tensor_tensor(stat[:, 24:28], stat[:, 16:20], stat[:, 20:24], ALU.add))
            step(v.reciprocal(stat[:, 28:32], stat[:, 24:28]))
            step(v.tensor_tensor(lb, stat[:, 16:20], stat[:, 28:32], ALU.mult))
            step(v.tensor_tensor(omlb, stat[:, 20:24], stat[:, 28:32], ALU.mult))
            for k in range(14):
                dve.wait_ge(S("pj_evac"), k + 1)
                e = shE[k % 2]
                es = e[:, 257:297].rearrange("p (b j) -> p b j", j=5)
                ds_ = shD[:, NP_:NT].rearrange("p (b j) -> p b j", j=TS)
                dst = quarter(fm[k // 4], k % 4) if k < 12 else (waT, glT)[k - 12]
                v.tensor_tensor(ds_, es[:, :, 0:4], es[:, :, 1:5], ALU.subtract).then_inc(S("shift_d"), 1)
                v.tensor_tensor(shD[:, 0:NP_], e[:, 0:256], e[:, 1:257], ALU.subtract).then_inc(S("shift_d"), 1)
                dve.wait_ge(S("shift_d"), 2 * k + 2)
                v.scalar_tensor_tensor(out=dst[:, NP_:NT].rearrange("p (b j) -> p b j", j=TS), in0=ds_, scalar=pc(par, k),
                                       in1=es[:, :, 1:5], op0=ALU.mult, op1=ALU.add)
                step(v.scalar_tensor_tensor(out=dst[:, 0:NP_], in0=shD[:, 0:NP_], scalar=pc(par, k), in1=e[:, 1:257],
                                            op0=ALU.mult, op1=ALU.add), "shift_done")
            dve.wait_ge(S("recip"), 1)
            step(v.tensor_scalar(waT[0:64, :], waT[0:64, :], -2.0, 1.0, ALU.mult, ALU.add), "lora_in")
            for q in range(4):
                i = v.tensor_scalar(quarter(fm[9], q), quarter(fm[1], q), pc(par, 22 + q), None, ALU.mult)
            step(i)
            dve.wait_ge(S("xT_done"), 5)
            dve.wait_ge(S("shift_out"), 32)
            step(v.tensor_tensor(z1, fm[9], fm[9], ALU.mult), "ksq")
            for q in range(4):
                dve.wait_ge(S("kn_done"), q + 1)
                step(v.tensor_scalar(quarter(fm[5], q), bank[4 + q % 2][:, 0:NT], 1e-24, None, ALU.max), "kn_evac")
            dve.wait_ge(S("recip"), 3)
            dve.wait_ge(S("masks"), 1)
            step(v.tensor_scalar(fm[3], fm[3], W_SCALE, None, ALU.mult), "rw_logw")
            step(v.tensor_tensor_scan(fm[7], scan_mask, fm[3], 0.0, ALU.mult, ALU.add))
            dve.wait_ge(S("rw_exp"), 1)
            step(v.tensor_tensor(fm[3], fm[7], fm[3], ALU.subtract), "rw_cex")
            dve.wait_ge(S("kn_rs"), 1)
            step(v.tensor_tensor(fm[9], fm[9], fm[5], ALU.mult))
            dve.wait_ge(S("recip"), 4)
            for q in range(4):
                i = v.tensor_scalar(quarter(fm[5], q), quarter(fm[4], q), pc(par, 26 + q), pc(omka, q), ALU.mult, ALU.add)
            step(i)
            step(v.tensor_tensor(fm[1], fm[1], fm[5], ALU.mult))
            dve.wait_ge(S("kn_done"), 4)
            for q in range(4):
                i = v.scalar_tensor_tensor(out=quarter(z1, q), in0=quarter(fm[0], q), scalar=pc(par, 30 + q),
                                           in1=quarter(fm[1], q), op0=ALU.mult, op1=ALU.mult)
            step(i, "bonus_in")
            dve.wait_ge(S("rw_exp"), 4)
            step(v.scalar_tensor_tensor(out=fm[5], in0=fm[9], scalar=-1.0, in1=fm[3], op0=ALU.mult, op1=ALU.mult))
            step(v.tensor_tensor(fm[3], fm[9], fm[4], ALU.mult), "smp_in")
            step(v.tensor_tensor(fm[6], fm[0], fm[8], ALU.mult))

            def chunk_last(a):
                a4 = a.rearrange("p (q t) -> p q t", q=4)
                return (a4[:, :, 0:NP_].rearrange("p q (c j) -> p q c j", j=C)[:, :, :, C - 1],
                        a4[:, :, NP_:NT].rearrange("p q (c j) -> p q c j", j=TS)[:, :, :, TS - 1])

            step(v.tensor_copy(gamR.rearrange("p (q c) -> p q c", q=4), chunk_last(fm[8])[0]))
            step(v.tensor_tensor(fm[8], fm[1], fm[7], ALU.mult))
            step(v.tensor_tensor(fm[7], fm[3], fm[7], ALU.mult))
            dve.wait_ge(S("recip"), 6)
            for q in range(4):
                i = v.tensor_scalar(quarter(z0, q), quarter(z0, q), pc(omlb, q), pc(lb, q), ALU.mult, ALU.add)
            step(i)
            dve.wait_ge(S("smp_T"), 6)
            step(v.tensor_scalar(fm[4], z0, -1.0, 1.0, ALU.mult, ALU.add), "hg_f")
            dve.wait_ge(S("recip"), 5)
            step(v.tensor_tensor(fm[10], fm[10], fm[11], ALU.mult))
            dve.wait_ge(S("hg_log"), 1)
            step(v.tensor_tensor_scan(fm[9], scan_mask, fm[3], 0.0, ALU.mult, ALU.add))

            def chunks(a):
                a4 = a.rearrange("p (q t) -> p q t", q=4)
                return (a4[:, :, 0:NP_].rearrange("p q (c j) -> p q c j", j=C),
                        a4[:, :, NP_:NT].rearrange("p q (c j) -> p q c j", j=TS))

            for s, (n, mid) in enumerate(((C, C // 2 - 1), (TS, TS // 2 - 1))):
                src, dst = chunks(fm[9])[s], chunks(fm[3])[s]
                i = v.tensor_tensor(dst, src, bcast(src[:, :, :, mid:mid + 1], [P, 4, NB, n]), ALU.subtract)
            step(i, "hg_b")
            last = stat[:, 0:64].rearrange("p (q c) -> p q c", q=4)
            gam = gamH.rearrange("p (q c) -> p q c", q=4)
            for s in range(2):
                i = v.tensor_copy(last[:, :, 8 * s:8 * s + 8], chunk_last(fm[9])[s])
            step(i)
            dve.wait_ge(S("hg_exp"), 3)
            for s, n in enumerate((C, TS)):
                a = chunks(fm[9])[s]
                i = v.tensor_tensor(a, bcast(last[:, :, 8 * s:8 * s + 8].unsqueeze(3), [P, 4, NB, n]), a, ALU.subtract)
            step(i, "hg_rev")
            for s in range(2):
                v.tensor_copy(gam[:, :, 8 * s:8 * s + 8], chunk_last(fm[0])[s])
            step(v.tensor_tensor(fm[11], fm[10], fm[11], ALU.mult))
            step(v.tensor_tensor(fm[1], fm[4], fm[1], ALU.mult))
            step(v.memset(qm, 0.0))
            step(v.tensor_tensor(fm[10], fm[10], fm[0], ALU.mult))
            step(v.tensor_copy(qm.rearrange("p (h b s) -> p h b s", h=HA, b=NB)[:, :, :, 0:TS],
                               fm[10].rearrange("p (h t) -> p h t", h=HA)[:, :, NP_:NT].rearrange("p h (b j) -> p h b j", j=TS)))
            dve.wait_ge(S("smp_st"), 96)
            v.memset(sH[:, 0:512], 0.0)
            dve.wait_ge(S("hg_exp"), 4)
            step(v.tensor_tensor(fm[4], fm[4], fm[9], ALU.mult), "hg_in")

            incl = mask4[:, P:2 * P]

            def hg_mask(n3, t):
                dve.wait_ge(S("hg_scores"), n3 + 1)
                if t < 2:
                    i = v.tensor_tensor(aT.rearrange("p (h t) -> p h t", h=4), bank[3].rearrange("p (h t) -> p h t", h=4),
                                        bcast(incl.unsqueeze(1), [P, 4, P]), ALU.mult)
                else:
                    i = v.tensor_tensor(aT[0:NS, 0:P].rearrange("p (h t) -> p h t", h=4),
                                        bank[3][0:NS, 0:P].rearrange("p (h t) -> p h t", h=4),
                                        bcast(smask[0:NS, :].unsqueeze(1), [NS, 4, NS]), ALU.mult)
                step(i, "hg_a")

            def hg_states(t):
                if t:
                    dve.wait_ge(S("hg_o"), 1)
                for c in range(4):
                    g = 4 * t + c
                    dve.wait_ge(S("hg_kv"), g + 1)
                    for h in range(HA):
                        a, b = (g % 5) * 512 + h * P, ((g + 1) % 5) * 512 + h * P
                        i = v.scalar_tensor_tensor(out=sH[:, b:b + P], in0=sH[:, a:a + P], scalar=pc(gamH, h * 16 + g),
                                                   in1=bank[4 + c][:, h * P:(h + 1) * P], op0=ALU.mult, op1=ALU.add)
                    step(i, "hg_state")

            hg_mask(0, 0)
            hg_states(0)
            hg_mask(1, 2)
            s0v = s0h.rearrange("p (b h v) -> p b h v", b=NB, h=HA)
            for h in range(HA):
                if h:
                    dve.wait_ge(S("hg_skv"), 2 * h)
                hv = hiT[0:NS, 1024 + h * P:1024 + (h + 1) * P]
                step(v.tensor_tensor(vexp[0:NS, :].rearrange("p (b v) -> p b v", b=NB), bcast(hv.unsqueeze(1), [NS, NB, P]),
                                     bcast(seqm[0:NS, :].unsqueeze(2), [NS, NB, P]), ALU.mult), "vexp")
                dve.wait_ge(S("hg_o"), 2)
                for g in range(2):
                    a = s0v[:, 4 * g:4 * g + 4, h, :]
                    i = v.tensor_tensor(a, a, bcast(gam[:, h, 8 + 4 * g:12 + 4 * g].unsqueeze(2), [P, 4, P]), ALU.mult)
                step(i)
                for g in range(2):
                    dve.wait_ge(S("hg_skv"), 2 * h + g + 1)
                    a = s0v[:, 4 * g:4 * g + 4, h, :]
                    step(v.tensor_tensor(a, a, bank[6 + g].rearrange("p (b v) -> p b v", b=4), ALU.add), "hg_upd")
            hg_mask(2, 1)
            hg_states(1)
            dve.wait_ge(S("hg_o_evac"), 3)
            step(v.memset(s_all[:, 0:256], 0.0), "rw_in")
            def heads(a, t, n, h=HB):
                return a[0:n, t * 512:(t + 1) * 512].rearrange("p (h c) -> p h c", h=h)

            def gate_a(t):
                n = TILES[t][1]
                c = slice(t * 512, (t + 1) * 512)
                dve.wait_ge(S("oa_in"), 1)
                step(v.tensor_tensor(hgT[0:n, c], hgT[0:n, c], sgT[0:n, c], ALU.mult))
                step(v.tensor_tensor(heads(hgT, t, n, HA), heads(hgT, t, n, HA), bcast(gn_bc[0:n, :].unsqueeze(1), [n, HA, DA]), ALU.mult))
                for h in range(HA):
                    a = slice(t * 512 + h * DA, t * 512 + (h + 1) * DA)
                    i = v.scalar_tensor_tensor(out=oH[0:n, a], in0=oH[0:n, a], scalar=stat[0:n, 24 + 4 * t + h:25 + 4 * t + h],
                                               in1=hgT[0:n, a], op0=ALU.mult, op1=ALU.mult)
                step(i, "oa_done")

            def center_b(t):
                n = TILES[t][1]
                if t == 2:
                    dve.wait_ge(S("ysm_ld"), 32)
                y = heads(yO, t, n)
                sums, means = st2[0:n, 8 * t:8 * t + 8], st2[0:n, 24 + 8 * t:32 + 8 * t]
                step(v.tensor_reduce(sums, y, AX.X, ALU.add))
                step(v.tensor_scalar(means, sums, 1.0 / DB, None, ALU.mult))
                step(v.tensor_tensor(y, y, bcast(means.unsqueeze(2), [n, HB, DB]), ALU.subtract))
                step(v.tensor_tensor(sqy[0:n, :], yO[0:n, t * 512:(t + 1) * 512], yO[0:n, t * 512:(t + 1) * 512], ALU.mult))
                step(v.tensor_reduce(st2[0:n, 48 + 8 * t:56 + 8 * t], sqy[0:n, :].rearrange("p (h c) -> p h c", h=HB), AX.X, ALU.add),
                     "ob_var")

            def gate_b(n3, t):
                n = TILES[t][1]
                c = slice(t * 512, (t + 1) * 512)
                y, b = heads(yO, t, n), [n, HB, DB]
                vv = heads(vT, t, n)
                dve.wait_ge(S("bonus_evac"), 1)
                step(v.tensor_tensor(vv, vv, bcast(rkb[0:n, 8 * t:8 * t + 8].unsqueeze(2), b), ALU.mult))
                step(v.tensor_tensor(vT[0:n, c], vT[0:n, c], lnb_bc[0:n, :], ALU.add))
                dve.wait_ge(S("ob_rstd"), n3 + 1)
                step(v.tensor_tensor(y, y, bcast(st2[0:n, 72 + 8 * t:80 + 8 * t].unsqueeze(2), b), ALU.mult))
                step(v.tensor_tensor(yO[0:n, c], yO[0:n, c], lnw_bc[0:n, :], ALU.mult))
                step(v.tensor_tensor(yO[0:n, c], yO[0:n, c], vT[0:n, c], ALU.add))
                dve.wait_ge(S("g_evac"), 3)
                step(v.tensor_tensor(yO[0:n, c], yO[0:n, c], gT[0:n, c], ALU.mult), "ob_done")

            Q4 = Qm.rearrange("p (a b c) -> p a b c", a=2, b=2)
            PM4 = PM.rearrange("p (h c) -> p h c", h=4)
            X4 = Xm.rearrange("p (h c) -> p h c", h=4)
            for u in range(4):
                t, G = u // 2, u % 2
                if u == 0:
                    dve.wait_ge(S("hgrn_out"), 32)
                for hh in range(4):
                    dve.wait_ge(S("rw_scores"), 4 * u + hh + 1)
                    step(v.tensor_tensor(PM4[:, hh, :], bank[4 + hh][:, :], mask4, ALU.mult), "rw_masked")
                dve.wait_ge(S("rw_L"), u + 1)
                for x in range(2):
                    step(v.tensor_tensor(Q4[:, :, x, :], bank[2 + x][:, 0:256].rearrange("p (a c) -> p a c", a=2),
                                         bcast(lower.unsqueeze(1), [P, 2, P]), ALU.mult), "rw_masked")
                step(v.tensor_tensor(X4, PM4[:, :, 0:P], bcast(ident.unsqueeze(1), [P, 4, P]), ALU.add), "rw_X")
                for lev in range(4):
                    dve.wait_ge(S("rw_XQ"), 4 * u + lev + 1)
                    step(v.tensor_tensor(Xm, Xm, bank[6][:, :], ALU.add), "rw_X")
                    if u == 1 and lev < 3:
                        gate_a(lev)
                    if u >= 2 and lev == 0:
                        center_b((0, 2)[u - 2])
                    if u >= 2 and lev == 1:
                        gate_b(u - 2, (0, 2)[u - 2])
                dve.wait_ge(S("rw_Y1"), u + 1)
                step(v.tensor_copy(yaT.rearrange("p (h c) -> p h c", h=4)[:, :, 0:64],
                                   bank[7][:, 0:256].rearrange("p (h c) -> p h c", h=4)), "rw_Y1_evac")
                dve.wait_ge(S("rw_R"), u + 1)
                rt = fm[6].rearrange("p (q t) -> p q t", q=4)[:, 2 * G:2 * G + 2, 128 * t:128 * t + 128]
                step(v.tensor_tensor(Rh.rearrange("p (q t) -> p q t", q=2), bank[7][:, 0:256].rearrange("p (q t) -> p q t", q=2),
                                     rt, ALU.add), "rw_R_evac")
                for c in range(4):
                    dve.wait_ge(S("rw_chunk"), 4 * u + c + 1)
                    step(v.tensor_tensor(phi[:, c * P:(c + 1) * P].rearrange("p (q c) -> p q c", q=2),
                                         bank[4 + c][:, 0:P].rearrange("p (q c) -> p q c", q=2),
                                         bcast(eye64.unsqueeze(1), [P, 2, 64]), ALU.add), "rw_phi")
                gr = gamR.rearrange("p (q c) -> p q c", q=4)
                for c in range(4):
                    g = 4 * t + c
                    dve.wait_ge(S("rw_chain"), 4 * u + c + 1)
                    a = (g + 1) * 256 + 2 * G * 64
                    step(v.tensor_tensor(s_all[:, a:a + P].rearrange("p (q v) -> p q v", q=2),
                                         bank[4 + c][:, P:2 * P].rearrange("p (q v) -> p q v", q=2),
                                         bcast(gr[:, 2 * G:2 * G + 2, g:g + 1], [P, 2, 64]), ALU.mult), "rw_state")
                dve.wait_ge(S("rw_y"), u + 1)
                y4 = yO[:, t * 512 + 256 * G:t * 512 + 256 * (G + 1)].rearrange("p (a b c) -> p a b c", a=2, b=2)
                v.tensor_copy(y4[:, :, 0, :], bank[2][:, 0:P].rearrange("p (a c) -> p a c", a=2))
                step(v.tensor_copy(y4[:, :, 1, :], bank[3][:, 0:P].rearrange("p (a c) -> p a c", a=2)), "rw_y_evac")
            center_b(1)
            gate_b(2, 1)
            for n in range(16):
                dve.wait_ge(S("branch"), n + 1)
                dve.wait_ge(S("sgate"), n // 4 + 1)
                dst, sg = mT[:, (n % 8) * NT:(n % 8 + 1) * NT], quarter(gate[n // 4], n % 4)
                if n < 8:
                    step(v.tensor_tensor(dst, bank[n % 2][:, 0:NT], sg, ALU.mult), "br_evac")
                else:
                    step(v.tensor_tensor(btmp, bank[n % 2][:, 0:NT], sg, ALU.mult), "br_evac")
                    step(v.tensor_tensor(dst, dst, btmp, ALU.add), "merged")
            def onehot(out, c0, w, slots, weights=None):
                for t, (o, rows) in enumerate(TILES):
                    dst, src, s1 = out[0:rows, t * w + c0:t * w + c0 + SLOTS], ramp[0:rows, 0:SLOTS], slots[0:rows, t:t + 1]
                    if weights is None:
                        i = v.tensor_scalar(dst, src, s1, None, ALU.is_equal)
                    else:
                        i = v.tensor_scalar(dst, src, s1, weights[0:rows, t:t + 1], ALU.is_equal, ALU.mult)
                return i

            dve.wait_ge(S("norm_loaded"), 32)

            def norm_rows(n, dst):
                for t, (o, rows) in enumerate(TILES):
                    dve.wait_ge(S("rstd"), 3 * n + t + 1)
                    for h in range(2):
                        src = acc(t, h) if t < 2 else res2[0:rows, h * 512:(h + 1) * 512]
                        i = v.scalar_tensor_tensor(out=dst[0:rows, t, h * 512:(h + 1) * 512], in0=src, scalar=st3[0:rows, 12 + t:13 + t],
                                                   in1=norm_bc[0:rows, h * 512:(h + 1) * 512], op0=ALU.mult, op1=ALU.mult)
                    step(i, "xn_done")

            norm_rows(1, x2)
            dve.wait_ge(S("ramp"), 1)
            dve.wait_ge(S("logits"), 1)
            v.tensor_tensor(lg[0:NS, 64:96], bank[0][0:NS, 64:96], rb_bc[0:NS, :], ALU.add)
            step(v.tensor_tensor(lg[:, 0:64].rearrange("p (t e) -> p t e", t=2), bank[0][:, 0:64].rearrange("p (t e) -> p t e", t=2),
                                 bcast(rb_bc.unsqueeze(1), [P, 2, NE]), ALU.add))
            for t in range(3):
                i = v.max(v8[:, 8 * t:8 * t + 8], lg[:, NE * t:NE * (t + 1)])
            step(i)
            for t in range(3):
                i = v.max_index(i8[:, 8 * t:8 * t + 8], v8[:, 8 * t:8 * t + 8], lg[:, NE * t:NE * (t + 1)])
            step(i)
            step(v.tensor_copy(i8f, i8[:, :]))
            top = i8f.rearrange("p (t j) -> p t j", t=3)[:, :, 0:TOPK]
            vals = v8.rearrange("p (t j) -> p t j", t=3)
            M4 = Mk.rearrange("p (t k e) -> p t k e", t=3, k=TOPK)
            k4 = [P, 3, TOPK, NE]
            step(v.tensor_tensor(M4, bcast(top.unsqueeze(3), k4), bcast(ramp[:, 0:NE].unsqueeze(1).unsqueeze(1), k4), ALU.is_equal))
            step(v.tensor_reduce(M.rearrange("p (t e) -> p t e", t=3), Mk.rearrange("p (t k e) -> p t e k", t=3, k=TOPK), AX.X, ALU.add),
                 "chosen")
            gk3 = gk.rearrange("p (t k) -> p t k", t=3)
            step(v.tensor_tensor(gk3, vals[:, :, 0:TOPK], bcast(vals[:, :, 0:1], [P, 3, TOPK]), ALU.subtract), "gk_in")
            dve.wait_ge(S("gk_exp"), 1)
            step(v.tensor_reduce(gsum[:, 0:3], gk3, AX.X, ALU.add))
            step(v.reciprocal(gsum[:, 3:6], gsum[:, 0:3]))
            step(v.tensor_tensor(gk3, gk3, bcast(gsum[:, 3:6].unsqueeze(2), [P, 3, TOPK]), ALU.mult))
            W4 = sk[:, 0:3 * TOPK * NE].rearrange("p (t k e) -> p t k e", t=3, k=TOPK)
            step(v.tensor_tensor(W4, M4, bcast(gk3.unsqueeze(3), k4), ALU.mult))
            step(v.tensor_reduce(wte.rearrange("p (t e) -> p t e", t=3), W4.rearrange("p t k e -> p t e k"), AX.X, ALU.add), "weights_ready")
            dve.wait_ge(S("ranks"), 1)
            v.tensor_copy(Rk[:, 0:64], bank[6][:, 0:64])
            v.tensor_copy(Rk[0:NS, 64:96], bank[6][0:NS, 64:96])
            step(v.tensor_copy(Ck, bank[6][:, 96:128]))
            R0, M0 = (a.rearrange("p (t e) -> p t e", t=3)[:, :, 0] for a in (Rk, M))
            step(v.scalar_tensor_tensor(out=selc, in0=R0, scalar=1.0, in1=M0, op0=ALU.add, op1=ALU.mult))
            step(v.tensor_scalar(selc, selc, -1.0, None, ALU.add))
            step(onehot(sel, 0, SLOTS, selc), "sel_ready")
            step(v.tensor_scalar(nov, Ck, float(SLOTS), None, ALU.is_gt))
            for j in range(2, (NT - 1) // SLOTS + 1):
                step(v.scalar_tensor_tensor(out=nov, in0=Ck, scalar=float(SLOTS * j), in1=nov, op0=ALU.is_gt, op1=ALU.add))
            step(v.tensor_tensor_scan(ovend, ones[:, 0:NE], nov, 0.0, ALU.mult, ALU.add))
            le3, j3 = le.rearrange("p (j e) -> p j e", e=NE), [P, TABS - NE, NE]
            v.tensor_copy(btf[:, 0:NE], ramp[:, 0:NE])
            v.tensor_scalar(Ck[0:1, 0:OVER], ramp[0:1, 0:OVER], 2.0, ovend[0:1, NE - 1:NE], ALU.mult, ALU.is_lt)
            step(v.tensor_tensor(le3, bcast(ovend.unsqueeze(1), j3), bcast(ramp[:, 0:TABS - NE].unsqueeze(2), j3), ALU.is_le))
            step(v.tensor_reduce(btf[:, NE:TABS], le3, AX.X, ALU.add))
            v.tensor_reduce(gsum[0:1, 1:2], Ck[0:1, 0:OVER], AX.X, ALU.add)
            step(v.tensor_scalar(btf[:, 0:TABS], btf[:, 0:TABS], float(NE - 1), None, ALU.min))
            v.tensor_copy(bt[0:1, 0:TABS], btf[0:1, 0:TABS])
            v.tensor_scalar(nblk[0:1, 0:1], gsum[0:1, 1:2], float(NE // 2), None, ALU.add)
            step(v.tensor_scalar(nblk[0:1, 1:2], gsum[0:1, 1:2], 2.0, float(NE - 1), ALU.mult, ALU.add), "blocks")
            step(v.tensor_tensor(off_e, ovend, nov, ALU.subtract))
            step(v.scalar_tensor_tensor(out=off_e, in0=off_e, scalar=float(SLOTS), in1=ramp64[:, 0:NE], op0=ALU.mult, op1=ALU.subtract))
            step(v.tensor_scalar(off_e, off_e, float(SLOTS * (NE - 1)), None, ALU.add))
            d3, r3 = (a.rearrange("p (t e) -> p t e", t=3) for a in (dst_e, Rk))
            e3 = [P, 3, NE]
            step(v.scalar_tensor_tensor(out=d3, in0=r3, scalar=float(SLOTS), in1=bcast(off_e.unsqueeze(1), e3),
                                        op0=ALU.is_ge, op1=ALU.mult))
            step(v.tensor_tensor(d3, d3, r3, ALU.add))
            step(v.tensor_tensor(d3, d3, bcast(ramp64[:, 0:NE].unsqueeze(1), e3), ALU.add))
            step(v.tensor_tensor(M4, M4, bcast(d3.unsqueeze(2), k4), ALU.mult))
            step(v.tensor_reduce(dest.rearrange("p (t k) -> p t k", t=3), M4, AX.X, ALU.add))
            b4 = [P, 3, TABS, TOPK]
            q4, in4, s4 = (a.rearrange("p (t b k) -> p t b k", t=3, b=TABS) for a in (qk, inb, sk))
            tab3 = tab.rearrange("p (b s) -> p s b", s=TW)
            step(v.tensor_tensor(q4, bcast(dest.rearrange("p (t k) -> p t k", t=3).unsqueeze(2), b4),
                                 bcast(ramp64[:, 0:TABS].unsqueeze(1).unsqueeze(3), b4), ALU.subtract))
            step(v.tensor_scalar(inb, qk, 0.0, None, ALU.is_ge))
            step(v.scalar_tensor_tensor(out=inb, in0=qk, scalar=float(SLOTS), in1=inb, op0=ALU.is_lt, op1=ALU.mult))
            step(v.scalar_tensor_tensor(out=sk, in0=qk, scalar=1.0, in1=inb, op0=ALU.add, op1=ALU.mult))
            step(v.tensor_reduce(tab3[:, 0:3, :], s4, AX.X, ALU.add))
            step(v.tensor_scalar(tab3[:, 0:3, :], tab3[:, 0:3, :], -1.0, None, ALU.add))
            step(v.tensor_tensor(s4, in4, bcast(gk3.unsqueeze(2), b4), ALU.mult))
            step(v.tensor_reduce(tab3[:, 3:6, :], s4, AX.X, ALU.add))
            step(v.tensor_scalar(tab3[:, 6, :], btf[:, 0:TABS], pmod, None, ALU.is_equal))

            LOOP_STEPS = 7
            def dve_pair(i):
                v.tensor_copy(gselc, tab[:, bass.ds(i * (2 * TW), 2 * TW)]).then_inc(S("loop_step"), 1)
                dve.wait_ge(S("loop_step"), i * LOOP_STEPS + 1)
                for x in range(2):
                    v.tensor_scalar(ind[:, x * SLOTS:(x + 1) * SLOTS], ones[:, 0:SLOTS],
                                    gselc[:, x * TW + 6:x * TW + 7], None, ALU.mult)
                    ins = onehot(gsel, x * SLOTS, P, gselc[:, x * TW:x * TW + 3], gselc[:, x * TW + 3:x * TW + 6])
                ins.then_inc(S("gsel_ready"), 1)
                dve.wait_ge(S("gsel_ready"), i + 1)
                for x in range(2):
                    dve.wait_ge(S("picked"), i * 2 + x + 1)
                    v.tensor_copy(selc, tab[:, bass.ds(i * (2 * TW) + TW * (x + 1), 3)]).then_inc(S("loop_step"), 1)
                    dve.wait_ge(S("loop_step"), i * LOOP_STEPS + 3 * x + 2)
                    onehot(sel, 0, SLOTS, selc).then_inc(S("sel_ready"), 1)
                    dve.wait_ge(S("sel_ready"), i * 2 + x + 2)
                    dve.wait_ge(w_used, i * (2 * ECH) + (ECH * x + KT))
                    for b in range(2):
                        ins = v.tensor_scalar(glu[:, b * 256:(b + 1) * 256], bank[b][:, 0:512:2], LIMIT, None, ALU.min)
                    ins.then_inc(S("glu_ready"), 1)
                    for b in range(2):
                        ins = v.tensor_scalar(lin[:, b * 256:(b + 1) * 256], bank[b][:, 1:512:2], LIMIT, -LIMIT, ALU.min, ALU.max)
                    ins.then_inc(S("loop_step"), 1)
                    dve.wait_ge(S("loop_step"), i * LOOP_STEPS + 3 * x + 3)
                    v.scalar_tensor_tensor(out=lin, in0=lin, scalar=1.0, in1=glu, op0=ALU.add, op1=ALU.mult).then_inc(S("loop_step"), 1)
                    dve.wait_ge(S("loop_step"), i * LOOP_STEPS + 3 * x + 4)
                    dve.wait_ge(S("sig_ready"), i * 2 + x + 1)
                    v.tensor_tensor(act_s, lin, sig, ALU.mult).then_inc(S("act_ready"), 1)
                    dve.wait_ge(w_used, i * (2 * ECH) + ECH * (x + 1))
                    v.tensor_copy(yo[64 * x:64 * x + 64, 512:1024], bank[1][64:128, :]).then_inc(S("y_evac"), 1)
                    dve.wait_ge(S("act_ready"), i * 2 + x + 1)

            dve_pair(0)
            with dve.Fori(1, dve.value_load(nblk[0:1, 0:1], min_val=NE // 2, max_val=TABS // 2)) as i:
                dve_pair(i)
            dve.wait_ge(S("norm_loaded"), 48)
            norm_rows(2, xr)

        @block.gpsimd
        def _(pool):
            g = nc.gpsimd

            def step(ins, name="pool_step"):
                done_wait(pool, ins, name)

            step(g.memset(epsc[:, 0:1], EPS), "eps")
            step(g.memset(ident, 0.0))
            step(g.affine_select(out=ident, in_=ident, compare_op=ALU.not_equal, fill=1.0, base=0, pattern=[[-1, P]],
                                 channel_multiplier=1), "ident")
            pool.dma_start(lora[0:64, :], rwkv_w2[0]).then_inc(S("const_loaded"), 16)
            pool.dma_start(lora[64:128, :], rwkv_a2[0]).then_inc(S("const_loaded"), 16)
            pool.dma_start(g2, rwkv_g2[0]).then_inc(S("const_loaded"), 16)
            pool.dma_start(lnw_bc, rwkv_ln_w.partition_broadcast(P)).then_inc(S("const_loaded"), 16)
            pool.dma_start(lnb_bc, rwkv_ln_b.partition_broadcast(P)).then_inc(S("const_loaded"), 16)
            pool.dma_start(rb_bc, router_b.partition_broadcast(P)).then_inc(S("const_loaded"), 16)
            step(g.memset(ones, 1.0))
            step(g.memset(mask4, 0.0))
            step(g.memset(lower, 0.0))
            step(g.memset(before, 1.0))
            step(g.memset(eye64, 0.0))
            step(g.memset(ones64, 0.0))
            step(g.memset(head2, 0.0))
            step(g.memset(smask[0:NS, :], 1.0))
            step(g.memset(seqm[0:NS, :], 1.0))
            step(g.memset(scan_mask, 1.0))

            def sel(out, op, base, pattern, mult, fill):
                return g.affine_select(out=out, in_=out, compare_op=op, fill=fill, base=base, pattern=pattern,
                                       channel_multiplier=mult)

            step(sel(before, ALU.is_gt, 0, [[1, P]], -1, 0.0))
            for x in range(2):
                step(sel(eye64[64 * x:64 * x + 64, :], ALU.not_equal, 0, [[-1, 64]], 1, 1.0))
                step(g.memset(ones64[64 * x:64 * x + 64, 64 * x:64 * x + 64], 1.0))
                step(g.memset(head2[64 * x:64 * x + 64, x:x + 1], 1.0))
            for c in range(4):
                rr = slice(C * c, C * c + C)
                for m in range(4):
                    step(g.memset(mask4[rr, m * P + C * c:m * P + C * c + C], 1.0))
                step(g.memset(lower[rr, C * c:C * c + C], 1.0))
            a4 = scan_mask.rearrange("p (q t) -> p q t", q=4)
            step(g.memset(a4[:, :, 0:NP_].rearrange("p q (c j) -> p q c j", j=C)[:, :, :, 0:1], 0.0))
            step(g.memset(a4[:, :, NP_:NT].rearrange("p q (c j) -> p q c j", j=TS)[:, :, :, 0:1], 0.0))
            for c in range(4):
                rr = slice(C * c, C * c + C)
                for m in range(4):
                    step(sel(mask4[rr, m * P + C * c:m * P + C * c + C], ALU.is_gt if m % 2 == 0 else ALU.is_ge, 0, [[1, C]], -1, 0.0))
                step(sel(lower[rr, C * c:C * c + C], ALU.is_gt, 0, [[-1, C]], 1, 0.0))
            sm = smask[0:NS, :].rearrange("p (b j) -> p b j", j=TS)
            step(sel(smask[0:NS, :], ALU.is_ge, 0, [[1, NS]], -1, 0.0))
            step(sel(sm, ALU.is_ge, 0, [[-TS, NB], [0, TS]], 1, 0.0))
            step(sel(seqm[0:NS, :], ALU.is_ge, 0, [[-TS, NB]], 1, 0.0))
            step(sel(seqm[0:NS, :], ALU.is_ge, TS - 1, [[TS, NB]], -1, 0.0))
            pool.wait_ge(S("const_loaded"), 16 * 6)
            step(g.memset(epsc[:, 1:2], GN_EPS), "masks")
            for x in range(2):
                step(g.memset(shE[x][:, 0:1], 0.0), "shift_zero")
            for x in range(2):
                pool.dma_start(S_s[64 * x:64 * x + 64, :],
                               state_rwkv[0][:, :, 32 * x:32 * x + 32, :].rearrange("b h v k -> h b (v k)"))\
                    .then_inc(S("smp_ld"), 16)
            pool.wait_ge(S("hg_log"), 1)
            pool.wait_ge(S("bonus_done"), 1)
            pool.dma_start(s0h.rearrange("p (b h v) -> p (b h) v", b=NB, h=HA), state_hgrn[0].rearrange("b h k v -> k (b h) v"))\
                .then_inc(S("s0h_loaded"), 16)
            pool.wait_ge(S("smp_evac"), 6)
            for a in range(6):
                pool.dma_start(smp_dram[:, :, :, a, :].rearrange("h b t c -> (b t) h c"),
                               stm[0:NS, a * 512:(a + 1) * 512].rearrange("p (h c) -> p h c", h=HB)).then_inc(S("smp_st"), 16)
            pool.wait_ge(S("smp_st"), 96)
            for x in range(2):
                pool.dma_start(vec_s[64 * x:64 * x + 64, :], smp_dram.rearrange("h b t a c -> (h b) (t a c)")).then_inc(S("smp_ld"), 16)
                pool.dma_start(v_s[64 * x:64 * x + 64, :].rearrange("p (t v) -> p t v", t=TS),
                               smp_dram[:, :, :, 5, 32 * x:32 * x + 32].rearrange("h b t v -> (h b) t v")).then_inc(S("smp_ld"), 16)
            pool.wait_ge(S("smp_ld"), 96)
            S3, T3 = (a.rearrange("p (v k) -> p v k", k=DB) for a in (S_s, tmp_s))

            def row_sums(out):
                w = DB // 2
                while w >= 1:
                    o = T3[:, :, 0:w] if w > 1 else out.unsqueeze(2)
                    step(g.tensor_tensor(o, T3[:, :, 0:w], T3[:, :, w:2 * w], ALU.add))
                    w //= 2

            def k_row(t, a):
                c = (t * 6 + a) * DB
                return bcast(vec_s[:, c:c + DB].unsqueeze(1), [P, 32, DB])

            def v_col(a):
                return bcast(a.unsqueeze(2), [P, 32, DB])

            for t in range(TS):
                step(g.tensor_tensor(T3, S3, k_row(t, 3), ALU.mult))
                row_sums(sa_s)
                step(g.tensor_tensor(S3, S3, k_row(t, 1), ALU.mult))
                step(g.tensor_tensor(T3, v_col(sa_s), k_row(t, 4), ALU.mult))
                step(g.tensor_tensor(S3, S3, T3, ALU.subtract))
                step(g.tensor_tensor(T3, v_col(v_s[:, t * 32:(t + 1) * 32]), k_row(t, 2), ALU.mult))
                step(g.tensor_tensor(S3, S3, T3, ALU.add))
                step(g.tensor_tensor(T3, S3, k_row(t, 0), ALU.mult))
                row_sums(y_s[:, t * 32:(t + 1) * 32])
            for x in range(2):
                pool.dma_start(rwkv_s[0][:, :, 32 * x:32 * x + 32, :].rearrange("b h v k -> h b (v k)"),
                               S_s[64 * x:64 * x + 64, :]).then_inc(S("rws_out"), 16)
                pool.dma_start(ysm_dram[x].rearrange("h b t v -> (h b) (t v)"), y_s[64 * x:64 * x + 64, :]).then_inc(S("ysm_st"), 16)
            pool.wait_ge(S("ysm_st"), 32)
            pool.wait_ge(S("rw_in"), 1)
            pool.wait_ge(S("hgrn_out"), 32)
            for x in range(2):
                pool.dma_start(yO[0:NS, 1024:1536].rearrange("p (h x v) -> p h x v", h=HB, x=2)[:, :, x, :],
                               ysm_dram[x].rearrange("h b t v -> (b t) h v")).then_inc(S("ysm_ld"), 16)
            pool.dma_start(rw_sb.rearrange("p (k e) -> p k e", k=KT), router_w[0].rearrange("(k p) e -> p k e", p=P))\
                .then_inc(S("router_loaded"), 16)
            pool.wait_ge(S("kn_done"), 4)
            pool.wait_ge(S("merged"), 8)
            step(g.iota(ramp_i.rearrange("p (a b) -> p a b", a=2), pattern=[[0, 2], [1, SLOTS]], base=0, channel_multiplier=0))
            step(g.tensor_copy(ramp, ramp_i))
            pool.wait_ge(S("rw_end"), 1)
            step(g.memset(lg, 0.0))
            step(g.memset(Rk, 0.0))
            for x in range(4):
                step(g.iota(ramp_i[NE * x:NE * x + NE, 0:1], pattern=[[0, 1]], base=0, channel_multiplier=1))
            step(g.tensor_copy(pmod, ramp_i[:, 0:1]))
            step(g.tensor_scalar(ramp64, ramp[:, 0:64], float(SLOTS), None, ALU.mult), "ramp")
            pool.wait_ge(S("braw_loaded"), 48)
            step(g.memset(bgu3[32:64, :], 0.0))
            step(g.tensor_copy(bgu3[0:32, :], braw[0:32, :]))
            step(g.tensor_copy(bgu3[64:128, :], braw[64:128, :]))
            for r in (slice(64, 128), slice(96, 128)):
                step(g.tensor_tensor(braw[r, :], braw[r, :], bgu3[r, :], ALU.subtract))
                i = g.tensor_copy(bgu3[r, :], braw[r, :])
                step(i, "bgu3" if r.start == 96 else "pool_step")
            pool.wait_ge(S("logits"), 1)
            g.memset(GT, 0.0).then_inc(S("gt_evac"), 1)
            for x in range(2):
                g.memset(yo[:, x * 512:(x + 1) * 512], 0.0).then_inc(S("y_evac"), 1)


_INS = ("x_prompt", "x_sample", "state_hgrn", "state_rwkv", "state_shift", "norm1_w", "w_in", "hgrn_lb_logits", "hgrn_gnorm_w",
        "rwkv_mu", "rwkv_w0", "rwkv_w2", "rwkv_a0", "rwkv_a2", "rwkv_g2", "rwkv_k_k", "rwkv_k_a", "rwkv_r_k", "rwkv_ln_w",
        "rwkv_ln_b", "w_branch_a", "w_branch_b", "w_out", "norm2_w", "router_w", "router_b", "expert_w_gu", "expert_b_gu",
        "expert_w_down", "expert_b_down", "final_norm_w")
_OUTS = ((1, NP_, D), (NB, TS, D), (1, 1, HA, DA, DA), (1, 1, HB, DB, DB), (1, 1, D), (1, NB, HA, DA, DA), (1, NB, HB, DB, DB),
         (1, NB, D))


def kernel(**inputs):
    import numpy as _np
    import concourse.bacc as _bacc
    from concourse import mybir as _mybir
    from concourse.bass_utils import run_bass_kernel_spmd as _run

    nc = _bacc.Bacc("TRN2", target_bir_lowering=False, num_devices=1)
    arrays, args = {}, []
    for name in _INS:
        a = _np.ascontiguousarray(inputs[name])
        arrays[f"in_{name}_dram"] = a
        args.append(nc.dram_tensor(f"in_{name}_dram", a.shape, _mybir.dt.from_np(a.dtype), kind="ExternalInput").ap())
    for i, shape in enumerate(_OUTS):
        args.append(nc.dram_tensor(f"out_{i}_dram", shape, _mybir.dt.float32, kind="ExternalOutput").ap())
    layer_kernel(nc, *args)
    r = _run(nc, [arrays], core_ids=[0])
    return tuple(r.results[0][f"out_{i}_dram"] for i in range(len(_OUTS)))
```
